# Optimizing a Trainium2 kernel written in Bass

```python
import jax, jax.numpy as jnp
from jax import lax
import numpy as np

'''Hybrid streaming-encoder trunk: DEPTH layers, each one sandwich-normalised mixer
sub-layer whose mixing width is split into two parallel head groups that read the
same normalised input through ONE combined input projection:
  group A: RWKV-7 time mixing (8 heads x 64, generalized delta rule with data-dependent
           decay and vector-valued in-context learning rate, value residual to layer 0)
  group B: Conformer convolution module (512 channels: GLU -> causal depthwise conv
           width 31 -> LayerNorm over channels -> swish)
Each group output is multiplied by its own SiLU gate path (Mamba-style widening), the
groups are concatenated and sent through ONE output projection (which also acts as the
Conformer's second pointwise projection), post-RMSNorm'd and added to the residual.
Input x: (BATCH, SEQ, D_MODEL) float32. Output: (BATCH, SEQ, D_MODEL).'''

D_MODEL = 1024
BATCH = 1
SEQ = 4096
DEPTH = 1

CHUNK = 64
D_MIX = D_MODEL
D_RWKV = D_MIX // 2
HEAD_DIM = 64
N_HEADS_RWKV = D_RWKV // HEAD_DIM
D_CONV = D_MIX - D_RWKV
CONV_WIDTH = 31
DECAY_LORA = 64
AAA_LORA = 64
MV_LORA = 32
N_SHIFT = 4 * D_RWKV + DECAY_LORA + AAA_LORA
N_IN = N_SHIFT + 3 * D_CONV
RMS_EPS = 1e-6
GN_EPS = 64e-5
LN_EPS = 1e-5

kernel_name = 'hybrid_rwkv7_conformer_conv_trunk'

def rmsnorm(x, g):
    xf = x.astype(jnp.float32)
    y = xf * lax.rsqrt(jnp.mean(xf * xf, axis=-1, keepdims=True) + RMS_EPS)
    return (y * g.astype(jnp.float32)).astype(x.dtype)

def layer_norm(x, g, b):
    xf = x.astype(jnp.float32)
    mu = jnp.mean(xf, axis=-1, keepdims=True)
    var = jnp.mean(jnp.square(xf - mu), axis=-1, keepdims=True)
    y = (xf - mu) * lax.rsqrt(var + LN_EPS) * g.astype(jnp.float32) + b.astype(jnp.float32)
    return y.astype(x.dtype)

def group_norm_heads(o, g, b):
    mu = jnp.mean(o, axis=-1, keepdims=True)
    var = jnp.mean(jnp.square(o - mu), axis=-1, keepdims=True)
    return (o - mu) * lax.rsqrt(var + GN_EPS) * g.astype(jnp.float32) + b.astype(jnp.float32)

def token_shift(p, mu):
    prev = jnp.pad(p, ((0, 0), (1, 0), (0, 0)))[:, :-1]
    return p + (prev - p) * mu

def split_heads(t):
    B, S, _ = t.shape
    return t.reshape(B, S, N_HEADS_RWKV, HEAD_DIM)

def wkv7_scan(r, w, k, v, kk, a):
    B, S, H, N = r.shape

    def step(state, inp):
        r_t, w_t, k_t, v_t, kk_t, a_t = inp
        sa = jnp.einsum('bhvk,bhk->bhv', state, -kk_t)
        state = (state * w_t[:, :, None, :]
                 + sa[..., None] * (kk_t * a_t)[:, :, None, :]
                 + v_t[..., None] * k_t[:, :, None, :])
        y = jnp.einsum('bhvk,bhk->bhv', state, r_t)
        return state, y

    xs = tuple(jnp.moveaxis(t.astype(jnp.float32), 1, 0) for t in (r, w, k, v, kk, a))
    s0 = jnp.zeros((B, H, N, N), jnp.float32)
    _, ys = lax.scan(step, s0, xs)
    return jnp.moveaxis(ys, 0, 1)

def causal_depthwise_conv(x, w, b):
    K, C = w.shape
    out = lax.conv_general_dilated(
        x, w[:, None, :].astype(x.dtype), window_strides=(1,), padding=[(K - 1, 0)],
        dimension_numbers=('NWC', 'WIO', 'NWC'), feature_group_count=C)
    return out + b

def setup_inputs(seed: int = 0) -> dict:
    key = jax.random.key(seed)
    ks = jax.random.split(key, 24)
    f32 = jnp.float32
    nrm = lambda k, shape, s: jax.random.normal(k, shape, f32) * s
    L, Lv = DEPTH, DEPTH - 1
    return {
        'x': nrm(ks[0], (BATCH, SEQ, D_MODEL), 1.0),
        'pre_g': 1.0 + nrm(ks[1], (L, D_MODEL), 0.05),
        'post_g': 1.0 + nrm(ks[2], (L, D_MODEL), 0.05),
        'w_in': nrm(ks[3], (L, D_MODEL, N_IN), D_MODEL ** -0.5),
        'mu_shift': jax.random.uniform(ks[4], (L, N_SHIFT), f32),
        'w0': jax.random.uniform(ks[5], (L, D_RWKV), f32, -5.0, 0.0),
        'w_up': nrm(ks[6], (L, DECAY_LORA, D_RWKV), 0.5 * DECAY_LORA ** -0.5),
        'a0': nrm(ks[7], (L, D_RWKV), 0.1),
        'a_up': nrm(ks[8], (L, AAA_LORA, D_RWKV), AAA_LORA ** -0.5),
        'v0': nrm(ks[9], (Lv, D_RWKV), 0.1),
        'v_down': nrm(ks[10], (Lv, D_RWKV, MV_LORA), D_RWKV ** -0.5),
        'v_up': nrm(ks[11], (Lv, MV_LORA, D_RWKV), MV_LORA ** -0.5),
        'k_k': 0.85 + nrm(ks[12], (L, D_RWKV), 0.05),
        'k_a': 1.0 + nrm(ks[13], (L, D_RWKV), 0.05),
        'r_k': nrm(ks[14], (L, N_HEADS_RWKV, HEAD_DIM), 0.1),
        'gn_g': 1.0 + nrm(ks[15], (L, D_RWKV), 0.05),
        'gn_b': nrm(ks[16], (L, D_RWKV), 0.01),
        'dw_w': nrm(ks[17], (L, CONV_WIDTH, D_CONV), CONV_WIDTH ** -0.5),
        'dw_b': nrm(ks[18], (L, D_CONV), 0.01),
        'ln_g': 1.0 + nrm(ks[19], (L, D_CONV), 0.05),
        'ln_b': nrm(ks[20], (L, D_CONV), 0.01),
        'w_out': nrm(ks[21], (L, D_MIX, D_MODEL), D_MIX ** -0.5),
    }

def reference(x, pre_g, post_g, w_in, mu_shift, w0, w_up, a0, a_up, v0, v_down, v_up,
              k_k, k_a, r_k, gn_g, gn_b, dw_w, dw_b, ln_g, ln_b, w_out):
    B, S, _ = x.shape
    H, N = N_HEADS_RWKV, HEAD_DIM
    v_first = None
    for l in range(DEPTH):
        h = rmsnorm(x, pre_g[l])
        p = h @ w_in[l]

        ps = token_shift(p[..., :N_SHIFT], mu_shift[l])
        r, k, v, z_r = (ps[..., i * D_RWKV:(i + 1) * D_RWKV] for i in range(4))
        wd = ps[..., 4 * D_RWKV:4 * D_RWKV + DECAY_LORA]
        ad = ps[..., 4 * D_RWKV + DECAY_LORA:]

        w_log = -jax.nn.softplus(-(w0[l] + jnp.tanh(wd) @ w_up[l])) - 0.5
        decay = jnp.exp(-jnp.exp(w_log.astype(jnp.float32)))
        a = jax.nn.sigmoid(a0[l] + ad @ a_up[l])
        if l == 0:
            v_first = v
        else:
            nu = jax.nn.sigmoid(v0[l - 1] + (v @ v_down[l - 1]) @ v_up[l - 1])
            v = v + (v_first - v) * nu
        kk = split_heads(k * k_k[l]).astype(jnp.float32)
        kk = kk * lax.rsqrt(jnp.maximum(jnp.sum(kk * kk, axis=-1, keepdims=True), 1e-24))
        k = k * (1.0 + (a - 1.0) * k_a[l])
        rh, kh, vh = split_heads(r), split_heads(k), split_heads(v)
        o = wkv7_scan(rh, split_heads(decay), kh, vh, kk, split_heads(a))
        o = group_norm_heads(o, gn_g[l].reshape(H, N), gn_b[l].reshape(H, N))
        o = o + jnp.sum(rh * kh * r_k[l], axis=-1, keepdims=True).astype(jnp.float32) * vh.astype(jnp.float32)
        y_rwkv = o.reshape(B, S, D_RWKV).astype(x.dtype) * jax.nn.silu(z_r)

        pc = p[..., N_SHIFT:]
        u, gt, z_c = (pc[..., i * D_CONV:(i + 1) * D_CONV] for i in range(3))
        c = causal_depthwise_conv(u * jax.nn.sigmoid(gt), dw_w[l], dw_b[l])
        c = layer_norm(c, ln_g[l], ln_b[l])
        y_conv = jax.nn.silu(c) * jax.nn.silu(z_c)

        out = jnp.concatenate([y_rwkv, y_conv], axis=-1) @ w_out[l]
        x = x + rmsnorm(out, post_g[l])
    return x


_drawn_inputs = setup_inputs


def setup_inputs(seed=0):
    import zlib

    import numpy as np

    out = dict(_drawn_inputs(seed))
    spreads = {}
    factors = {'w_up': 3.283, 'gn_b': 8.0, 'dw_b': 7.358, 'ln_b': 8.0}
    for name, (base, spread) in spreads.items():
        noise = np.random.default_rng([zlib.crc32(name.encode()), seed]).standard_normal(out[name].shape)
        drawn = base * np.exp(spread * noise) if base else spread * noise
        out[name] = __import__('jax').numpy.asarray(drawn.astype(out[name].dtype))
    for name, factor in factors.items():
        out[name] = (out[name] * factor).astype(out[name].dtype)
    return out
```

```python
from contextlib import ExitStack

import numpy as np

import concourse.bass as bass
from concourse import mybir
from concourse.alu_op_type import AluOpType as ALU

F32 = mybir.dt.float32
F32R = mybir.dt.float32r
F16 = mybir.dt.float16
I32 = mybir.dt.int32
ACT = mybir.ActivationFunctionType
AX = mybir.AxisListType.X
RMAX = bass.bass_isa.ReduceOp.max

P = 128
SEQ, D = 4096, 1024
DR = 512
DC = 512
NP = DR // P
HD = 64
NH = DR // HD
CH = 64
TAPS = 31
HALO = TAPS - 1
LORA = 64
NSH = 4 * DR + 2 * LORA
NU = NSH // P
NIN = NSH + 3 * DC
KB = D // P
TB = 512
NB = SEQ // TB
TT = 128
JT = TB // TT
RB = 256
NRB = SEQ // RB
RJ = RB // TT
NT = SEQ // TT
KAPPA = float(np.exp(-0.5))
H_SCALE = 1024.0
W_TOP = 16384.0
RMS_EPS, GN_EPS, LN_EPS = 1e-6, 64e-5, 1e-5
CREDIT = 1
LEVELS = (2, 4, 8, 16, 32)


def shape_constants():
    s = np.arange(P)[:, None]
    t = np.arange(P)[None, :]
    same = s // CH == t // CH
    tc = np.arange(CH)[None, :]
    parts = {
        "ident": s == t,
        "tri": same & (s <= t),
        "strict": same & (s < t),
        "pair0": (t % 2 == 1) & (s == t - 1),
        "mask_r": s % CH <= tc,
        "mask_a": s % CH < tc,
        "heads": s // HD == t // HD,
        "sel2": s // HD == np.arange(2)[None, :],
        "mean": np.full((P, P), 1.0 / DC),
    }
    for b in LEVELS:
        parts[f"level{b}"] = (s // b % 2 == 1) & (t // b == s // b - 1)
    place, at = {}, 0
    for name, a in parts.items():
        place[name] = (at, a.shape[1])
        at += a.shape[1]
    return np.concatenate([a.astype(np.float32) for a in parts.values()], axis=1), place


class Chain:

    def __init__(self, eng, sem):
        self.eng, self.sem, self.n = eng, sem, 0

    def mark(self, ins):
        ins.then_inc(self.sem, 1)
        self.n += 1
        return self.n

    def wait(self, n):
        self.eng.wait_ge(self.sem, n)

    def link(self, ins):
        self.wait(self.mark(ins))

    def restart(self):
        if self.n:
            self.wait(self.n)
            self.eng.sem_clear(self.sem)
        self.n = 0


def rsqrt_small(v, chain, x, y, t):
    chain.link(v.tensor_scalar(y.bitcast(I32), x.bitcast(I32), 1, None, ALU.logical_shift_right))
    chain.link(v.tensor_scalar(y.bitcast(I32), y.bitcast(I32), -1.0, float(0x5F3759DF), ALU.mult, ALU.add))
    for _ in range(3):
        chain.link(v.tensor_tensor(t, x, y, ALU.mult))
        chain.link(v.scalar_tensor_tensor(t, t, -0.5, y, ALU.mult, ALU.mult))
        chain.link(v.scalar_tensor_tensor(y, t, 1.5, y, ALU.add, ALU.mult))


def weights_phase(nc, w_in, pre_g, whi_r, wlo_r, whi_c, wlo_c, unscale):
    with ExitStack() as ctx:
        sb = lambda name, shape, dt=F32: ctx.enter_context(nc.sbuf_tensor(name, shape, dt))
        sem = lambda name: ctx.enter_context(nc.semaphore(name))
        wbuf = sb("w_stage", [P, 3, NIN])
        wmax = sb("w_max", [P, KB])
        gcol = sb("pre_g_col", [P, KB])
        m2 = sb("w_m2", [P, 2])
        m2a = sb("w_m2a", [P, 2])
        pw = sb("w_pow", [P, 4])
        gs = sb("pre_g_scaled", [P, KB])
        w_loaded = [sem(f"w_loaded{b}") for b in range(3)]
        g_loaded = sem("g_loaded")
        w_freed = sem("w_freed")
        w_ready = sem("w_scaled")
        hi_done = sem("w_hi_done")
        max_ready = sem("w_max_ready")
        max_all = sem("w_max_all")
        vch = sem("w_vchain")
        block = ctx.enter_context(nc.Block())

        @block.sync
        def _(sp):
            with nc.allow_non_contiguous_dma("64 columns of one number"):
                sp.dma_start(gcol[:], pre_g.rearrange("a (k p) -> p (a k)", p=P)).then_inc(g_loaded, 16)
            for n in range(2 * KB):
                if n >= 3:
                    sp.wait_ge(w_freed, n - 2)
                kb = n % KB
                sp.dma_start(wbuf[:, n % 3, :], w_in[0, kb * P:(kb + 1) * P, :]).then_inc(w_loaded[n % 3], 16)

        @block.gpsimd
        def _(pool):
            pool.wait_ge(max_ready, 1)
            nc.gpsimd.partition_all_reduce(m2a[:], m2[:], P, RMAX).then_inc(max_all, 1)

        @block.vector
        def _(v):
            ch = Chain(v, vch)
            for n in range(KB):
                v.wait_ge(w_loaded[n % 3], 16 * (n // 3 + 1))
                v.tensor_reduce(wmax[:, n:n + 1], wbuf[:, n % 3, :], AX, ALU.max,
                                apply_absolute_value=True).then_inc(w_freed, 1)
            v.wait_ge(w_freed, KB)
            ch.link(v.tensor_reduce(m2[:, 0:1], wmax[:], AX, ALU.max))
            v.wait_ge(g_loaded, 16)
            v.tensor_reduce(m2[:, 1:2], gcol[:], AX, ALU.max, apply_absolute_value=True).then_inc(max_ready, 1)
            v.wait_ge(max_all, 1)
            ch.link(v.tensor_scalar(pw[:, 0:1], m2a[:, 0:1], m2a[:, 1:2], 1e-30, ALU.mult, ALU.max))
            ch.link(v.tensor_scalar(pw[:, 1:2].bitcast(I32), pw[:, 0:1].bitcast(I32), 0x7F800000, None,
                                    ALU.bitwise_and))
            ch.link(v.reciprocal(pw[:, 2:3], pw[:, 1:2]))
            ch.link(v.tensor_scalar(pw[:, 3:4], pw[:, 2:3], W_TOP, None, ALU.mult))
            ch.link(v.tensor_scalar(gs[:], gcol[:], pw[:, 3:4], None, ALU.mult))
            ch.link(v.tensor_scalar(unscale, pw[:, 1:2], 1.0 / (W_TOP * H_SCALE), None, ALU.mult))
            for kb in range(KB):
                n = KB + kb
                v.wait_ge(w_loaded[n % 3], 16 * (n // 3 + 1))
                v.tensor_scalar(wbuf[:, n % 3, :], wbuf[:, n % 3, :], gs[:, kb:kb + 1], None,
                                ALU.mult).then_inc(w_ready, 1)
                v.wait_ge(hi_done, 2 * kb + 2)
                v.tensor_tensor(wlo_r[:, kb, :], wbuf[:, n % 3, 0:NSH], whi_r[:, kb, :], ALU.subtract)
                v.tensor_tensor(wlo_c[:, kb, :], wbuf[:, n % 3, NSH:NIN], whi_c[:, kb, :],
                                ALU.subtract).then_inc(w_freed, 1)

        @block.scalar
        def _(act):
            for kb in range(KB):
                n = KB + kb
                act.wait_ge(w_ready, kb + 1)
                act.activation(whi_r[:, kb, :], wbuf[:, n % 3, 0:NSH], ACT.Copy).then_inc(hi_done, 1)
                act.activation(whi_c[:, kb, :], wbuf[:, n % 3, NSH:NIN], ACT.Copy).then_inc(hi_done, 1)


def conv_phase(nc, cst, x, dw_w, dw_b, ln_g, ln_b, whi, wlo, unscale, ht_dram, y_dram):
    with ExitStack() as ctx:
        sb = lambda name, shape, dt=F32: ctx.enter_context(nc.sbuf_tensor(name, shape, dt))
        ps = lambda name, shape, dt=F32: ctx.enter_context(nc.psum_tensor(name, shape, dt))
        sem = lambda name: ctx.enter_context(nc.semaphore(name))
        xt = sb("c_x", [P, JT, D])
        hh = sb("c_h_hi", [P, D], F16)
        hl = sb("c_h_lo", [P, D], F16)
        ht = sb("c_hT", [P, 2, KB, TB], F16)
        ident16 = sb("c_ident16", [P, P], F16)
        ss = sb("c_ss", [P, JT])
        rs = sb("c_rs", [P, JT])
        rt = sb("c_rt", [P, JT])
        gate = sb("c_gate", [P, TB])
        G = sb("c_glu", [P, NP, HALO + TB])
        acc = sb("c_acc", [P, NP, TB])
        odd = sb("c_acc_odd", [P, TB])
        tz = sb("c_tanh_z", [P, TB])
        sz = sb("c_silu_z", [P, NP, TB])
        sq = sb("c_sq", [P, NP, TB])
        std = sb("c_std", [P, TB])
        tn = sb("c_tanh_n", [P, NP, TB])
        wcv = sb("c_w", [P, NP, TAPS])
        cols = sb("c_cols", [P, 3, NP])
        half = sb("c_half", [P, 4])
        tp = [ps(f"c_tp{b}", [P, KB, P], F16) for b in range(2)]
        pj = [ps(f"c_pj{b}", [P, TB]) for b in range(3)]
        pst = ps("c_stat", [P, 2, TB])
        x_loaded, c_loaded = sem("c_x_loaded"), sem("c_const_loaded")
        ss_ready = sem("c_ss_ready")
        rs_ready = sem("c_rs_ready")
        hi_ready = sem("c_hi_ready")
        lo_ready = sem("c_lo_ready")
        tp_filled, tp_drained = sem("c_tp_filled"), sem("c_tp_drained")
        ht_stored = sem("c_hT_stored")
        pj_filled = sem("c_pj_filled")
        gate_ready = sem("c_gate_ready")
        glu_ready = sem("c_glu_ready")
        tz_ready = sem("c_tz_ready")
        sz_ready = sem("c_sz_ready")
        acc_ready = sem("c_acc_ready")
        mean_filled = sem("c_mean_filled")
        cen_ready = sem("c_centred")
        sq_ready = sem("c_sq_ready")
        var_filled = sem("c_var_filled")
        std_ready = sem("c_std_ready")
        n_ready = sem("c_norm_ready")
        aff_ready = sem("c_affine_ready")
        tn_ready = sem("c_tanh_n_ready")
        y_ready, y_stored = sem("c_y_ready"), sem("c_y_stored")
        vch = sem("c_vchain")
        ech = sem("c_echain")
        setup = sem("c_setup")
        block = ctx.enter_context(nc.Block())
        x_v = x[0].rearrange("(n j p) d -> n p j d", p=P, j=JT)

        @block.sync
        def _(sp):
            for credited in (ss_ready, rs_ready, hi_ready, lo_ready, tp_filled, tp_drained, ht_stored, pj_filled,
                             gate_ready, glu_ready, tz_ready, sz_ready, acc_ready, mean_filled, cen_ready, sq_ready,
                             var_filled, std_ready, n_ready, aff_ready, tn_ready, y_ready, y_stored):
                sp.sem_inc(credited, CREDIT)
            with nc.allow_non_contiguous_dma("small constants"):
                for b in range(NP):
                    sp.dma_start(wcv[:, b, :], dw_w[0, :, b * P:(b + 1) * P].rearrange("t p -> p t")).then_inc(c_loaded, 16)
                for k, c in enumerate((dw_b, ln_g, ln_b)):
                    sp.dma_start(cols[:, k, :], c.rearrange("a (b p) -> p (a b)", p=P)).then_inc(c_loaded, 16)
            sp.dma_start(xt[:], x_v[0]).then_inc(x_loaded, 16)

            def block_io(i, following):
                if following is not None:
                    sp.wait_ge(hi_ready, CREDIT + i * JT + JT)
                    sp.wait_ge(lo_ready, CREDIT + i * JT + JT)
                    sp.dma_start(xt[:], x_v[following]).then_inc(x_loaded, 16)
                sp.wait_ge(tp_drained, CREDIT + i * 8 + 8)
                for b in range(TB // RB):
                    sp.dma_start(ht_dram[i * (TB // RB) + b], ht[:, :, :, b * RB:(b + 1) * RB]).then_inc(ht_stored, 16)
                sp.wait_ge(y_ready, CREDIT + i * NP + NP)
                sp.dma_start(y_dram[:, bass.ts(i, TB)].rearrange("(b p) t -> p b t", p=P),
                             acc[:]).then_inc(y_stored, 16)

            with sp.Fori(0, NB - 1) as i:
                block_io(i, i + 1)
            block_io(NB - 1, None)
            sp.wait_ge(y_stored, CREDIT + NB * 16)
            sp.wait_ge(ht_stored, CREDIT + NB * 32)

        @block.scalar
        def _(act):
            ch = Chain(act, ech)
            act.wait_ge(setup, 2)
            with act.Fori(0, NB) as i:
                act.wait_ge(x_loaded, i * 16 + 16)
                for j in range(JT):
                    if j == 0:
                        act.wait_ge(std_ready, CREDIT + i)
                    last = act.activation(sq[:, 0:2, :], xt[:, j, :].rearrange("p (a b) -> p a b", a=2), ACT.Square,
                                          accum_out=ss[:, j:j + 1])
                    if j < JT - 1:
                        ch.link(last)
                last.then_inc(ss_ready, 1)
                act.wait_ge(ss_ready, CREDIT + i + 1)
                act.wait_ge(rs_ready, CREDIT + i + 1)
                for j in range(JT):
                    act.wait_ge(tp_filled, CREDIT + i * 8 + 2 * j)
                    act.activation(hh[:], xt[:, j, :], ACT.Copy, scale=rs[:, j:j + 1]).then_inc(hi_ready, 1)
                    if j == 0:
                        act.wait_ge(ht_stored, CREDIT + i * 32)
                        act.wait_ge(pj_filled, CREDIT + i * 12)
                    for part in range(2):
                        act.wait_ge(tp_filled, CREDIT + i * 8 + 2 * j + part + 1)
                        act.activation(ht[:, part, :, j * P:(j + 1) * P], tp[part][:], ACT.Copy).then_inc(tp_drained, 1)
                for b in range(NP):
                    act.wait_ge(pj_filled, CREDIT + i * 12 + 3 * b + 1)
                    act.wait_ge(glu_ready, CREDIT + i * NP + b)
                    act.activation(gate[:], pj[0][:], ACT.Tanh, scale=half[:, 0:1]).then_inc(gate_ready, 1)
                    act.wait_ge(pj_filled, CREDIT + i * 12 + 3 * b + 3)
                    act.wait_ge(sz_ready, CREDIT + i * NP + b)
                    act.activation(tz[:], pj[2][:], ACT.Tanh, scale=half[:, 0:1]).then_inc(tz_ready, 1)
                ch.restart()
                act.wait_ge(cen_ready, CREDIT + i * NP + NP)
                act.activation(sq[:], acc[:], ACT.Square).then_inc(sq_ready, 1)
                act.wait_ge(var_filled, CREDIT + i + 1)
                act.activation(std[:], pst[:, 1, :], ACT.Sqrt, bias=half[:, 2:3]).then_inc(std_ready, 1)
                for b in range(NP):
                    act.wait_ge(n_ready, CREDIT + i * NP + b + 1)
                    act.activation(acc[:, b, :], acc[:, b, :], ACT.Identity, scale=cols[:, 1, b:b + 1],
                                   bias=cols[:, 2, b:b + 1]).then_inc(aff_ready, 1)
                act.wait_ge(aff_ready, CREDIT + i * NP + NP)
                act.wait_ge(y_ready, CREDIT + i * NP)
                act.activation(tn[:], acc[:], ACT.Tanh, scale=0.5).then_inc(tn_ready, 1)

        @block.vector
        def _(v):
            ch = Chain(v, vch)
            ch.link(v.tensor_copy(ident16[:], cst("ident")))
            v.wait_ge(c_loaded, 16 * (NP + 3))
            ch.link(v.tensor_scalar(half[:, 0:1], unscale, 0.5, None, ALU.mult))
            ch.link(v.tensor_scalar(half[:, 1:2], unscale, 0.25, None, ALU.mult))
            ch.link(v.memset(half[:, 2:3], LN_EPS))
            ch.link(v.memset(half[:, 3:4], 0.0))
            v.tensor_scalar(wcv[:], wcv[:], half[:, 0:1], None, ALU.mult).then_inc(setup, 1)
            v.memset(G[:], 0.0).then_inc(setup, 1)
            v.wait_ge(setup, 2)
            ch.restart()
            with v.Fori(0, NB) as i:
                v.wait_ge(ss_ready, CREDIT + i + 1)
                ch.link(v.tensor_scalar(rt[:], ss[:], 1.0 / D, RMS_EPS, ALU.mult, ALU.add))
                v.wait_ge(hi_ready, CREDIT + i * JT)
                rsqrt_small(v, ch, rt[:], rs[:], ss[:])
                v.tensor_scalar(rs[:], rs[:], H_SCALE, None, ALU.mult).then_inc(rs_ready, 1)
                v.wait_ge(rs_ready, CREDIT + i + 1)
                for j in range(JT):
                    v.wait_ge(hi_ready, CREDIT + i * JT + j + 1)
                    v.wait_ge(tp_filled, CREDIT + i * 8 + 2 * j)
                    v.scalar_tensor_tensor(hl[:], xt[:, j, :], rs[:, j:j + 1], hh[:], ALU.mult,
                                           ALU.subtract).then_inc(lo_ready, 1)
                for b in range(NP):
                    v.wait_ge(pj_filled, CREDIT + i * 12 + 3 * b + 2)
                    v.wait_ge(gate_ready, CREDIT + i * NP + b + 1)
                    v.scalar_tensor_tensor(G[:, b, HALO:], gate[:], 1.0, pj[1][:], ALU.add,
                                           ALU.mult).then_inc(glu_ready, 1)
                    v.wait_ge(tz_ready, CREDIT + i * NP + b + 1)
                    v.scalar_tensor_tensor(sz[:, b, :], tz[:], 1.0, pj[2][:], ALU.add, ALU.mult).then_inc(sz_ready, 1)
                    if b == 0:
                        v.wait_ge(y_stored, CREDIT + i * 16)
                    v.wait_ge(glu_ready, CREDIT + i * NP + b + 1)
                    chains = [ch.mark(v.tensor_scalar(acc[:, b, :], G[:, b, 0:TB], wcv[:, b, 0:1], cols[:, 0, b:b + 1],
                                                      ALU.mult, ALU.add)),
                              ch.mark(v.tensor_scalar(odd[:], G[:, b, 1:1 + TB], wcv[:, b, 1:2], None, ALU.mult))]
                    for t in range(2, TAPS):
                        o = acc[:, b, :] if t % 2 == 0 else odd[:]
                        ch.wait(chains[t % 2])
                        chains[t % 2] = ch.mark(v.scalar_tensor_tensor(o, G[:, b, t:t + TB], wcv[:, b, t:t + 1], o,
                                                                       ALU.mult, ALU.add))
                    ch.wait(max(chains))
                    v.tensor_tensor(acc[:, b, :], acc[:, b, :], odd[:], ALU.add).then_inc(acc_ready, 1)
                    v.wait_ge(acc_ready, CREDIT + i * NP + b + 1)
                    ch.link(v.tensor_copy(G[:, b, 0:HALO], G[:, b, TB:TB + HALO]))
                    ch.restart()
                v.wait_ge(mean_filled, CREDIT + i + 1)
                for b in range(NP):
                    v.tensor_tensor(acc[:, b, :], acc[:, b, :], pst[:, 0, :], ALU.subtract).then_inc(cen_ready, 1)
                v.wait_ge(std_ready, CREDIT + i + 1)
                v.wait_ge(cen_ready, CREDIT + i * NP + NP)
                ch.link(v.reciprocal(std[:], std[:]))
                v.wait_ge(sq_ready, CREDIT + i + 1)
                for b in range(NP):
                    v.tensor_tensor(acc[:, b, :], acc[:, b, :], std[:], ALU.mult).then_inc(n_ready, 1)
                v.wait_ge(tn_ready, CREDIT + i + 1)
                v.wait_ge(sz_ready, CREDIT + i * NP + NP)
                for b in range(NP):
                    m = ch.mark(v.scalar_tensor_tensor(tn[:, b, :], tn[:, b, :], 1.0, acc[:, b, :], ALU.add, ALU.mult))
                ch.wait(m)
                for b in range(NP):
                    v.scalar_tensor_tensor(acc[:, b, :], tn[:, b, :], half[:, 1:2], sz[:, b, :], ALU.mult,
                                           ALU.mult).then_inc(y_ready, 1)
                ch.restart()

        @block.tensor
        def _(pe):
            pe.wait_ge(setup, 2)
            with pe.Fori(0, NB) as i:
                for j in range(JT):
                    for part, (ready, src) in enumerate(((hi_ready, hh), (lo_ready, hl))):
                        pe.wait_ge(ready, CREDIT + i * JT + j + 1)
                        pe.wait_ge(tp_drained, CREDIT + (i * 8 + 2 * j + part - 1 if (j or part) else i * 8))
                        for kb in range(KB):
                            last = pe.transpose(tp[part][:, kb, :], src[:, kb * P:(kb + 1) * P], ident16[:])
                        last.then_inc(tp_filled, 1)
                pe.wait_ge(tp_drained, CREDIT + i * 8 + 8)
                for b in range(NP):
                    for n, unit in enumerate((NP + b, b, 2 * NP + b)):
                        pe.wait_ge(sz_ready if n == 2 else glu_ready, CREDIT + i * NP + b)
                        project(pe, pj[n][:], whi, wlo, ht, unit).then_inc(pj_filled, 1)
                pe.wait_ge(acc_ready, CREDIT + i * NP + NP)
                for b in range(NP):
                    last = pe.matmul(pst[:, 0, :], cst("mean"), acc[:, b, :], start=b == 0, stop=b == NP - 1)
                last.then_inc(mean_filled, 1)
                pe.wait_ge(sq_ready, CREDIT + i + 1)
                for b in range(NP):
                    last = pe.matmul(pst[:, 1, :], cst("mean"), sq[:, b, :], start=b == 0, stop=b == NP - 1)
                last.then_inc(var_filled, 1)


def project_steps(pe, out, whi, wlo, ht, unit):
    cols = slice(unit * P, (unit + 1) * P)
    for kb in range(KB):
        for n, (w, part) in enumerate(((whi, 0), (whi, 1), (wlo, 0))):
            yield pe.matmul(out, w[:, kb, cols], ht[:, part, kb, :], start=kb == 0 and n == 0,
                            stop=kb == KB - 1 and n == 2)


def project(pe, out, whi, wlo, ht, unit):
    for last in project_steps(pe, out, whi, wlo, ht, unit):
        pass
    return last


def tile_uses():
    uses = [("lora_w", 1), ("lora_a", 1), ("kk_sum", 1), ("cum", 1), ("kk_scale", 1), ("bonus", 1),
            ("bkT0", 1), ("bkT1", 1), ("avT0", 2), ("avT1", 2), ("aa0", 1), ("aa1", 1), ("aa2", 1), ("aa3", 1),
            ("lt0", 1), ("lt1", 1), ("ut0", 1), ("ut1", 1)]
    for b in LEVELS:
        uses += [(f"q{b}_{g}", 1) for g in range(2)] + [(f"d{b}_{g}", 1) for g in range(2)]
        if b != LEVELS[-1]:
            uses += [(f"t{b}_{g}", 1) for g in range(2)]
    uses += [("akv", 1), ("x0", 2), ("x1", 2), ("rm0", 1), ("rm1", 1), ("sy0_0", 2), ("sy0_1", 2), ("sy1_0", 2), ("sy1_1", 2),
             ("yT", 1)]
    return uses


USES = tile_uses()
ORDER = {name: n for n, (name, _) in enumerate(USES)}
RING = 6
PER_BANK = [len(USES[b::RING]) for b in range(RING)]
DRAINS = [sum(d for n, (_, d) in enumerate(USES) if n % RING == b) for b in range(RING)]
SLICE = 4


def units_of(j):
    per = (NU - 1) // RJ
    return list(range(j * per, (j + 1) * per)) + ([NU - 1] if j == RJ - 1 else [])


def slices_due(j, n):
    total = len(units_of(j)) * 24 // SLICE
    return -(-(n + 1) * total // len(USES))


class Tile:

    def __init__(self, i, j, filled, drained):
        self.i, self.j, self.filled_sems, self.drained_sems = i, j, filled, drained

    def count(self, per_tile, k):
        return self.i * (RJ * per_tile) + (self.j * per_tile + k)

    def before_fill(self, eng, name):
        n = ORDER[name]
        b = n % RING
        eng.wait_ge(self.drained_sems[b], CREDIT + self.count(DRAINS[b], sum(d for _, d in USES[b:n:RING])))

    def filled(self, ins, name):
        ins.then_inc(self.filled_sems[ORDER[name] % RING], 1)

    def wait_filled(self, eng, name):
        n = ORDER[name]
        eng.wait_ge(self.filled_sems[n % RING], CREDIT + self.count(PER_BANK[n % RING], n // RING + 1))

    def drained(self, ins, name):
        ins.then_inc(self.drained_sems[ORDER[name] % RING], 1)

    def wait_drained(self, eng, name):
        n = ORDER[name]
        b = n % RING
        eng.wait_ge(self.drained_sems[b], CREDIT + self.count(DRAINS[b], sum(d for _, d in USES[b:n + 1:RING])))


def rwkv_phase(nc, cst, inp, whi, wlo, unscale, ht_dram, y_dram):
    with ExitStack() as ctx:
        sb = lambda name, shape, dt=F32: ctx.enter_context(nc.sbuf_tensor(name, shape, dt))
        ps = lambda name, shape, dt=F32: ctx.enter_context(nc.psum_tensor(name, shape, dt))
        sem = lambda name: ctx.enter_context(nc.semaphore(name))
        ht = sb("r_hT", [P, 2, KB, RB], F16)
        raw = sb("r_raw", [P, 2, RB + 1])
        keep = sb("r_keep", [P, 2, RB])
        carry = sb("r_carry", [P, NU])
        mix = sb("r_mix", [P, NU - 1, 2 * RB])
        lora = sb("r_lora", [P, RB])
        lw = sb("r_lw", [P, DR])
        la = sb("r_a", [P, NP, TT])
        kk = sb("r_kk", [P, NP, TT])
        sq = sb("r_sq", [P, NP, TT])
        rn = sb("r_rn", [P, 3, NH])
        rnb = sb("r_rnb", [P, NH, HD])
        km = sb("r_kmod", [P, NP, TT])
        W = sb("r_W", [P, NP * 2, CH + 1])
        Wi = sb("r_Winv", [P, NP * 2, CH])
        bonv = sb("r_bonus", [P, NP, TT])
        BK = sb("r_BK", [P, NP * 2, 2 * CH])
        RAV = sb("r_RAV", [P, NP * 2, 3 * CH])
        FB = sb("r_FB", [P, 2, NP, 4 * HD])
        AkT = sb("r_AkT", [P, 2, NH, CH])
        XA = sb("r_XA", [P, NH, 2 * HD])
        XG = sb("r_XG", [P, 2, NH, 2 * HD])
        LT = sb("r_LT", [P, NH, TT])
        U = sb("r_U", [P, NH, TT])
        UT = sb("r_UT", [P, NH, TT])
        Q = sb("r_Q", [P, NH, TT])
        t1, yg = U[:, 0:NP, :], Q[:, 0:NP, :]
        RM = sb("r_RM", [P, 2, NP, 2 * HD])
        S = sb("r_S", [P, NP, HD])
        Y = sb("r_Y", [P, NP, 2, HD])
        sz = sb("r_sz", [P, NP, TT])
        yo = sb("r_yo", [P, 2, NP, TT])
        w0b = sb("r_w0", [P, DR])
        lup = sb("r_lora_up", [P, DR])
        rk1 = sb("r_rk_ones", [P, NP, P])
        vec = sb("r_vec", [P, 6, NP])
        omk = sb("r_1_k_a", [P, NP])
        mu = sb("r_mu", [P, NU])
        mq = sb("r_1_mu", [P, NU])
        pj = [ps(f"r_pj{b}", [P, RB]) for b in range(2)]
        bank = [ps(f"r_bank{b}", [P, 512]) for b in range(RING)]
        filled = [sem(f"r_filled{b}") for b in range(RING)]
        drained = [sem(f"r_drained{b}") for b in range(RING)]
        c_loaded, ht_loaded = sem("r_const_loaded"), sem("r_hT_loaded")
        pj_filled = [sem(f"r_pj_filled{b}") for b in range(2)]
        pj_drained = [sem(f"r_pj_drained{b}") for b in range(2)]
        shifted = sem("r_shifted")
        lora_ready = sem("r_lora_ready")
        tw_ready, ta_ready = sem("r_tanh_w"), sem("r_tanh_a")
        kk_ready, sq_ready = sem("r_kk_ready"), sem("r_sq_ready")
        ld_ready, rk_ready = sem("r_decay_ready"), sem("r_rk_ready")
        ops_ready, v_ready = sem("r_ops_ready"), sem("r_v_ready")
        ut_ready = sem("r_ut_ready")
        yc_ready, yq_ready, yn_ready = sem("r_y_centred"), sem("r_y_squared"), sem("r_y_normed")
        tz_ready = sem("r_tanh_z")
        y_ready = sem("r_y_ready")
        y_stored = [sem(f"r_y_stored{b}") for b in range(2)]
        vch, ech, setup = sem("r_vchain"), sem("r_echain"), sem("r_setup")
        passed = sem("r_passed")
        block = ctx.enter_context(nc.Block())
        y_v = y_dram.rearrange("(b p) t -> p b t", p=P)

        def pj_count(n, u):
            b = u % 2
            return n * ((NU + 1 - b) // 2) + u // 2

        def heads4(name):
            return bank[ORDER[name] % RING][:].rearrange("p (h t) -> p h t", h=4)

        def heads8(name):
            return bank[ORDER[name] % RING][:].rearrange("p (h t) -> p h t", h=8)

        def flat(name):
            return bank[ORDER[name] % RING][:]

        def chunks(name):
            return bank[ORDER[name] % RING][:].rearrange("p (c t) -> p c t", t=CH)

        def bc(col, n):
            return col.unsqueeze(2).to_broadcast([P, col.shape[1], n])

        def by_pair(a):
            return a.rearrange("p (g a) d -> p a g d", g=2)

        def part(group, i, j):
            return mix[:, group * NP:(group + 1) * NP, bass.ds((i % 2) * RB + j * TT, TT)]

        @block.sync
        def _(sp):
            for credited in (*filled, *drained, *pj_filled, *pj_drained, *y_stored, shifted, lora_ready, tw_ready,
                             ta_ready, kk_ready, sq_ready, ld_ready, rk_ready, ops_ready, v_ready, ut_ready,
                             yc_ready, yq_ready, yn_ready, tz_ready, y_ready):
                sp.sem_inc(credited, CREDIT)
            with nc.allow_non_contiguous_dma("small constants"):
                for k, name in enumerate(("a0", "k_k", "k_a", "r_k", "gn_g", "gn_b")):
                    src = inp[name].rearrange("a h d -> a (h d)") if name == "r_k" else inp[name]
                    sp.dma_start(vec[:, k, :], src.rearrange("a (b p) -> p (a b)", p=P)).then_inc(c_loaded, 16)
                sp.dma_start(mu[:], inp["mu_shift"].rearrange("a (b p) -> p (a b)", p=P)).then_inc(c_loaded, 16)
                sp.dma_start(w0b[:], inp["w0"][0:1, :].to_broadcast([P, DR])).then_inc(c_loaded, 16)
            sp.dma_start(lup[0:LORA, :], inp["w_up"][0]).then_inc(c_loaded, 16)
            sp.dma_start(lup[LORA:P, :], inp["a_up"][0]).then_inc(c_loaded, 16)
            sp.dma_start(ht[:], ht_dram[0]).then_inc(ht_loaded, 16)

            def stores(i):
                for j in range(RJ):
                    sp.wait_ge(y_ready, CREDIT + i * RJ + j + 1)
                    sp.dma_start(y_v[:, 0:NP, bass.ds(i * RB + j * TT, TT)], yo[:, j]).then_inc(y_stored[j], 16)

            with sp.Fori(0, NRB - 1) as i:
                sp.wait_ge(pj_filled[0], CREDIT + pj_count(i, NU - 1) + 1)
                sp.dma_start(ht[:], ht_dram[i + 1]).then_inc(ht_loaded, 16)
                stores(i)
            stores(NRB - 1)
            for j in range(RJ):
                sp.wait_ge(y_stored[j], CREDIT + NRB * 16)

        @block.scalar
        def _(act):
            ch = Chain(act, ech)

            def drain_unit(n, u):
                b = u % 2
                act.wait_ge(shifted, CREDIT + (n * NU + u - 1 if u else n * NU))
                act.activation(raw[:, b, 0:1], carry[:, u:u + 1], ACT.Copy)
                act.wait_ge(pj_filled[b], CREDIT + pj_count(n, u) + 1)
                act.activation(raw[:, b, 1:], pj[b][:], ACT.Copy, scale=unscale)
                act.activation(keep[:, b, :], pj[b][:], ACT.Copy, scale=mq[:, u:u + 1]).then_inc(pj_drained[b], 1)

            def lora_tanh(n):
                act.wait_ge(shifted, CREDIT + n * NU + NU)
                act.activation(lora[0:LORA, :], lora[0:LORA, :], ACT.Tanh).then_inc(lora_ready, 1)

            def tile(i, j, beside):
                t = Tile(i, j, filled, drained)
                todo = units_of(j) if beside else []
                taken = [0]

                def hook(name):
                    while taken[0] < len(todo) and slices_due(j, ORDER[name]) * SLICE >= 24 * (taken[0] + 1):
                        u = todo[taken[0]]
                        drain_unit(i + 1, u)
                        if u == NU - 1:
                            lora_tanh(i + 1)
                        taken[0] += 1

                act.wait_ge(shifted, CREDIT + i * NU + NU)
                act.wait_ge(kk_ready, CREDIT + t.count(1, 1))
                act.activation(sq[:], kk[:], ACT.Square).then_inc(sq_ready, 1)
                t.wait_drained(act, "lora_w")
                act.activation(lw[:], lw[:], ACT.Tanh, scale=0.5).then_inc(tw_ready, 1)
                t.wait_drained(act, "lora_a")
                act.activation(la[:], la[:], ACT.Tanh, scale=0.5).then_inc(ta_ready, 1)
                act.activation(RAV[:, :, 2 * CH:].rearrange("p (a c) t -> p a c t", c=2),
                               part(2, i, j).rearrange("p a (c t) -> p a c t", c=2), ACT.Copy).then_inc(v_ready, 1)
                t.wait_filled(act, "cum")
                act.activation(W[:, :, 1:], chunks("cum"), ACT.Exp)
                t.drained(act.activation(Wi[:], chunks("cum"), ACT.Exp, scale=-1.0), "cum")
                act.activation(sz[:], part(3, i, j), ACT.Tanh, scale=0.5).then_inc(tz_ready, 1)
                hook("bonus")
                for c in range(2):
                    t.wait_filled(act, f"bkT{c}")
                    src = heads4(f"bkT{c}").rearrange("p a (h d) -> p a h d", h=2)
                    t.drained(act.activation(FB[:, c].rearrange("p a (h d) -> p a h d", h=4)[:, :, 0:4:3, :], src,
                                             ACT.Copy), f"bkT{c}")
                    t.wait_filled(act, f"avT{c}")
                    t.drained(act.activation(by_pair(XG[CH:, c, :, HD:]),
                                             heads4(f"avT{c}")[CH:].rearrange("p a (g d) -> p a g d", g=2), ACT.Copy), f"avT{c}")
                hook("aa3")
                for g in range(2):
                    t.wait_filled(act, f"ut{g}")
                    t.drained(act.activation(U[:, 4 * g:4 * g + 4, :], heads4(f"ut{g}"), ACT.Copy), f"ut{g}")
                for b in LEVELS[:-1]:
                    hook(f"d{b}_0")
                    for g in range(2):
                        t.wait_filled(act, f"t{b}_{g}")
                        t.drained(act.activation(U[:, 4 * g:4 * g + 4, :], heads4(f"t{b}_{g}"), ACT.Copy), f"t{b}_{g}")
                hook(f"d{LEVELS[-1]}_0")
                t.wait_filled(act, "akv")
                t.drained(act.activation(XA[:, :, HD:], heads8("akv"), ACT.Copy), "akv")
                for g in range(2):
                    t.wait_filled(act, f"x{g}")
                    t.drained(act.activation(XG[0:CH, 0, 4 * g:4 * g + 4, :], heads4(f"x{g}")[0:CH], ACT.Copy), f"x{g}")
                hook("rm1")
                for c in range(2):
                    for g in range(2):
                        rows = slice((1 - g) * CH, (2 - g) * CH)
                        t.wait_filled(act, f"sy{c}_{g}")
                        t.drained(act.activation(Y[c * CH:(c + 1) * CH, :, g, :], heads8(f"sy{c}_{g}")[rows, 0:NP],
                                                 ACT.Copy), f"sy{c}_{g}")
                act.wait_ge(yc_ready, CREDIT + t.count(1, 1))
                act.activation(yg[:], Y[:].rearrange("p a h d -> p a (h d)"), ACT.Square).then_inc(yq_ready, 1)
                t.wait_filled(act, "yT")
                for p in range(NP):
                    last = act.activation(yg[:, p, :], heads4("yT")[:, p, :], ACT.Identity, scale=vec[:, 4, p:p + 1],
                                          bias=vec[:, 5, p:p + 1])
                t.drained(last, "yT")
                hook("yT")

            act.wait_ge(setup, 2)
            for u in range(NU):
                drain_unit(0, u)
            lora_tanh(0)
            with act.Fori(0, NRB - 1) as i:
                for j in range(RJ):
                    tile(i, j, True)
            for j in range(RJ):
                tile(NRB - 1, j, False)

        @block.vector
        def _(v):
            ch = Chain(v, vch)
            MUL, ADD = ALU.mult, ALU.add
            level = {b: cst(f"level{b}") for b in LEVELS}

            def over4(mask):
                return mask.unsqueeze(1).to_broadcast([mask.shape[0], 4, mask.shape[1]])

            def shift_unit(n, u):
                b = u % 2
                v.wait_ge(pj_drained[b], CREDIT + pj_count(n, u) + 1)
                dst = lora[:] if u == NU - 1 else mix[:, u, bass.ds((n % 2) * RB, RB)]
                v.tensor_copy(carry[:, u:u + 1], raw[:, b, RB:])
                v.scalar_tensor_tensor(dst, raw[:, b, 0:RB], mu[:, u:u + 1], keep[:, b, :], MUL,
                                       ADD).then_inc(shifted, 1)

            def tile(i, j, beside):
                t = Tile(i, j, filled, drained)
                todo = units_of(j) if beside else []
                taken = [0]

                def hook(name):
                    while taken[0] < len(todo) and slices_due(j, ORDER[name]) * SLICE >= 24 * (taken[0] + 1):
                        shift_unit(i + 1, todo[taken[0]])
                        taken[0] += 1

                ch.restart()
                r, k, vv, z = (part(g, i, j) for g in range(4))
                v.wait_ge(shifted, CREDIT + i * NU + NU)
                v.tensor_tensor(kk[:], k, bc(vec[:, 1, :], TT), MUL).then_inc(kk_ready, 1)
                t.wait_filled(v, "lora_w")
                t.drained(v.tensor_tensor(lw[:], flat("lora_w"), w0b[:], ADD), "lora_w")
                t.wait_filled(v, "lora_a")
                t.drained(v.tensor_tensor(la[:], heads4("lora_a"), bc(vec[:, 0, :], TT), ADD), "lora_a")
                v.wait_ge(tw_ready, CREDIT + t.count(1, 1))
                v.tensor_scalar(lw[:], lw[:], -KAPPA / 2, -KAPPA / 2, MUL, ADD).then_inc(ld_ready, 1)
                t.wait_filled(v, "kk_sum")
                m = ch.mark(v.tensor_scalar(rn[:, 0, :], flat("kk_sum")[:, 0:NH], 1e-24, None, ALU.max))
                ch.wait(m)
                rsqrt_small(v, ch, rn[:, 0, :], rn[:, 1, :], rn[:, 2, :])
                t.drained(v.tensor_copy(rnb[:], bc(rn[:, 1, :], HD)), "kk_sum")
                v.wait_ge(ta_ready, CREDIT + t.count(1, 1))
                ch.link(v.tensor_scalar(la[:], la[:], 0.5, 0.5, MUL, ADD))
                ch.link(v.tensor_tensor(t1[:], la[:], bc(vec[:, 2, :], TT), MUL))
                ch.link(v.tensor_tensor(t1[:], t1[:], bc(omk[:], TT), ADD))
                ch.link(v.tensor_tensor(km[:], k, t1[:], MUL))
                v.tensor_tensor(sq[:], r, km[:], MUL).then_inc(rk_ready, 1)
                t.wait_filled(v, "kk_scale")
                t.drained(v.tensor_tensor(kk[:], kk[:], heads4("kk_scale"), MUL), "kk_scale")
                t.wait_drained(v, "cum")
                as8 = lambda a: a.rearrange("p a (c t) -> p (a c) t", c=2)
                v.tensor_tensor(RAV[:, :, 0:CH].rearrange("p (a c) t -> p a c t", c=2),
                                r.rearrange("p a (c t) -> p a c t", c=2),
                                W[:, :, 1:].rearrange("p (a c) t -> p a c t", c=2), MUL)
                v.tensor_tensor(BK[:, :, CH:], as8(km[:]), Wi[:], MUL)
                t.wait_drained(v, "kk_scale")
                v.scalar_tensor_tensor(RAV[:, :, CH:2 * CH], as8(kk[:]), -1.0, W[:, :, 0:CH], MUL, MUL)
                ch.link(v.tensor_tensor(la[:], la[:], kk[:], MUL))
                v.tensor_tensor(BK[:, :, 0:CH], as8(la[:]), Wi[:], MUL).then_inc(ops_ready, 1)
                t.wait_filled(v, "bonus")
                t.drained(v.tensor_tensor(bonv[:], heads4("bonus"), vv, MUL), "bonus")
                v.wait_ge(tz_ready, CREDIT + t.count(1, 1))
                v.scalar_tensor_tensor(sz[:], sz[:], 1.0, z, ADD, MUL)
                hook("bonus")
                for c in range(2):
                    t.wait_filled(v, f"avT{c}")
                    t.drained(v.tensor_copy(by_pair(XA[c * CH:(c + 1) * CH, :, 0:HD]),
                                            heads4(f"avT{c}")[0:CH].rearrange("p a (g d) -> p a g d", g=2)), f"avT{c}")
                for n in range(4):
                    c, g = n // 2, n % 2
                    t.wait_filled(v, f"aa{n}")
                    v.tensor_tensor(FB[:, c, :, (1 + g) * HD:(2 + g) * HD], heads4(f"aa{n}")[:, :, 0:CH],
                                    over4(cst("mask_r")), MUL)
                    t.drained(v.tensor_tensor(AkT[CH:, c, 4 * g:4 * g + 4, :], heads4(f"aa{n}")[CH:, :, CH:],
                                              over4(cst("mask_a")[CH:]), MUL), f"aa{n}")
                hook("aa3")
                for g in range(2):
                    hs = slice(4 * g, 4 * g + 4)
                    t.wait_filled(v, f"lt{g}")
                    t.drained(v.tensor_tensor(LT[:, hs, :], heads4(f"lt{g}"), over4(cst("strict")), MUL), f"lt{g}")
                    t.wait_drained(v, f"lt{g}")
                    ch.link(v.tensor_tensor(UT[:, hs, :], LT[:, hs, :], over4(cst("pair0")), MUL))
                    v.tensor_tensor(UT[:, hs, :], UT[:, hs, :], over4(cst("ident")), ADD).then_inc(ut_ready, 1)
                v.wait_ge(ut_ready, CREDIT + t.count(2, 2))
                for b in LEVELS:
                    for g in range(2):
                        t.wait_filled(v, f"q{b}_{g}")
                        t.drained(v.tensor_tensor(Q[:, 4 * g:4 * g + 4, :], heads4(f"q{b}_{g}"), over4(level[b]), MUL),
                                  f"q{b}_{g}")
                    hook(f"d{b}_0")
                    for g in range(2):
                        hs = slice(4 * g, 4 * g + 4)
                        t.wait_filled(v, f"d{b}_{g}")
                        t.drained(v.tensor_tensor(UT[:, hs, :], UT[:, hs, :], heads4(f"d{b}_{g}"), ADD), f"d{b}_{g}")
                    t.wait_drained(v, f"d{b}_0")
                    t.wait_drained(v, f"d{b}_1")
                for g in range(2):
                    t.wait_filled(v, f"x{g}")
                    t.drained(v.tensor_copy(XG[0:CH, 1, 4 * g:4 * g + 4, :], heads4(f"x{g}")[CH:]), f"x{g}")
                for c in range(2):
                    t.wait_filled(v, f"rm{c}")
                    rw = RAV[:].rearrange("p (a c) t -> p a c t", c=2)[:, :, c, 0:CH]
                    one = cst("ident")
                    src = heads4(f"rm{c}")
                    v.tensor_tensor(RM[0:HD, c, :, 0:HD], src[0:HD, :, 0:HD], over4(one[0:HD, 0:HD]), ADD)
                    v.tensor_tensor(RM[0:HD, c, :, HD:], src[0:HD, :, HD:], rw[0:HD], ADD)
                    v.tensor_tensor(RM[HD:, c, :, 0:HD], src[HD:, :, 0:HD], rw[HD:], ADD)
                    t.drained(v.tensor_tensor(RM[HD:, c, :, HD:], src[HD:, :, HD:], over4(one[HD:, HD:]), ADD), f"rm{c}")
                hook("rm1")
                for c in range(2):
                    wc = W[:].rearrange("p (a c) t -> p a c t", c=2)[:, :, c, CH:]
                    for g in range(2):
                        rows = slice(g * HD, (g + 1) * HD)
                        t.wait_filled(v, f"sy{c}_{g}")
                        t.drained(v.tensor_tensor(S[rows], heads8(f"sy{c}_{g}")[rows, 0:NP],
                                                  wc[rows].to_broadcast([HD, NP, HD]), MUL), f"sy{c}_{g}")
                t.wait_drained(v, "sy1_0")
                t.wait_drained(v, "sy1_1")
                y8 = Y[:].rearrange("p a h d -> p (a h) d")
                ch.link(v.tensor_reduce(rn[:, 0, :], y8, AX, ADD))
                v.scalar_tensor_tensor(y8, bc(rn[:, 0, :], HD), -1.0 / HD, y8, MUL, ADD).then_inc(yc_ready, 1)
                v.wait_ge(yq_ready, CREDIT + t.count(1, 1))
                ch.link(v.tensor_reduce(rn[:, 0, :], yg[:].rearrange("p a (h d) -> p (a h) d", h=2), AX, ADD))
                ch.link(v.tensor_scalar(rn[:, 0, :], rn[:, 0, :], 1.0 / HD, GN_EPS, MUL, ADD))
                rsqrt_small(v, ch, rn[:, 0, :], rn[:, 1, :], rn[:, 2, :])
                v.tensor_tensor(y8, y8, bc(rn[:, 1, :], HD), MUL).then_inc(yn_ready, 1)
                t.wait_drained(v, "yT")
                ch.link(v.tensor_tensor(yg[:], yg[:], bonv[:], ADD))
                v.wait_ge(y_stored[j], CREDIT + i * 16)
                v.scalar_tensor_tensor(yo[:, j], yg[:], 0.5, sz[:], MUL, MUL).then_inc(y_ready, 1)
                hook("yT")

            v.memset(S[:], 0.0)
            v.memset(carry[:], 0.0)
            v.memset(W[:], 1.0).then_inc(setup, 1)
            v.wait_ge(c_loaded, 16 * 10)
            ch.link(v.tensor_scalar(mq[:], mu[:], -1.0, 1.0, MUL, ADD))
            ch.link(v.tensor_scalar(omk[:], vec[:, 2, :], -1.0, 1.0, MUL, ADD))
            for p in range(NP):
                last = v.tensor_scalar(rk1[:, p, :], cst("heads"), vec[:, 3, p:p + 1], None, MUL)
            ch.link(last)
            v.tensor_scalar(mq[:], mq[:], unscale, None, MUL).then_inc(setup, 1)
            v.wait_ge(setup, 2)
            for u in range(NU):
                shift_unit(0, u)
            ch.restart()
            with v.Fori(0, NRB - 1) as i:
                for j in range(RJ):
                    tile(i, j, True)
                ch.restart()
            for j in range(RJ):
                tile(NRB - 1, j, False)

        @block.tensor
        def _(pe):
            ident = cst("ident")

            def unit_steps(n, u):
                b = u % 2
                pe.wait_ge(pj_drained[b], CREDIT + pj_count(n, u))
                if u == 0:
                    pe.wait_ge(ht_loaded, n * 16 + 16)
                for k, last in enumerate(project_steps(pe, pj[b][:], whi, wlo, ht, u)):
                    if k == 23:
                        last.then_inc(pj_filled[b], 1)
                    yield

            def tile(i, j, beside):
                t = Tile(i, j, filled, drained)
                steps = (s for u in (units_of(j) if beside else []) for s in unit_steps(i + 1, u))
                issued = [0]

                def end(name, last):
                    t.filled(last, name)
                    while issued[0] < slices_due(j, ORDER[name]) * SLICE and beside:
                        next(steps)
                        issued[0] += 1

                ts = slice(j * TT, (j + 1) * TT)
                pe.wait_ge(lora_ready, CREDIT + i + 1)
                t.before_fill(pe, "lora_w")
                end("lora_w", pe.matmul(flat("lora_w"), lora[0:LORA, ts], lup[0:LORA, :], start=True, stop=True))
                t.before_fill(pe, "lora_a")
                for p in range(NP):
                    last = pe.matmul(heads4("lora_a")[:, p, :], lup[LORA:, p * P:(p + 1) * P], lora[LORA:, ts],
                                     start=True, stop=True)
                end("lora_a", last)
                pe.wait_ge(sq_ready, CREDIT + t.count(1, 1))
                t.before_fill(pe, "kk_sum")
                for p in range(NP):
                    last = pe.matmul(flat("kk_sum")[:, 2 * p:2 * p + 2], sq[:, p, :], cst("sel2"), start=True, stop=True)
                end("kk_sum", last)
                pe.wait_ge(ld_ready, CREDIT + t.count(1, 1))
                t.before_fill(pe, "cum")
                for p in range(NP):
                    last = pe.matmul(heads4("cum")[:, p, :], lw[:, p * P:(p + 1) * P], cst("tri"), start=True, stop=True)
                end("cum", last)
                t.wait_drained(pe, "kk_sum")
                t.before_fill(pe, "kk_scale")
                for p in range(NP):
                    last = pe.matmul(heads4("kk_scale")[:, p, :], rnb[:, 2 * p:2 * p + 2, :].rearrange("p h d -> p (h d)"),
                                     ident, start=True, stop=True)
                end("kk_scale", last)
                pe.wait_ge(rk_ready, CREDIT + t.count(1, 1))
                t.before_fill(pe, "bonus")
                for p in range(NP):
                    last = pe.matmul(heads4("bonus")[:, p, :], rk1[:, p, :], sq[:, p, :], start=True, stop=True)
                end("bonus", last)
                pe.wait_ge(ops_ready, CREDIT + t.count(1, 1))
                for c in range(2):
                    t.before_fill(pe, f"bkT{c}")
                    for p in range(NP):
                        last = pe.transpose(heads4(f"bkT{c}")[:, p, :], BK[:, 2 * p + c, :], ident)
                    end(f"bkT{c}", last)
                pe.wait_ge(v_ready, CREDIT + t.count(1, 1))
                for c in range(2):
                    t.before_fill(pe, f"avT{c}")
                    for p in range(NP):
                        last = pe.transpose(heads4(f"avT{c}")[:, p, :], RAV[:, 2 * p + c, CH:], ident)
                    end(f"avT{c}", last)
                for n in range(4):
                    c, h = n // 2, slice(n % 2 * HD, (n % 2 + 1) * HD)
                    t.before_fill(pe, f"aa{n}")
                    for p in range(NP):
                        last = pe.matmul(heads4(f"aa{n}")[:, p, :], BK[h, 2 * p + c, :], RAV[h, 2 * p + c, 0:2 * CH],
                                         start=True, stop=True)
                    end(f"aa{n}", last)
                for g in range(2):
                    t.before_fill(pe, f"lt{g}")
                    pe.sem_inc(passed, 1)
                    h = slice(g * HD, (g + 1) * HD)
                    for p in range(NP):
                        for c in range(2):
                            last = pe.matmul(heads4(f"lt{g}")[c * CH:(c + 1) * CH, p, :], BK[h, 2 * p + c, 0:CH],
                                             RAV[h, 2 * p:2 * p + 2, CH:2 * CH], start=True, stop=True)
                    end(f"lt{g}", last)

                def turn(name, g):
                    t.before_fill(pe, name)
                    for q in range(4):
                        last = pe.transpose(heads4(name)[:, q, :], UT[:, 4 * g + q, :], ident)
                    end(name, last)

                for g in range(2):
                    pe.wait_ge(ut_ready, CREDIT + t.count(2, g + 1))
                    turn(f"ut{g}", g)
                source = "ut{g}"
                for b in LEVELS:
                    for g in range(2):
                        t.wait_drained(pe, source.format(g=g))
                        t.before_fill(pe, f"q{b}_{g}")
                        for q in range(4):
                            last = pe.matmul(heads4(f"q{b}_{g}")[:, q, :], LT[:, 4 * g + q, :], U[:, 4 * g + q, :],
                                             start=True, stop=True)
                        end(f"q{b}_{g}", last)
                    for g in range(2):
                        t.wait_drained(pe, f"q{b}_{g}")
                        t.before_fill(pe, f"d{b}_{g}")
                        for q in range(4):
                            last = pe.matmul(heads4(f"d{b}_{g}")[:, q, :], Q[:, 4 * g + q, :], UT[:, 4 * g + q, :],
                                             start=True, stop=True)
                        end(f"d{b}_{g}", last)
                    if b != LEVELS[-1]:
                        for g in range(2):
                            t.wait_drained(pe, f"d{b}_{g}")
                            turn(f"t{b}_{g}", g)
                        source = f"t{b}_" + "{g}"
                t.before_fill(pe, "akv")
                pe.sem_inc(passed, 1)
                for c in range(2):
                    for h in range(NH):
                        last = pe.matmul(heads8("akv")[c * CH:(c + 1) * CH, h, :], AkT[CH:, c, h, :],
                                         XG[CH:, c, h, HD:], start=True, stop=True)
                end("akv", last)
                t.wait_drained(pe, "akv")
                for g in range(2):
                    t.wait_drained(pe, f"d{LEVELS[-1]}_{g}")
                    t.before_fill(pe, f"x{g}")
                    for q in range(4):
                        last = pe.matmul(heads4(f"x{g}")[:, q, :], UT[:, 4 * g + q, :], XA[:, 4 * g + q, :],
                                         start=True, stop=True)
                    end(f"x{g}", last)
                t.wait_drained(pe, "x0")
                t.wait_drained(pe, "x1")
                for c in range(2):
                    t.before_fill(pe, f"rm{c}")
                    pe.sem_inc(passed, 1)
                    for h in range(NH):
                        g, p = h // NP, h % NP
                        last = pe.matmul(heads4(f"rm{c}")[g * HD:(g + 1) * HD, p, :], XG[0:CH, c, h, 0:HD],
                                         FB[0:CH, c, p, g * 2 * HD:(g + 1) * 2 * HD], start=True, stop=True)
                    end(f"rm{c}", last)
                for c in range(2):
                    t.wait_drained(pe, f"rm{c}")
                    for g in range(2):
                        if c:
                            t.wait_drained(pe, f"sy0_{g}")
                        t.before_fill(pe, f"sy{c}_{g}")
                        rows = slice(g * HD, (g + 1) * HD)
                        for p in range(NP):
                            out = heads8(f"sy{c}_{g}")[:, p, :]
                            pe.matmul(out, FB[:, c, p, g * 2 * HD:(g + 1) * 2 * HD], XG[:, c, g * NP + p, HD:],
                                      start=True, stop=False)
                            last = pe.matmul(out, RM[rows, c, p, :], S[rows, p, :], start=False, stop=True)
                        end(f"sy{c}_{g}", last)
                pe.wait_ge(yn_ready, CREDIT + t.count(1, 1))
                t.before_fill(pe, "yT")
                for p in range(NP):
                    last = pe.transpose(heads4("yT")[:, p, :], Y[:, p].rearrange("p h d -> p (h d)"), ident)
                end("yT", last)

            pe.wait_ge(setup, 2)
            for u in range(NU):
                for _ in unit_steps(0, u):
                    pass
            with pe.Fori(0, NRB - 1) as i:
                for j in range(RJ):
                    tile(i, j, True)
            for j in range(RJ):
                tile(NRB - 1, j, False)


def out_phase(nc, x, w_out, post_g, y_dram, out):
    with ExitStack() as ctx:
        sb = lambda name, shape, dt=F32: ctx.enter_context(nc.sbuf_tensor(name, shape, dt))
        ps = lambda name, shape, dt=F32: ctx.enter_context(nc.psum_tensor(name, shape, dt))
        sem = lambda name: ctx.enter_context(nc.semaphore(name))
        wst = sb("o_w_stage", [P, D])
        whi = sb("o_w_hi", [P, KB, D], F32R)
        wlo = sb("o_w_lo", [P, KB, D], F32R)
        yt = sb("o_y", [P, 2, KB, TT])
        yhi = sb("o_y_hi", [P, 2, KB, TT], F32R)
        ylo = sb("o_y_lo", [P, 2, KB, TT], F32R)
        xt = sb("o_x", [P, 2, D])
        ot = sb("o_out", [P, 2, D])
        junk = sb("o_junk", [P, D])
        pg = sb("o_post_g", [P, D])
        ss = sb("o_ss", [P, 2])
        eps = sb("o_eps", [P, 1])
        pO = [ps(f"o_acc{b}", [P, D]) for b in range(2)]
        w_loaded, w_hi, w_freed, g_loaded = sem("o_w_loaded"), sem("o_w_hi_ready"), sem("o_w_freed"), sem("o_g_loaded")
        y_loaded, x_loaded = [sem(f"o_y_loaded{b}") for b in range(2)], [sem(f"o_x_loaded{b}") for b in range(2)]
        y_hi, y_lo = sem("o_y_hi_ready"), sem("o_y_lo_ready")
        filled, squared, rooted, drained = sem("o_filled"), sem("o_squared"), sem("o_rooted"), sem("o_drained")
        ready = sem("o_ready")
        stored = [sem(f"o_stored{b}") for b in range(2)]
        vch = sem("o_vchain")
        setup = sem("o_setup")
        block = ctx.enter_context(nc.Block())
        y_v = y_dram.rearrange("(b p) t -> p b t", p=P)

        @block.sync
        def _(sp):
            for credited in (y_hi, y_lo, filled, squared, rooted, drained, ready, *stored):
                sp.sem_inc(credited, CREDIT)
            with nc.allow_non_contiguous_dma("broadcast over partitions"):
                sp.dma_start(pg[:], post_g[0:1, :].to_broadcast([P, D])).then_inc(g_loaded, 16)
            for kb in range(KB):
                if kb:
                    sp.wait_ge(w_freed, kb)
                sp.dma_start(wst[:], w_out[0, kb * P:(kb + 1) * P, :]).then_inc(w_loaded, 16)

            def load(t, u):
                if not (isinstance(t, int) and t == 0):
                    sp.wait_ge(y_lo, CREDIT + t - 1)
                sp.dma_start(yt[:, u], y_v[:, :, bass.ds(t * TT, TT)]).then_inc(y_loaded[u], 16)

            def store(t, u):
                sp.wait_ge(ready, CREDIT + t * 2 + 2)
                sp.dma_start(out[0, bass.ds(t * TT, TT), :], ot[:, u, :]).then_inc(stored[u], 16)

            load(0, 0)
            with sp.Fori(0, NT // 2 - 1) as pair:
                load(pair * 2 + 1, 1)
                store(pair * 2, 0)
                load(pair * 2 + 2, 0)
                store(pair * 2 + 1, 1)
            load(NT - 1, 1)
            store(NT - 2, 0)
            store(NT - 1, 1)
            for u in range(2):
                sp.wait_ge(stored[u], CREDIT + NT // 2 * 16)

        @block.gpsimd
        def _(pool):
            with pool.Fori(0, NT // 2) as pair:
                i = pair * 2
                for u in range(2):
                    pool.wait_ge(ready, CREDIT + i * 2)
                    pool.dma_start(xt[:, u, :], x[0, bass.ts(i + u, TT), :]).then_inc(x_loaded[u], 16)

        @block.scalar
        def _(act):
            for kb in range(KB):
                act.wait_ge(w_loaded, 16 * (kb + 1))
                act.activation(whi[:, kb, :], wst[:], ACT.Copy).then_inc(w_hi, 1)
            act.wait_ge(setup, 1)
            with act.Fori(0, NT // 2) as pair:
                i = pair * 2
                for u in range(2):
                    act.wait_ge(y_loaded[u], i * 8 + 16)
                    act.wait_ge(drained, CREDIT + i)
                    act.activation(yhi[:, u], yt[:, u], ACT.Copy).then_inc(y_hi, 1)
                    act.wait_ge(filled, CREDIT + i + u + 1)
                    act.wait_ge(squared, CREDIT + i + u)
                    act.wait_ge(drained, CREDIT + i + u)
                    act.activation(junk[:], pO[u][:], ACT.Square, accum_out=ss[:, 0:1]).then_inc(squared, 1)
                    act.wait_ge(squared, CREDIT + i + u + 1)
                    act.activation(ss[:, 1:2], ss[:, 0:1], ACT.Sqrt, scale=1.0 / D, bias=eps[:]).then_inc(rooted, 1)

        @block.vector
        def _(v):
            ch = Chain(v, vch)
            v.memset(eps[:], RMS_EPS).then_inc(setup, 1)
            for kb in range(KB):
                v.wait_ge(w_hi, kb + 1)
                v.tensor_tensor(wlo[:, kb, :], wst[:], whi[:, kb, :].bitcast(F32), ALU.subtract).then_inc(w_freed, 1)
            v.wait_ge(g_loaded, 16)
            with v.Fori(0, NT // 2) as pair:
                i = pair * 2
                for u in range(2):
                    v.wait_ge(y_hi, CREDIT + i + u + 1)
                    v.tensor_tensor(ylo[:, u], yt[:, u], yhi[:, u].bitcast(F32), ALU.subtract).then_inc(y_lo, 1)
                    v.wait_ge(rooted, CREDIT + i + u + 1)
                    ch.link(v.reciprocal(ss[:, 1:2], ss[:, 1:2]))
                    v.wait_ge(stored[u], CREDIT + i * 8)
                    for c in range(2):
                        cs = slice(c * 512, (c + 1) * 512)
                        last = v.scalar_tensor_tensor(ot[:, u, cs], pO[u][:, cs], ss[:, 1:2], pg[:, cs], ALU.mult,
                                                      ALU.mult)
                        if c == 0:
                            m = ch.mark(last)
                    last.then_inc(drained, 1)
                    v.wait_ge(x_loaded[u], i * 8 + 16)
                    ch.wait(m)
                    v.wait_ge(drained, CREDIT + i + u + 1)
                    for c in range(2):
                        cs = slice(c * 512, (c + 1) * 512)
                        v.tensor_tensor(ot[:, u, cs], ot[:, u, cs], xt[:, u, cs], ALU.add).then_inc(ready, 1)
                    ch.restart()

        @block.tensor
        def _(pe):
            pe.wait_ge(w_freed, KB)
            with pe.Fori(0, NT // 2) as pair:
                i = pair * 2
                for u in range(2):
                    pe.wait_ge(y_lo, CREDIT + i + u + 1)
                    pe.wait_ge(drained, CREDIT + i)
                    for c in range(2):
                        cs = slice(c * 512, (c + 1) * 512)
                        for kb in range(KB):
                            for n, (y, w) in enumerate(((yhi, whi), (yhi, wlo), (ylo, whi))):
                                last = pe.matmul(pO[u][:, cs], y[:, u, kb, :], w[:, kb, cs], start=kb == 0 and n == 0,
                                                 stop=kb == KB - 1 and n == 2)
                    last.then_inc(filled, 1)


def hybrid_kernel(nc, inp, consts, place, out):
    ht_dram = nc.dram_tensor("hT_blocks", [NRB, P, 2, KB, RB], F16, kind="Internal").ap()
    y_dram = nc.dram_tensor("mixed_T", [D, SEQ], F32, kind="Internal").ap()
    with ExitStack() as ctx:
        sb = lambda name, shape, dt=F32: ctx.enter_context(nc.sbuf_tensor(name, shape, dt))
        ct = sb("constants", [P, consts.shape[1]])
        unscale_t = sb("unscale", [P, 1])

        def cst(name):
            at, n = place[name]
            return ct[:, at:at + n]

        with nc.semaphore("consts_loaded") as loaded, nc.Block() as block:
            @block.sync
            def _(sp):
                sp.dma_start(ct[:], consts).then_inc(loaded, 16)
                sp.wait_ge(loaded, 16)
        with ExitStack() as rw:
            whi_r = rw.enter_context(nc.sbuf_tensor("w_rwkv_hi", [P, KB, NSH], F16))
            wlo_r = rw.enter_context(nc.sbuf_tensor("w_rwkv_lo", [P, KB, NSH], F16))
            with ExitStack() as cv:
                whi_c = cv.enter_context(nc.sbuf_tensor("w_conv_hi", [P, KB, 3 * DC], F16))
                wlo_c = cv.enter_context(nc.sbuf_tensor("w_conv_lo", [P, KB, 3 * DC], F16))
                weights_phase(nc, inp["w_in"], inp["pre_g"], whi_r, wlo_r, whi_c, wlo_c, unscale_t[:])
                conv_phase(nc, cst, inp["x"], inp["dw_w"], inp["dw_b"], inp["ln_g"], inp["ln_b"], whi_c, wlo_c,
                           unscale_t[:], ht_dram, y_dram[DR:, :])
            rwkv_phase(nc, cst, inp, whi_r, wlo_r, unscale_t[:], ht_dram, y_dram[0:DR, :])
        out_phase(nc, inp["x"], inp["w_out"], inp["post_g"], y_dram, out)


_INS = ["x", "pre_g", "post_g", "w_in", "mu_shift", "w0", "w_up", "a0", "a_up", "k_k", "k_a", "r_k", "gn_g", "gn_b",
        "dw_w", "dw_b", "ln_g", "ln_b", "w_out"]


def kernel(**inputs):
    import concourse.bacc as bacc
    from concourse.bass_utils import run_bass_kernel_spmd

    nc = bacc.Bacc("TRN2", target_bir_lowering=False, num_devices=1)
    arrays, aps = {}, {}
    for name in _INS:
        a = np.ascontiguousarray(inputs[name])
        arrays[f"in_{name}"] = a
        aps[name] = nc.dram_tensor(f"in_{name}", a.shape, mybir.dt.from_np(a.dtype), kind="ExternalInput").ap()
    consts, place = shape_constants()
    arrays["in_consts"] = consts
    cap = nc.dram_tensor("in_consts", consts.shape, F32, kind="ExternalInput").ap()
    out = nc.dram_tensor("out_x", [1, SEQ, D], F32, kind="ExternalOutput").ap()
    hybrid_kernel(nc, aps, cap, place, out)
    r = run_bass_kernel_spmd(nc, [arrays], core_ids=[0])
    return r.results[0]["out_x"]
```

```python
import math
from contextlib import ExitStack

import numpy as np

import concourse.bass as bass
from concourse import mybir
from concourse.alu_op_type import AluOpType as ALU

F32 = mybir.dt.float32
F32R = mybir.dt.float32r
F16 = mybir.dt.float16
I32 = mybir.dt.int32
ACT = mybir.ActivationFunctionType
AX = mybir.AxisListType.X
RMAX = bass.bass_isa.ReduceOp.max

P = 128
SEQ, D = 4096, 1024
DR = 512
DC = 512
NP = DR // P
HD = 64
NH = DR // HD
CH = 64
TAPS = 31
HALO = TAPS - 1
LORA = 64
NSH = 4 * DR + 2 * LORA
NU = NSH // P
NIN = NSH + 3 * DC
KB = D // P
TB = 512
NB = SEQ // TB
TT = 128
JT = TB // TT
RB = 256
NRB = SEQ // RB
RJ = RB // TT
NT = SEQ // TT
KAPPA = float(np.exp(-0.5))
H_SCALE = 1024.0
W_TOP = 16384.0
RMS_EPS, GN_EPS, LN_EPS = 1e-6, 64e-5, 1e-5
CREDIT = 1
LEVELS = (2, 4, 8, 16, 32)


def shape_constants():
    s = np.arange(P)[:, None]
    t = np.arange(P)[None, :]
    same = s // CH == t // CH
    tc = np.arange(CH)[None, :]
    parts = {
        "ident": s == t,
        "tri": same & (s <= t),
        "strict": same & (s < t),
        "pair0": (t % 2 == 1) & (s == t - 1),
        "mask_r": s % CH <= tc,
        "mask_a": s % CH < tc,
        "heads": s // HD == t // HD,
        "sel2": s // HD == np.arange(2)[None, :],
        "mean": np.full((P, P), 1.0 / DC),
    }
    for b in LEVELS:
        parts[f"level{b}"] = (s // b % 2 == 1) & (tc // b == s // b // 2)
    place, at = {}, 0
    for name, a in parts.items():
        place[name] = (at, a.shape[1])
        at += a.shape[1]
    return np.concatenate([a.astype(np.float32) for a in parts.values()], axis=1), place


class Chain:

    def __init__(self, eng, sem):
        self.eng, self.sem, self.n = eng, sem, 0

    def mark(self, ins):
        ins.then_inc(self.sem, 1)
        self.n += 1
        return self.n

    def wait(self, n):
        self.eng.wait_ge(self.sem, n)

    def link(self, ins):
        self.wait(self.mark(ins))

    def restart(self):
        if self.n:
            self.wait(self.n)
            self.eng.sem_clear(self.sem)
        self.n = 0


def rsqrt_small(v, chain, x, y, t):
    chain.link(v.tensor_scalar(y.bitcast(I32), x.bitcast(I32), 1, None, ALU.logical_shift_right))
    chain.link(v.tensor_scalar(y.bitcast(I32), y.bitcast(I32), -1.0, float(0x5F3759DF), ALU.mult, ALU.add))
    for _ in range(3):
        chain.link(v.tensor_tensor(t, x, y, ALU.mult))
        chain.link(v.scalar_tensor_tensor(t, t, -0.5, y, ALU.mult, ALU.mult))
        chain.link(v.scalar_tensor_tensor(y, t, 1.5, y, ALU.add, ALU.mult))


def weights_phase(nc, w_in, pre_g, whi_r, wlo_r, whi_c, wlo_c, unscale):
    with ExitStack() as ctx:
        sb = lambda name, shape, dt=F32: ctx.enter_context(nc.sbuf_tensor(name, shape, dt))
        sem = lambda name: ctx.enter_context(nc.semaphore(name))
        wbuf = sb("w_stage", [P, 3, NIN])
        wmax = sb("w_max", [P, KB])
        gcol = sb("pre_g_col", [P, KB])
        m2 = sb("w_m2", [P, 2])
        m2a = sb("w_m2a", [P, 2])
        pw = sb("w_pow", [P, 4])
        gs = sb("pre_g_scaled", [P, KB])
        w_loaded = [sem(f"w_loaded{b}") for b in range(3)]
        g_loaded = sem("g_loaded")
        w_freed = sem("w_freed")
        w_ready = sem("w_scaled")
        hi_done = sem("w_hi_done")
        max_ready = sem("w_max_ready")
        max_all = sem("w_max_all")
        vch = sem("w_vchain")
        block = ctx.enter_context(nc.Block())

        @block.sync
        def _(sp):
            with nc.allow_non_contiguous_dma("64 columns of one number"):
                sp.dma_start(gcol[:], pre_g.rearrange("a (k p) -> p (a k)", p=P)).then_inc(g_loaded, 16)
            for n in range(2 * KB):
                if n >= 3:
                    sp.wait_ge(w_freed, n - 2)
                kb = n % KB
                sp.dma_start(wbuf[:, n % 3, :], w_in[0, kb * P:(kb + 1) * P, :]).then_inc(w_loaded[n % 3], 16)

        @block.gpsimd
        def _(pool):
            pool.wait_ge(max_ready, 1)
            nc.gpsimd.partition_all_reduce(m2a[:], m2[:], P, RMAX).then_inc(max_all, 1)

        @block.vector
        def _(v):
            ch = Chain(v, vch)
            for n in range(KB):
                v.wait_ge(w_loaded[n % 3], 16 * (n // 3 + 1))
                v.tensor_reduce(wmax[:, n:n + 1], wbuf[:, n % 3, :], AX, ALU.max,
                                apply_absolute_value=True).then_inc(w_freed, 1)
            v.wait_ge(w_freed, KB)
            ch.link(v.tensor_reduce(m2[:, 0:1], wmax[:], AX, ALU.max))
            v.wait_ge(g_loaded, 16)
            v.tensor_reduce(m2[:, 1:2], gcol[:], AX, ALU.max, apply_absolute_value=True).then_inc(max_ready, 1)
            v.wait_ge(max_all, 1)
            ch.link(v.tensor_scalar(pw[:, 0:1], m2a[:, 0:1], m2a[:, 1:2], 1e-30, ALU.mult, ALU.max))
            ch.link(v.tensor_scalar(pw[:, 1:2].bitcast(I32), pw[:, 0:1].bitcast(I32), 0x7F800000, None,
                                    ALU.bitwise_and))
            ch.link(v.reciprocal(pw[:, 2:3], pw[:, 1:2]))
            ch.link(v.tensor_scalar(pw[:, 3:4], pw[:, 2:3], W_TOP, None, ALU.mult))
            ch.link(v.tensor_scalar(gs[:], gcol[:], pw[:, 3:4], None, ALU.mult))
            ch.link(v.tensor_scalar(unscale, pw[:, 1:2], 1.0 / (W_TOP * H_SCALE), None, ALU.mult))
            for kb in range(KB):
                n = KB + kb
                v.wait_ge(w_loaded[n % 3], 16 * (n // 3 + 1))
                v.tensor_scalar(wbuf[:, n % 3, :], wbuf[:, n % 3, :], gs[:, kb:kb + 1], None,
                                ALU.mult).then_inc(w_ready, 1)
                v.wait_ge(hi_done, 2 * kb + 2)
                v.tensor_tensor(wlo_r[:, kb, :], wbuf[:, n % 3, 0:NSH], whi_r[:, kb, :], ALU.subtract)
                v.tensor_tensor(wlo_c[:, kb, :], wbuf[:, n % 3, NSH:NIN], whi_c[:, kb, :],
                                ALU.subtract).then_inc(w_freed, 1)

        @block.scalar
        def _(act):
            for kb in range(KB):
                n = KB + kb
                act.wait_ge(w_ready, kb + 1)
                act.activation(whi_r[:, kb, :], wbuf[:, n % 3, 0:NSH], ACT.Copy).then_inc(hi_done, 1)
                act.activation(whi_c[:, kb, :], wbuf[:, n % 3, NSH:NIN], ACT.Copy).then_inc(hi_done, 1)


def conv_phase(nc, cst, x, dw_w, dw_b, ln_g, ln_b, whi, wlo, unscale, ht_dram, y_dram):
    with ExitStack() as ctx:
        sb = lambda name, shape, dt=F32: ctx.enter_context(nc.sbuf_tensor(name, shape, dt))
        ps = lambda name, shape, dt=F32: ctx.enter_context(nc.psum_tensor(name, shape, dt))
        sem = lambda name: ctx.enter_context(nc.semaphore(name))
        xt = sb("c_x", [P, JT, D])
        hh = sb("c_h_hi", [P, D], F16)
        hl = sb("c_h_lo", [P, D], F16)
        ht = sb("c_hT", [P, 2, KB, TB], F16)
        ident16 = sb("c_ident16", [P, P], F16)
        ss = sb("c_ss", [P, JT])
        rs = sb("c_rs", [P, JT])
        rt = sb("c_rt", [P, JT])
        G = sb("c_glu", [P, NP, HALO + TB])
        acc = sb("c_acc", [P, 2, NP, TB])
        odd = sb("c_acc_odd", [P, TB])
        sz = sb("c_silu_z", [P, 2, NP, TB])
        sq = sb("c_sq", [P, 2, TB])
        tn = sb("c_tanh_n", [P, 2, TB])
        wcv = sb("c_w", [P, NP, TAPS])
        cols = sb("c_cols", [P, 3, NP])
        half = sb("c_half", [P, 3])
        tp = [ps(f"c_tp{b}", [P, KB, P], F16) for b in range(2)]
        pj = [ps(f"c_pj{b}", [P, TB]) for b in range(3)]
        pmean, pvar = ps("c_mean", [P, TB]), ps("c_var", [P, TB])
        c_loaded = sem("c_const_loaded")
        x_loaded = sem("c_x_loaded")
        ss_ready = sem("c_ss_ready")
        rs_ready = sem("c_rs_ready")
        hi_ready = sem("c_hi_ready")
        lo_ready = sem("c_lo_ready")
        tp_filled, tp_drained = sem("c_tp_filled"), sem("c_tp_drained")
        ht_stored = sem("c_hT_stored")
        pj_filled = sem("c_pj_filled")
        gate_ready = sem("c_gate_ready")
        glu_ready = sem("c_glu_ready")
        tz_ready = sem("c_tz_ready")
        sz_ready = sem("c_sz_ready")
        acc_ready = sem("c_acc_ready")
        halo_kept = sem("c_halo_kept")
        mean_filled = sem("c_mean_filled")
        cen_ready = sem("c_centred")
        sq_ready = sem("c_sq_ready")
        sq_used = sem("c_sq_used")
        std_ready = sem("c_std_ready")
        n_ready = sem("c_norm_ready")
        aff_ready = sem("c_affine_ready")
        tn_ready = sem("c_tanh_n_ready")
        y_ready, y_stored = sem("c_y_ready"), sem("c_y_stored")
        vch = sem("c_vchain")
        ech = sem("c_echain")
        setup = sem("c_setup")
        block = ctx.enter_context(nc.Block())
        x_v = x[0].rearrange("(n j p) d -> n p j d", p=P, j=JT)

        def run(engine, step, first, last):
            first()
            step(0, 0, False, True)
            with engine.Fori(0, (NB - 2) // 2) as k:
                step(k * 2 + 1, 1, True, True)
                step(k * 2 + 2, 0, True, True)
            step(NB - 1, 1, True, False)
            last(NB, 0)

        @block.sync
        def _(sp):
            for credited in (ss_ready, rs_ready, hi_ready, lo_ready, tp_filled, tp_drained, ht_stored, pj_filled,
                             gate_ready, glu_ready, tz_ready, sz_ready, acc_ready, halo_kept, mean_filled, cen_ready,
                             sq_ready, sq_used, std_ready, n_ready, aff_ready, tn_ready, y_ready, y_stored):
                sp.sem_inc(credited, CREDIT)
            with nc.allow_non_contiguous_dma("small constants"):
                for b in range(NP):
                    sp.dma_start(wcv[:, b, :], dw_w[0, :, b * P:(b + 1) * P].rearrange("t p -> p t")).then_inc(c_loaded, 16)
                for k, c in enumerate((dw_b, ln_g, ln_b)):
                    sp.dma_start(cols[:, k, :], c.rearrange("a (b p) -> p (a b)", p=P)).then_inc(c_loaded, 16)

            def first():
                sp.dma_start(xt[:], x_v[0]).then_inc(x_loaded, 16)

            def store_y(i, buf):
                sp.wait_ge(y_ready, CREDIT + i * NP)
                sp.dma_start(y_dram[:, bass.ds((i - 1) * TB, TB)].rearrange("(b p) t -> p b t", p=P),
                             acc[:, 1 - buf]).then_inc(y_stored, 16)

            def step(i, buf, has_last, has_next):
                sp.wait_ge(tp_drained, CREDIT + i * 8 + 8)
                for b in range(TB // RB):
                    sp.dma_start(ht_dram[i * (TB // RB) + b], ht[:, :, :, b * RB:(b + 1) * RB]).then_inc(ht_stored, 16)
                if has_next:
                    sp.wait_ge(lo_ready, CREDIT + i * JT + JT)
                    sp.wait_ge(hi_ready, CREDIT + i * JT + JT)
                    sp.dma_start(xt[:], x_v[i + 1]).then_inc(x_loaded, 16)
                if has_last:
                    store_y(i, buf)

            run(sp, step, first, store_y)
            sp.wait_ge(y_stored, CREDIT + NB * 16)
            sp.wait_ge(ht_stored, CREDIT + NB * 32)

        @block.scalar
        def _(act):
            ch = Chain(act, ech)
            act.wait_ge(setup, 2)

            def squares(i):
                act.wait_ge(x_loaded, i * 16 + 16)
                act.wait_ge(tp_filled, CREDIT + i * 8)
                for j in range(JT):
                    last = act.activation(hh[:], xt[:, j, :], ACT.Square, accum_out=ss[:, j:j + 1])
                    if j < JT - 1:
                        ch.link(last)
                last.then_inc(ss_ready, 1)
                ch.restart()
                act.wait_ge(ss_ready, CREDIT + i + 1)

            def parts(i):
                act.wait_ge(rs_ready, CREDIT + i + 1)
                for j in range(JT):
                    act.wait_ge(tp_filled, CREDIT + i * 8 + 2 * j)
                    if j:
                        act.wait_ge(lo_ready, CREDIT + i * JT + j)
                    act.activation(hh[:], xt[:, j, :], ACT.Copy, scale=rs[:, j:j + 1]).then_inc(hi_ready, 1)
                    if j == 0:
                        act.wait_ge(ht_stored, CREDIT + i * 32)
                        act.wait_ge(pj_filled, CREDIT + i * 12)
                    for part in range(2):
                        act.wait_ge(tp_filled, CREDIT + i * 8 + 2 * j + part + 1)
                        act.activation(ht[:, part, :, j * P:(j + 1) * P], tp[part][:], ACT.Copy).then_inc(tp_drained, 1)

            def first():
                squares(0)
                parts(0)

            def variance(i, buf):
                for q in range(NP):
                    act.wait_ge(cen_ready, CREDIT + (i - 1) * NP + q + 1)
                    act.wait_ge(sq_used, CREDIT + ((i - 1) * NP + q - 1 if q else (i - 1) * NP))
                    act.activation(sq[:, q % 2, :], acc[:, 1 - buf, q, :], ACT.Square).then_inc(sq_ready, 1)
                act.wait_ge(sq_used, CREDIT + i * NP)
                act.activation(pvar[:], pvar[:], ACT.Sqrt, bias=half[:, 2:3]).then_inc(std_ready, 1)

            def affine(i, buf):
                for q in range(NP):
                    a = acc[:, 1 - buf, q, :]
                    act.wait_ge(n_ready, CREDIT + (i - 1) * NP + q + 1)
                    act.activation(a, a, ACT.Identity, scale=cols[:, 1, q:q + 1], bias=cols[:, 2, q:q + 1]).then_inc(aff_ready, 1)
                for q in range(NP):
                    act.wait_ge(aff_ready, CREDIT + (i - 1) * NP + q + 1)
                    act.wait_ge(y_ready, CREDIT + ((i - 1) * NP + q - 1 if q else (i - 1) * NP))
                    act.activation(tn[:, q % 2, :], acc[:, 1 - buf, q, :], ACT.Tanh, scale=0.5).then_inc(tn_ready, 1)

            def step(i, buf, has_last, has_next):
                for b in range(NP):
                    act.wait_ge(pj_filled, CREDIT + i * 12 + 3 * b + 1)
                    act.wait_ge(halo_kept, CREDIT + i * NP + b)
                    act.activation(G[:, b, HALO:], pj[0][:], ACT.Tanh, scale=half[:, 0:1]).then_inc(gate_ready, 1)
                    act.wait_ge(pj_filled, CREDIT + i * 12 + 3 * b + 3)
                    act.activation(sz[:, buf, b, :], pj[2][:], ACT.Tanh, scale=half[:, 0:1]).then_inc(tz_ready, 1)
                    if b == 0 and has_last:
                        variance(i, buf)
                    if b == 2 and has_last:
                        affine(i, buf)
                    if b == 2 and has_next:
                        squares(i + 1)
                if has_next:
                    parts(i + 1)

            def last(i, buf):
                variance(i, buf)
                affine(i, buf)

            run(act, step, first, last)

        @block.vector
        def _(v):
            ch = Chain(v, vch)
            ch.link(v.tensor_copy(ident16[:], cst("ident")))
            v.wait_ge(c_loaded, 16 * (NP + 3))
            ch.link(v.tensor_scalar(half[:, 0:1], unscale, 0.5, None, ALU.mult))
            ch.link(v.tensor_scalar(half[:, 1:2], unscale, 0.25, None, ALU.mult))
            ch.link(v.memset(half[:, 2:3], LN_EPS))
            v.tensor_scalar(wcv[:], wcv[:], half[:, 0:1], None, ALU.mult).then_inc(setup, 1)
            v.memset(G[:], 0.0).then_inc(setup, 1)
            v.wait_ge(setup, 2)
            ch.restart()

            def scales(i):
                v.wait_ge(ss_ready, CREDIT + i + 1)
                v.wait_ge(hi_ready, CREDIT + i * JT)
                ch.link(v.tensor_scalar(rt[:], ss[:], 1.0 / D, RMS_EPS, ALU.mult, ALU.add))
                rsqrt_small(v, ch, rt[:], rs[:], ss[:])
                v.tensor_scalar(rs[:], rs[:], H_SCALE, None, ALU.mult).then_inc(rs_ready, 1)

            def low(i, j):
                v.wait_ge(hi_ready, CREDIT + i * JT + j + 1)
                v.wait_ge(tp_filled, CREDIT + i * 8 + 2 * j)
                v.scalar_tensor_tensor(hl[:], xt[:, j, :], rs[:, j:j + 1], hh[:], ALU.mult,
                                       ALU.subtract).then_inc(lo_ready, 1)

            def first():
                scales(0)
                for j in range(JT):
                    low(0, j)
                ch.restart()

            def centre(i, buf):
                v.wait_ge(mean_filled, CREDIT + i)
                for q in range(NP):
                    a = acc[:, 1 - buf, q, :]
                    v.tensor_tensor(a, a, pmean[:], ALU.subtract).then_inc(cen_ready, 1)

            def normalise(i, buf):
                v.wait_ge(std_ready, CREDIT + i)
                ch.link(v.reciprocal(pvar[:], pvar[:]))
                for q in range(NP):
                    a = acc[:, 1 - buf, q, :]
                    v.wait_ge(sq_ready, CREDIT + (i - 1) * NP + q + 1)
                    v.tensor_tensor(a, a, pvar[:], ALU.mult).then_inc(n_ready, 1)

            def gated(i, buf):
                for q in range(NP):
                    v.wait_ge(tn_ready, CREDIT + (i - 1) * NP + q + 1)
                    tq, a = tn[:, q % 2, :], acc[:, 1 - buf, q, :]
                    ch.link(v.scalar_tensor_tensor(tq, tq, 1.0, a, ALU.add, ALU.mult))
                    v.scalar_tensor_tensor(a, tq, half[:, 1:2], sz[:, 1 - buf, q, :], ALU.mult, ALU.mult).then_inc(y_ready, 1)

            def step(i, buf, has_last, has_next):
                for b in range(NP):
                    g = G[:, b, HALO:]
                    v.wait_ge(pj_filled, CREDIT + i * 12 + 3 * b + 2)
                    v.wait_ge(gate_ready, CREDIT + i * NP + b + 1)
                    v.scalar_tensor_tensor(g, g, 1.0, pj[1][:], ALU.add, ALU.mult).then_inc(glu_ready, 1)
                    v.wait_ge(tz_ready, CREDIT + i * NP + b + 1)
                    z = sz[:, buf, b, :]
                    v.scalar_tensor_tensor(z, z, 1.0, pj[2][:], ALU.add, ALU.mult).then_inc(sz_ready, 1)
                    if b == 0 and has_last:
                        v.wait_ge(y_stored, CREDIT + (i - 1) * 16)
                    if b == NP - 1 and has_next:
                        scales(i + 1)
                    v.wait_ge(glu_ready, CREDIT + i * NP + b + 1)
                    a = acc[:, buf, b, :]
                    marks = [ch.mark(v.tensor_scalar(a, G[:, b, 0:TB], wcv[:, b, 0:1], cols[:, 0, b:b + 1],
                                                     ALU.mult, ALU.add)),
                             ch.mark(v.tensor_scalar(odd[:], G[:, b, 1:1 + TB], wcv[:, b, 1:2], None, ALU.mult))]
                    for t in range(2, TAPS):
                        o = a if t % 2 == 0 else odd[:]
                        ch.wait(marks[t % 2])
                        marks[t % 2] = ch.mark(v.scalar_tensor_tensor(o, G[:, b, t:t + TB], wcv[:, b, t:t + 1], o,
                                                                      ALU.mult, ALU.add))
                        if b == NP - 1 and has_next and t % 4 == 1 and t // 4 - 1 < JT and t >= 5:
                            low(i + 1, t // 4 - 1)
                    ch.wait(max(marks))
                    v.tensor_tensor(a, a, odd[:], ALU.add).then_inc(acc_ready, 1)
                    v.wait_ge(acc_ready, CREDIT + i * NP + b + 1)
                    v.tensor_copy(G[:, b, 0:HALO], G[:, b, TB:TB + HALO]).then_inc(halo_kept, 1)
                    ch.restart()
                    if has_last:
                        (centre, normalise, gated, lambda *_: None)[b](i, buf)
                ch.restart()

            def last(i, buf):
                centre(i, buf)
                normalise(i, buf)
                gated(i, buf)

            run(v, step, first, last)

        @block.tensor
        def _(pe):
            pe.wait_ge(setup, 2)

            def transposes(i):
                for j in range(JT):
                    for part, (ready, src) in enumerate(((hi_ready, hh), (lo_ready, hl))):
                        pe.wait_ge(ready, CREDIT + i * JT + j + 1)
                        pe.wait_ge(tp_drained, CREDIT + (i * 8 + 2 * j + part - 1 if j else i * 8))
                        for kb in range(KB):
                            last = pe.transpose(tp[part][:, kb, :], src[:, kb * P:(kb + 1) * P], ident16[:])
                        last.then_inc(tp_filled, 1)

            def mean(i, buf):
                pe.wait_ge(acc_ready, CREDIT + i * NP)
                for q in range(NP):
                    last = pe.matmul(pmean[:], cst("mean"), acc[:, 1 - buf, q, :], start=q == 0, stop=q == NP - 1)
                last.then_inc(mean_filled, 1)

            def variance(i):
                for q in range(NP):
                    pe.wait_ge(sq_ready, CREDIT + (i - 1) * NP + q + 1)
                    pe.matmul(pvar[:], cst("mean"), sq[:, q % 2, :], start=q == 0, stop=q == NP - 1).then_inc(sq_used, 1)

            def step(i, buf, has_last, has_next):
                pe.wait_ge(tp_drained, CREDIT + i * 8 + 8)
                for b in range(NP):
                    for n, unit in enumerate((NP + b, b, 2 * NP + b)):
                        pe.wait_ge(sz_ready if n == 2 else glu_ready, CREDIT + i * NP + b)
                        project(pe, pj[n][:], whi, wlo, (ht[:, 0], ht[:, 1]), unit).then_inc(pj_filled, 1)
                    if b == 0 and has_last:
                        mean(i, buf)
                    if b == 1 and has_last:
                        variance(i)
                if has_next:
                    transposes(i + 1)

            def last(i, buf):
                mean(i, buf)
                variance(i)

            run(pe, step, lambda: transposes(0), last)


def project_steps(pe, out, whi, wlo, ht, unit):
    cols = slice(unit * P, (unit + 1) * P)
    for kb in range(KB):
        for n, (w, part) in enumerate(((whi, 0), (whi, 1), (wlo, 0))):
            yield pe.matmul(out, w[:, kb, cols], ht[part][:, kb, :], start=kb == 0 and n == 0,
                            stop=kb == KB - 1 and n == 2)


def project(pe, out, whi, wlo, ht, unit):
    for last in project_steps(pe, out, whi, wlo, ht, unit):
        pass
    return last


def tile_uses():
    uses = [("lora_w", 1), ("lora_a", 1), ("kk_sum", 1), ("cum", 1), ("kk_scale", 1), ("bonus", 1),
            ("bkT0", 1), ("bkT1", 1), ("avT0", 2), ("avT1", 2), ("aa0", 1), ("aa1", 1), ("aa2", 1), ("aa3", 1),
            ("lt0", 1), ("lt1", 1), ("ut0", 1), ("ut1", 1)]
    for b in LEVELS:
        uses += [(f"q{b}_{g}", 2) for g in range(2)] + [(f"d{b}_{g}", 1) for g in range(2)]
        if b != LEVELS[-1]:
            uses += [(f"t{b}_{g}", 1) for g in range(2)]
    uses += [("akv", 1), ("x0", 2), ("x1", 2), ("rm0", 1), ("rm1", 1), ("sy0_0", 2), ("sy0_1", 2), ("sy1_0", 2), ("sy1_1", 2),
             ("yT", 1)]
    return uses


USES = tile_uses()
ORDER = {name: n for n, (name, _) in enumerate(USES)}
RING = 6
PER_BANK = [len(USES[b::RING]) for b in range(RING)]
DRAINS = [sum(d for n, (_, d) in enumerate(USES) if n % RING == b) for b in range(RING)]
GROUP_NORM = ("norm0", "norm1", "norm2")


def fill_plan():
    shares = {"lora_w": 0, "lora_a": 0, "kk_sum": 12, "cum": 16, "kk_scale": 12, "bonus": 26, "bkT": 4, "avT": 5, "aa": 4,
              "lt": 5, "ut": 5, "q": 1.5, "d": 1.5, "t": 1.5, "akv": 3, "x": 7, "rm": 4, "sy": 4, "norm": 16, "yT": 0}
    points = [name for name, _ in USES[:-1]] + list(GROUP_NORM) + [USES[-1][0]]
    kind = lambda name: name if name in shares else name.rstrip("0123456789_")
    return [(name, shares[kind(name)]) for name in points]


FILL = fill_plan()
LORA_AT = (NU - 1) // RJ


def unit_at(o):
    return o if o < LORA_AT else NU - 1 if o == LORA_AT else o - 1


def units_of(j):
    return list(range(0, LORA_AT) if j == 0 else range(LORA_AT, NU))


def steps_due(j, name):
    total, share, by_then = len(units_of(j)) * 24, sum(w for _, w in FILL), 0
    for point, w in FILL:
        by_then += w
        if point == name:
            return math.ceil(total * by_then / share - 1e-9)


class Tile:

    def __init__(self, i, j, filled, drained):
        self.i, self.j, self.filled_sems, self.drained_sems = i, j, filled, drained

    def count(self, per_tile, k):
        return self.i * (RJ * per_tile) + (self.j * per_tile + k)

    def before_fill(self, eng, name):
        n = ORDER[name]
        b = n % RING
        eng.wait_ge(self.drained_sems[b], CREDIT + self.count(DRAINS[b], sum(d for _, d in USES[b:n:RING])))

    def filled(self, ins, name):
        ins.then_inc(self.filled_sems[ORDER[name] % RING], 1)

    def wait_filled(self, eng, name):
        n = ORDER[name]
        eng.wait_ge(self.filled_sems[n % RING], CREDIT + self.count(PER_BANK[n % RING], n // RING + 1))

    def drained(self, ins, name):
        ins.then_inc(self.drained_sems[ORDER[name] % RING], 1)

    def wait_drained(self, eng, name):
        n = ORDER[name]
        b = n % RING
        eng.wait_ge(self.drained_sems[b], CREDIT + self.count(DRAINS[b], sum(d for _, d in USES[b:n + 1:RING])))


def rwkv_phase(nc, cst, inp, whi, wlo, unscale, ht_dram, y_dram):
    with ExitStack() as ctx:
        sb = lambda name, shape, dt=F32: ctx.enter_context(nc.sbuf_tensor(name, shape, dt))
        ps = lambda name, shape, dt=F32: ctx.enter_context(nc.psum_tensor(name, shape, dt))
        sem = lambda name: ctx.enter_context(nc.semaphore(name))
        ht = sb("r_hT", [P, 4, KB, RB], F16)
        raw = sb("r_raw", [P, 2, RB + 1])
        keep = sb("r_keep", [P, 2, RB])
        carry = sb("r_carry", [P, NU])
        mix = sb("r_mix", [P, NU - 1, 2 * RB])
        lora = sb("r_lora", [P, RB])
        rn = sb("r_rn", [P, 3, NH])
        rnb = sb("r_rnb", [P, NH, HD])
        W = sb("r_W", [P, NP * 2, CH + 1])
        Wi = sb("r_Winv", [P, NP * 2, CH])
        bonv = sb("r_bonus", [P, NP, TT])
        BK = sb("r_BK", [P, NP * 2, 2 * CH])
        RAV = sb("r_RAV", [P, NP * 2, 3 * CH])
        FB = sb("r_FB", [P, 2, NP, 4 * HD])
        AkT = sb("r_AkT", [P, 2, NH, CH])
        XA = sb("r_XA", [P, NH, 2 * HD])
        XG = sb("r_XG", [P, 2, NH, 2 * HD])
        LT = sb("r_LT", [P, NH, TT])
        U = sb("r_U", [P, NH, TT])
        UT = sb("r_UT", [P, NH, TT])
        Q = sb("r_Q", [P, NH, TT])
        la, kk = UT[:, 0:NP, :], UT[:, NP:, :]
        km, sq = U[:, 0:NP, :], U[:, NP:, :]
        t1 = yg = Q[:, 0:NP, :]
        lw = Q[:, NP:, :].rearrange("p a t -> p (a t)")
        RM = sb("r_RM", [P, 2, NP, 2 * HD])
        S = sb("r_S", [P, NP, HD])
        Y = sb("r_Y", [P, NP, 2, HD])
        sz = sb("r_sz", [P, NP, TT])
        yo = sb("r_yo", [P, 2, NP, TT])
        w0b = sb("r_w0", [P, DR])
        lup = sb("r_lora_up", [P, DR])
        rk1 = sb("r_rk_ones", [P, NP, P])
        vec = sb("r_vec", [P, 6, NP])
        omk = sb("r_1_k_a", [P, NP])
        zero = sb("r_zero", [P, 1])
        mu = sb("r_mu", [P, NU])
        mq = sb("r_1_mu", [P, NU])
        pj = [ps(f"r_pj{b}", [P, RB]) for b in range(2)]
        bank = [ps(f"r_bank{b}", [P, 512]) for b in range(RING)]
        filled = [sem(f"r_filled{b}") for b in range(RING)]
        drained = [sem(f"r_drained{b}") for b in range(RING)]
        c_loaded, ht_loaded = sem("r_const_loaded"), sem("r_hT_loaded")
        pj_filled = [sem(f"r_pj_filled{b}") for b in range(2)]
        pj_drained = [sem(f"r_pj_drained{b}") for b in range(2)]
        shifted = sem("r_shifted")
        lora_ready = sem("r_lora_ready")
        tw_ready, ta_ready = sem("r_tanh_w"), sem("r_tanh_a")
        sq_ready = sem("r_sq_ready")
        ld_ready, rk_ready = sem("r_decay_ready"), sem("r_rk_ready")
        ops_ready, v_ready = sem("r_ops_ready"), sem("r_v_ready")
        ut_ready = sem("r_ut_ready")
        yc_ready, yq_ready, yn_ready = sem("r_y_centred"), sem("r_y_squared"), sem("r_y_normed")
        tz_ready = sem("r_tanh_z")
        y_ready = sem("r_y_ready")
        y_stored = [sem(f"r_y_stored{b}") for b in range(2)]
        vch, ech, setup = sem("r_vchain"), sem("r_echain"), sem("r_setup")
        passed = sem("r_passed")
        block = ctx.enter_context(nc.Block())
        y_v = y_dram.rearrange("(b p) t -> p b t", p=P)

        def pj_count(n, o):
            b = o % 2
            return n * ((NU + 1 - b) // 2) + o // 2

        def heads4(name):
            return bank[ORDER[name] % RING][:].rearrange("p (h t) -> p h t", h=4)

        def heads8(name):
            return bank[ORDER[name] % RING][:].rearrange("p (h t) -> p h t", h=8)

        def flat(name):
            return bank[ORDER[name] % RING][:]

        def chunks(name):
            return bank[ORDER[name] % RING][:].rearrange("p (c t) -> p c t", t=CH)

        def halves(name, b):
            return bank[ORDER[name] % RING][:].rearrange("p (x h n t) -> p x h n t", x=2, h=4, t=b)

        def block_cols(a, g, b, odd):
            return a[:, 4 * g:4 * g + 4, :].rearrange("p h (n two t) -> p h two n t", two=2, t=b)[:, :, odd]

        def bc(col, n):
            return col.unsqueeze(2).to_broadcast([P, col.shape[1], n])

        def by_pair(a):
            return a.rearrange("p (g a) d -> p a g d", g=2)

        def part(group, i, j):
            return mix[:, group * NP:(group + 1) * NP, bass.ds((i % 2) * RB + j * TT, TT)]

        @block.sync
        def _(sp):
            for credited in (*filled, *drained, *pj_filled, *pj_drained, *y_stored, shifted, lora_ready, tw_ready,
                             ta_ready, sq_ready, ld_ready, rk_ready, ops_ready, v_ready, ut_ready,
                             yc_ready, yq_ready, yn_ready, tz_ready, y_ready):
                sp.sem_inc(credited, CREDIT)
            with nc.allow_non_contiguous_dma("small constants"):
                for k, name in enumerate(("a0", "k_k", "k_a", "r_k", "gn_g", "gn_b")):
                    src = inp[name].rearrange("a h d -> a (h d)") if name == "r_k" else inp[name]
                    sp.dma_start(vec[:, k, :], src.rearrange("a (b p) -> p (a b)", p=P)).then_inc(c_loaded, 16)
                sp.dma_start(mu[:], inp["mu_shift"].rearrange("a (b p) -> p (a b)", p=P)).then_inc(c_loaded, 16)
                sp.dma_start(w0b[:], inp["w0"][0:1, :].to_broadcast([P, DR])).then_inc(c_loaded, 16)
            sp.dma_start(lup[0:LORA, :], inp["w_up"][0]).then_inc(c_loaded, 16)
            sp.dma_start(lup[LORA:P, :], inp["a_up"][0]).then_inc(c_loaded, 16)
            for n in range(2):
                sp.dma_start(ht[:, 2 * n:2 * n + 2], ht_dram[n]).then_inc(ht_loaded, 16)
                sp.wait_ge(ht_loaded, 16 * (n + 1))

            def stores(i):
                for j in range(RJ):
                    sp.wait_ge(y_ready, CREDIT + i * RJ + j + 1)
                    sp.dma_start(y_v[:, 0:NP, bass.ds(i * RB + j * TT, TT)], yo[:, j]).then_inc(y_stored[j], 16)

            with sp.Fori(0, NRB - 2) as i:
                sp.wait_ge(pj_filled[0], CREDIT + pj_count(i, NU - 1) + 1)
                sp.wait_ge(ht_loaded, i * 16 + 32)
                sp.dma_start(ht[:, bass.ds((i % 2) * 2, 2)], ht_dram[i + 2]).then_inc(ht_loaded, 16)
                stores(i)
            for n in (NRB - 2, NRB - 1):
                stores(n)
            for j in range(RJ):
                sp.wait_ge(y_stored[j], CREDIT + NRB * 16)

        @block.scalar
        def _(act):
            ch = Chain(act, ech)

            def drain_unit(n, o):
                b, u = o % 2, unit_at(o)
                act.wait_ge(shifted, CREDIT + (n * NU + o - 1 if o else n * NU))
                act.activation(raw[:, b, 0:1], carry[:, u:u + 1], ACT.Copy)
                act.wait_ge(pj_filled[b], CREDIT + pj_count(n, o) + 1)
                act.activation(raw[:, b, 1:], pj[b][:], ACT.Copy, scale=unscale)
                act.activation(keep[:, b, :], pj[b][:], ACT.Copy, scale=mq[:, u:u + 1]).then_inc(pj_drained[b], 1)

            def lora_tanh(n):
                act.wait_ge(shifted, CREDIT + n * NU + LORA_AT + 1)
                act.activation(lora[0:LORA, :], lora[0:LORA, :], ACT.Tanh).then_inc(lora_ready, 1)

            def tile(i, j, beside):
                t = Tile(i, j, filled, drained)
                todo = units_of(j) if beside else []
                taken = [0]

                def hook(name):
                    while taken[0] < len(todo) and steps_due(j, name) >= 24 * (taken[0] + 1):
                        o = todo[taken[0]]
                        drain_unit(i + 1, o)
                        if o == LORA_AT + 1:
                            lora_tanh(i + 1)
                        taken[0] += 1

                act.wait_ge(shifted, CREDIT + i * NU + NU)
                for p in range(NP):
                    last = act.activation(sq[:, p, :], part(1, i, j)[:, p, :], ACT.Square, scale=vec[:, 1, p:p + 1])
                last.then_inc(sq_ready, 1)
                t.wait_drained(act, "lora_w")
                act.activation(lw[:], lw[:], ACT.Tanh, scale=0.5).then_inc(tw_ready, 1)
                t.wait_filled(act, "lora_a")
                for p in range(NP):
                    last = act.activation(la[:, p, :], heads4("lora_a")[:, p, :], ACT.Tanh, scale=0.5,
                                          bias=vec[:, 0, p:p + 1])
                    if p == 0:
                        act.wait_ge(tw_ready, CREDIT + t.count(1, 1))
                        act.activation(lw[:], lw[:], ACT.Copy, scale=-KAPPA / 2, bias=-KAPPA / 2).then_inc(ld_ready, 1)
                t.drained(last, "lora_a")
                t.wait_drained(act, "lora_a")
                for p in range(NP):
                    last = act.activation(t1[:, p, :], la[:, p, :], ACT.Identity, scale=vec[:, 2, p:p + 1],
                                          bias=omk[:, p:p + 1])
                last.then_inc(ta_ready, 1)
                act.wait_ge(ta_ready, CREDIT + t.count(2, 1))
                act.activation(la[:], la[:], ACT.Copy, scale=0.5, bias=0.5).then_inc(ta_ready, 1)
                act.activation(RAV[:, :, 2 * CH:].rearrange("p (a c) t -> p a c t", c=2),
                               part(2, i, j).rearrange("p a (c t) -> p a c t", c=2), ACT.Copy).then_inc(v_ready, 1)
                t.wait_filled(act, "cum")
                act.activation(W[:, :, 1:], chunks("cum"), ACT.Exp)
                t.drained(act.activation(Wi[:], chunks("cum"), ACT.Exp, scale=-1.0), "cum")
                act.activation(sz[:], part(3, i, j), ACT.Tanh, scale=0.5).then_inc(tz_ready, 1)
                hook("bonus")
                for c in range(2):
                    t.wait_filled(act, f"bkT{c}")
                    src = heads4(f"bkT{c}").rearrange("p a (h d) -> p a h d", h=2)
                    t.drained(act.activation(FB[:, c].rearrange("p a (h d) -> p a h d", h=4)[:, :, 0:4:3, :], src,
                                             ACT.Copy), f"bkT{c}")
                    t.wait_filled(act, f"avT{c}")
                    t.drained(act.activation(by_pair(XG[CH:, c, :, HD:]),
                                             heads4(f"avT{c}")[CH:].rearrange("p a (g d) -> p a g d", g=2), ACT.Copy), f"avT{c}")
                hook("aa3")
                for g in range(2):
                    t.wait_filled(act, f"ut{g}")
                    t.drained(act.activation(U[:, 4 * g:4 * g + 4, :], heads4(f"ut{g}"), ACT.Copy), f"ut{g}")
                for b in LEVELS:
                    for g in range(2):
                        t.wait_filled(act, f"q{b}_{g}")
                        t.drained(act.activation(block_cols(Q, g, b, 1), zero[:, 0:1].unsqueeze(2).unsqueeze(3).to_broadcast(
                            [P, 4, CH // b, b]), ACT.Copy), f"q{b}_{g}")
                    hook(f"d{b}_0")
                    for g in range(2 if b != LEVELS[-1] else 0):
                        t.wait_filled(act, f"t{b}_{g}")
                        t.drained(act.activation(block_cols(U, g, b, 0), block_cols(heads4(f"t{b}_{g}"), 0, b, 0),
                                                 ACT.Copy), f"t{b}_{g}")
                t.wait_filled(act, "akv")
                t.drained(act.activation(XA[:, :, HD:], heads8("akv"), ACT.Copy), "akv")
                for g in range(2):
                    t.wait_filled(act, f"x{g}")
                    t.drained(act.activation(XG[0:CH, 0, 4 * g:4 * g + 4, :], heads4(f"x{g}")[0:CH], ACT.Copy), f"x{g}")
                hook("rm1")
                for c in range(2):
                    for g in range(2):
                        rows = slice((1 - g) * CH, (2 - g) * CH)
                        t.wait_filled(act, f"sy{c}_{g}")
                        t.drained(act.activation(Y[c * CH:(c + 1) * CH, :, g, :], heads8(f"sy{c}_{g}")[rows, 0:NP],
                                                 ACT.Copy), f"sy{c}_{g}")
                act.wait_ge(yc_ready, CREDIT + t.count(1, 1))
                act.activation(yg[:], Y[:].rearrange("p a h d -> p a (h d)"), ACT.Square).then_inc(yq_ready, 1)
                for name in GROUP_NORM:
                    hook(name)
                t.wait_filled(act, "yT")
                for p in range(NP):
                    last = act.activation(yg[:, p, :], heads4("yT")[:, p, :], ACT.Identity, scale=vec[:, 4, p:p + 1],
                                          bias=vec[:, 5, p:p + 1])
                t.drained(last, "yT")
                hook("yT")

            act.wait_ge(setup, 2)
            for o in range(NU):
                drain_unit(0, o)
            lora_tanh(0)
            with act.Fori(0, NRB - 1) as i:
                for j in range(RJ):
                    tile(i, j, True)
            for j in range(RJ):
                tile(NRB - 1, j, False)

        @block.vector
        def _(v):
            ch = Chain(v, vch)
            MUL, ADD = ALU.mult, ALU.add
            level = {b: cst(f"level{b}") for b in LEVELS}

            def over4(mask):
                return mask.unsqueeze(1).to_broadcast([mask.shape[0], 4, mask.shape[1]])

            def shift_unit(n, o):
                b, u = o % 2, unit_at(o)
                v.wait_ge(pj_drained[b], CREDIT + pj_count(n, o) + 1)
                dst = lora[:] if u == NU - 1 else mix[:, u, bass.ds((n % 2) * RB, RB)]
                v.tensor_copy(carry[:, u:u + 1], raw[:, b, RB:])
                v.scalar_tensor_tensor(dst, raw[:, b, 0:RB], mu[:, u:u + 1], keep[:, b, :], MUL,
                                       ADD).then_inc(shifted, 1)

            def tile(i, j, beside):
                t = Tile(i, j, filled, drained)
                todo = units_of(j) if beside else []
                taken = [0]

                def hook(name):
                    while taken[0] < len(todo) and steps_due(j, name) >= 24 * (taken[0] + 1):
                        shift_unit(i + 1, todo[taken[0]])
                        taken[0] += 1

                ch.restart()
                r, k, vv, z = (part(g, i, j) for g in range(4))
                v.wait_ge(shifted, CREDIT + i * NU + NU)
                t.wait_filled(v, "lora_w")
                t.drained(v.tensor_tensor(lw[:], flat("lora_w"), w0b[:], ADD), "lora_w")
                t.wait_filled(v, "kk_sum")
                m = ch.mark(v.tensor_scalar(rn[:, 0, :], flat("kk_sum")[:, 0:NH], 1e-24, None, ALU.max))
                kk_made = ch.mark(v.tensor_tensor(kk[:], k, bc(vec[:, 1, :], TT), MUL))
                ch.wait(m)
                rsqrt_small(v, ch, rn[:, 0, :], rn[:, 1, :], rn[:, 2, :])
                t.drained(v.tensor_copy(rnb[:], bc(rn[:, 1, :], HD)), "kk_sum")
                v.wait_ge(ta_ready, CREDIT + t.count(2, 1))
                ch.link(v.tensor_tensor(km[:], k, t1[:], MUL))
                v.tensor_tensor(sq[:], r, km[:], MUL).then_inc(rk_ready, 1)
                t.wait_filled(v, "kk_scale")
                ch.wait(kk_made)
                t.drained(v.tensor_tensor(kk[:], kk[:], heads4("kk_scale"), MUL), "kk_scale")
                t.wait_drained(v, "cum")
                as8 = lambda a: a.rearrange("p a (c t) -> p (a c) t", c=2)
                v.tensor_tensor(RAV[:, :, 0:CH].rearrange("p (a c) t -> p a c t", c=2),
                                r.rearrange("p a (c t) -> p a c t", c=2),
                                W[:, :, 1:].rearrange("p (a c) t -> p a c t", c=2), MUL)
                v.tensor_tensor(BK[:, :, CH:], as8(km[:]), Wi[:], MUL)
                t.wait_drained(v, "kk_scale")
                v.scalar_tensor_tensor(RAV[:, :, CH:2 * CH], as8(kk[:]), -1.0, W[:, :, 0:CH], MUL, MUL)
                v.wait_ge(ta_ready, CREDIT + t.count(2, 2))
                ch.link(v.tensor_tensor(la[:], la[:], kk[:], MUL))
                v.tensor_tensor(BK[:, :, 0:CH], as8(la[:]), Wi[:], MUL).then_inc(ops_ready, 1)
                hook("kk_scale")
                t.wait_filled(v, "bonus")
                t.drained(v.tensor_tensor(bonv[:], heads4("bonus"), vv, MUL), "bonus")
                hook("bonus")
                for c in range(2):
                    t.wait_filled(v, f"avT{c}")
                    t.drained(v.tensor_copy(by_pair(XA[c * CH:(c + 1) * CH, :, 0:HD]),
                                            heads4(f"avT{c}")[0:CH].rearrange("p a (g d) -> p a g d", g=2)), f"avT{c}")
                v.wait_ge(tz_ready, CREDIT + t.count(1, 1))
                v.scalar_tensor_tensor(sz[:], sz[:], 1.0, z, ADD, MUL)
                for n in range(4):
                    c, g = n // 2, n % 2
                    t.wait_filled(v, f"aa{n}")
                    v.tensor_tensor(FB[:, c, :, (1 + g) * HD:(2 + g) * HD], heads4(f"aa{n}")[:, :, 0:CH],
                                    over4(cst("mask_r")), MUL)
                    t.drained(v.tensor_tensor(AkT[CH:, c, 4 * g:4 * g + 4, :], heads4(f"aa{n}")[CH:, :, CH:],
                                              over4(cst("mask_a")[CH:]), MUL), f"aa{n}")
                hook("aa3")
                for g in range(2):
                    hs = slice(4 * g, 4 * g + 4)
                    t.wait_filled(v, f"lt{g}")
                    t.drained(v.tensor_tensor(LT[:, hs, :], heads4(f"lt{g}"), over4(cst("strict")), MUL), f"lt{g}")
                    t.wait_drained(v, f"lt{g}")
                    ch.link(v.tensor_tensor(UT[:, hs, :], LT[:, hs, :], over4(cst("pair0")), MUL))
                    v.tensor_tensor(UT[:, hs, :], UT[:, hs, :], over4(cst("ident")), ADD).then_inc(ut_ready, 1)
                v.wait_ge(ut_ready, CREDIT + t.count(2, 2))
                for b in LEVELS:
                    for g in range(2):
                        t.wait_filled(v, f"q{b}_{g}")
                        mask = level[b].rearrange("p (n t) -> p n t", t=b).unsqueeze(1).to_broadcast([P, 4, CH // b, b])
                        t.drained(v.tensor_tensor(block_cols(Q, g, b, 0), halves(f"q{b}_{g}", b)[:, 0], mask, MUL),
                                  f"q{b}_{g}")
                    hook(f"d{b}_0")
                    for g in range(2):
                        t.wait_filled(v, f"d{b}_{g}")
                        cols = block_cols(UT, g, b, 1)
                        t.drained(v.tensor_tensor(cols, cols, halves(f"d{b}_{g}", b)[:, 0], ADD), f"d{b}_{g}")
                    t.wait_drained(v, f"d{b}_0")
                    t.wait_drained(v, f"d{b}_1")
                for g in range(2):
                    t.wait_filled(v, f"x{g}")
                    t.drained(v.tensor_copy(XG[0:CH, 1, 4 * g:4 * g + 4, :], heads4(f"x{g}")[CH:]), f"x{g}")
                for c in range(2):
                    t.wait_filled(v, f"rm{c}")
                    rw = RAV[:].rearrange("p (a c) t -> p a c t", c=2)[:, :, c, 0:CH]
                    one = cst("ident")
                    src = heads4(f"rm{c}")
                    v.tensor_tensor(RM[0:HD, c, :, 0:HD], src[0:HD, :, 0:HD], over4(one[0:HD, 0:HD]), ADD)
                    v.tensor_tensor(RM[0:HD, c, :, HD:], src[0:HD, :, HD:], rw[0:HD], ADD)
                    v.tensor_tensor(RM[HD:, c, :, 0:HD], src[HD:, :, 0:HD], rw[HD:], ADD)
                    t.drained(v.tensor_tensor(RM[HD:, c, :, HD:], src[HD:, :, HD:], over4(one[HD:, HD:]), ADD), f"rm{c}")
                hook("rm1")
                for c in range(2):
                    wc = W[:].rearrange("p (a c) t -> p a c t", c=2)[:, :, c, CH:]
                    for g in range(2):
                        rows = slice(g * HD, (g + 1) * HD)
                        t.wait_filled(v, f"sy{c}_{g}")
                        t.drained(v.tensor_tensor(S[rows], heads8(f"sy{c}_{g}")[rows, 0:NP],
                                                  wc[rows].to_broadcast([HD, NP, HD]), MUL), f"sy{c}_{g}")
                t.wait_drained(v, "sy1_0")
                t.wait_drained(v, "sy1_1")
                y8 = Y[:].rearrange("p a h d -> p (a h) d")
                ch.link(v.tensor_reduce(rn[:, 0, :], y8, AX, ADD))
                v.scalar_tensor_tensor(y8, bc(rn[:, 0, :], HD), -1.0 / HD, y8, MUL, ADD).then_inc(yc_ready, 1)
                v.wait_ge(yq_ready, CREDIT + t.count(1, 1))
                ch.link(v.tensor_reduce(rn[:, 0, :], yg[:].rearrange("p a (h d) -> p (a h) d", h=2), AX, ADD))
                ch.link(v.tensor_scalar(rn[:, 0, :], rn[:, 0, :], 1.0 / HD, GN_EPS, MUL, ADD))
                hook("norm0")
                rsqrt_small(v, ch, rn[:, 0, :], rn[:, 1, :], rn[:, 2, :])
                hook("norm1")
                v.tensor_tensor(y8, y8, bc(rn[:, 1, :], HD), MUL).then_inc(yn_ready, 1)
                hook("norm2")
                t.wait_drained(v, "yT")
                ch.link(v.tensor_tensor(yg[:], yg[:], bonv[:], ADD))
                v.wait_ge(y_stored[j], CREDIT + i * 16)
                v.scalar_tensor_tensor(yo[:, j], yg[:], 0.5, sz[:], MUL, MUL).then_inc(y_ready, 1)
                hook("yT")

            v.memset(S[:], 0.0)
            v.memset(carry[:], 0.0)
            v.memset(zero[:], 0.0)
            v.memset(W[:], 1.0).then_inc(setup, 1)
            v.wait_ge(c_loaded, 16 * 10)
            ch.link(v.tensor_scalar(mq[:], mu[:], -1.0, 1.0, MUL, ADD))
            ch.link(v.tensor_scalar(vec[:, 2, :], vec[:, 2, :], 0.5, None, MUL))
            ch.link(v.tensor_scalar(omk[:], vec[:, 2, :], -1.0, 1.0, MUL, ADD))
            ch.link(v.tensor_scalar(vec[:, 0, :], vec[:, 0, :], 0.5, None, MUL))
            for p in range(NP):
                last = v.tensor_scalar(rk1[:, p, :], cst("heads"), vec[:, 3, p:p + 1], None, MUL)
            ch.link(last)
            v.tensor_scalar(mq[:], mq[:], unscale, None, MUL).then_inc(setup, 1)
            v.wait_ge(setup, 2)
            for o in range(NU):
                shift_unit(0, o)
            ch.restart()
            with v.Fori(0, NRB - 1) as i:
                for j in range(RJ):
                    tile(i, j, True)
                ch.restart()
            for j in range(RJ):
                tile(NRB - 1, j, False)

        @block.tensor
        def _(pe):
            ident = cst("ident")

            def unit_steps(n, o):
                b, u = o % 2, unit_at(o)
                block_ht = [ht[:, bass.ds((n % 2) * 2 + part, 1)].rearrange("p a k t -> p (a k) t") for part in range(2)]
                pe.wait_ge(pj_drained[b], CREDIT + pj_count(n, o))
                if o == 0:
                    pe.wait_ge(ht_loaded, n * 16 + 16)
                for k, last in enumerate(project_steps(pe, pj[b][:], whi, wlo, block_ht, u)):
                    if k == 23:
                        last.then_inc(pj_filled[b], 1)
                    yield

            def tile(i, j, beside):
                t = Tile(i, j, filled, drained)
                steps = (s for u in (units_of(j) if beside else []) for s in unit_steps(i + 1, u))
                issued = [0]

                def end(name, last):
                    t.filled(last, name)
                    fill(name)

                def fill(name):
                    while issued[0] < steps_due(j, name) and beside:
                        next(steps)
                        issued[0] += 1

                ts = slice(j * TT, (j + 1) * TT)
                pe.wait_ge(lora_ready, CREDIT + i + 1)
                t.before_fill(pe, "lora_w")
                end("lora_w", pe.matmul(flat("lora_w"), lora[0:LORA, ts], lup[0:LORA, :], start=True, stop=True))
                t.before_fill(pe, "lora_a")
                for p in range(NP):
                    last = pe.matmul(heads4("lora_a")[:, p, :], lup[LORA:, p * P:(p + 1) * P], lora[LORA:, ts],
                                     start=True, stop=True)
                end("lora_a", last)
                pe.wait_ge(sq_ready, CREDIT + t.count(1, 1))
                t.before_fill(pe, "kk_sum")
                for p in range(NP):
                    last = pe.matmul(flat("kk_sum")[:, 2 * p:2 * p + 2], sq[:, p, :], cst("sel2"), start=True, stop=True)
                end("kk_sum", last)
                pe.wait_ge(ld_ready, CREDIT + t.count(1, 1))
                t.before_fill(pe, "cum")
                for p in range(NP):
                    last = pe.matmul(heads4("cum")[:, p, :], lw[:, p * P:(p + 1) * P], cst("tri"), start=True, stop=True)
                end("cum", last)
                t.wait_drained(pe, "kk_sum")
                t.before_fill(pe, "kk_scale")
                for p in range(NP):
                    last = pe.matmul(heads4("kk_scale")[:, p, :], rnb[:, 2 * p:2 * p + 2, :].rearrange("p h d -> p (h d)"),
                                     ident, start=True, stop=True)
                end("kk_scale", last)
                pe.wait_ge(rk_ready, CREDIT + t.count(1, 1))
                t.before_fill(pe, "bonus")
                for p in range(NP):
                    last = pe.matmul(heads4("bonus")[:, p, :], rk1[:, p, :], sq[:, p, :], start=True, stop=True)
                end("bonus", last)
                pe.wait_ge(ops_ready, CREDIT + t.count(1, 1))
                for c in range(2):
                    t.before_fill(pe, f"bkT{c}")
                    for p in range(NP):
                        last = pe.transpose(heads4(f"bkT{c}")[:, p, :], BK[:, 2 * p + c, :], ident)
                    end(f"bkT{c}", last)
                pe.wait_ge(v_ready, CREDIT + t.count(1, 1))
                for c in range(2):
                    t.before_fill(pe, f"avT{c}")
                    for p in range(NP):
                        last = pe.transpose(heads4(f"avT{c}")[:, p, :], RAV[:, 2 * p + c, CH:], ident)
                    end(f"avT{c}", last)
                for n in range(4):
                    c, h = n // 2, slice(n % 2 * HD, (n % 2 + 1) * HD)
                    t.before_fill(pe, f"aa{n}")
                    for p in range(NP):
                        last = pe.matmul(heads4(f"aa{n}")[:, p, :], BK[h, 2 * p + c, :], RAV[h, 2 * p + c, 0:2 * CH],
                                         start=True, stop=True)
                    end(f"aa{n}", last)
                for g in range(2):
                    t.before_fill(pe, f"lt{g}")
                    pe.sem_inc(passed, 1)
                    h = slice(g * HD, (g + 1) * HD)
                    for p in range(NP):
                        for c in range(2):
                            last = pe.matmul(heads4(f"lt{g}")[c * CH:(c + 1) * CH, p, :], BK[h, 2 * p + c, 0:CH],
                                             RAV[h, 2 * p:2 * p + 2, CH:2 * CH], start=True, stop=True)
                    end(f"lt{g}", last)

                def turn(name, g):
                    t.before_fill(pe, name)
                    for q in range(4):
                        last = pe.transpose(heads4(name)[:, q, :], UT[:, 4 * g + q, :], ident)
                    end(name, last)

                for g in range(2):
                    pe.wait_ge(ut_ready, CREDIT + t.count(2, g + 1))
                    turn(f"ut{g}", g)
                source = "ut{g}"
                for b in LEVELS:
                    for g in range(2):
                        t.wait_drained(pe, source.format(g=g))
                        t.before_fill(pe, f"q{b}_{g}")
                        for q in range(4):
                            last = pe.matmul(halves(f"q{b}_{g}", b)[:, 0, q], LT[:, 4 * g + q, :],
                                             block_cols(U, g, b, 0)[:, q], start=True, stop=True)
                        end(f"q{b}_{g}", last)
                    for g in range(2):
                        t.wait_drained(pe, f"q{b}_{g}")
                        t.before_fill(pe, f"d{b}_{g}")
                        for q in range(4):
                            last = pe.matmul(halves(f"d{b}_{g}", b)[:, 0, q], Q[:, 4 * g + q, :],
                                             block_cols(UT, g, b, 1)[:, q], start=True, stop=True)
                        end(f"d{b}_{g}", last)
                    if b != LEVELS[-1]:
                        for g in range(2):
                            t.wait_drained(pe, f"d{b}_{g}")
                            turn(f"t{b}_{g}", g)
                        source = f"t{b}_" + "{g}"
                t.before_fill(pe, "akv")
                pe.sem_inc(passed, 1)
                for c in range(2):
                    for h in range(NH):
                        last = pe.matmul(heads8("akv")[c * CH:(c + 1) * CH, h, :], AkT[CH:, c, h, :],
                                         XG[CH:, c, h, HD:], start=True, stop=True)
                end("akv", last)
                t.wait_drained(pe, "akv")
                for g in range(2):
                    t.wait_drained(pe, f"d{LEVELS[-1]}_{g}")
                    t.before_fill(pe, f"x{g}")
                    for q in range(4):
                        last = pe.matmul(heads4(f"x{g}")[:, q, :], UT[:, 4 * g + q, :], XA[:, 4 * g + q, :],
                                         start=True, stop=True)
                    end(f"x{g}", last)
                t.wait_drained(pe, "x0")
                t.wait_drained(pe, "x1")
                for c in range(2):
                    t.before_fill(pe, f"rm{c}")
                    pe.sem_inc(passed, 1)
                    for h in range(NH):
                        g, p = h // NP, h % NP
                        last = pe.matmul(heads4(f"rm{c}")[g * HD:(g + 1) * HD, p, :], XG[0:CH, c, h, 0:HD],
                                         FB[0:CH, c, p, g * 2 * HD:(g + 1) * 2 * HD], start=True, stop=True)
                    end(f"rm{c}", last)
                for c in range(2):
                    t.wait_drained(pe, f"rm{c}")
                    for g in range(2):
                        if c:
                            t.wait_drained(pe, f"sy0_{g}")
                        t.before_fill(pe, f"sy{c}_{g}")
                        rows = slice(g * HD, (g + 1) * HD)
                        for p in range(NP):
                            out = heads8(f"sy{c}_{g}")[:, p, :]
                            pe.matmul(out, FB[:, c, p, g * 2 * HD:(g + 1) * 2 * HD], XG[:, c, g * NP + p, HD:],
                                      start=True, stop=False)
                            last = pe.matmul(out, RM[rows, c, p, :], S[rows, p, :], start=False, stop=True)
                        end(f"sy{c}_{g}", last)
                for name in GROUP_NORM:
                    fill(name)
                pe.wait_ge(yn_ready, CREDIT + t.count(1, 1))
                t.before_fill(pe, "yT")
                for p in range(NP):
                    last = pe.transpose(heads4("yT")[:, p, :], Y[:, p].rearrange("p h d -> p (h d)"), ident)
                end("yT", last)

            pe.wait_ge(setup, 2)
            for u in range(NU):
                for _ in unit_steps(0, u):
                    pass
            with pe.Fori(0, NRB - 1) as i:
                for j in range(RJ):
                    tile(i, j, True)
            for j in range(RJ):
                tile(NRB - 1, j, False)


def out_phase(nc, x, w_out, post_g, y_dram, out):
    with ExitStack() as ctx:
        sb = lambda name, shape, dt=F32: ctx.enter_context(nc.sbuf_tensor(name, shape, dt))
        ps = lambda name, shape, dt=F32: ctx.enter_context(nc.psum_tensor(name, shape, dt))
        sem = lambda name: ctx.enter_context(nc.semaphore(name))
        wst = sb("o_w_stage", [P, D])
        whi = sb("o_w_hi", [P, KB, D], F32R)
        wlo = sb("o_w_lo", [P, KB, D], F32R)
        yt = sb("o_y", [P, 2, KB, TT])
        yhi = sb("o_y_hi", [P, 2, KB, TT], F32R)
        ylo = sb("o_y_lo", [P, 2, KB, TT], F32R)
        xt = sb("o_x", [P, 2, D])
        ot = sb("o_out", [P, 2, D])
        junk = sb("o_junk", [P, D])
        pg = sb("o_post_g", [P, D])
        ss = sb("o_ss", [P, 2])
        eps = sb("o_eps", [P, 1])
        pO = [ps(f"o_acc{b}", [P, D]) for b in range(2)]
        w_loaded, w_hi, w_freed, g_loaded = sem("o_w_loaded"), sem("o_w_hi_ready"), sem("o_w_freed"), sem("o_g_loaded")
        y_loaded, x_loaded = [sem(f"o_y_loaded{b}") for b in range(2)], [sem(f"o_x_loaded{b}") for b in range(2)]
        y_hi, y_lo = sem("o_y_hi_ready"), sem("o_y_lo_ready")
        filled, squared, rooted, drained = sem("o_filled"), sem("o_squared"), sem("o_rooted"), sem("o_drained")
        ready = sem("o_ready")
        stored = [sem(f"o_stored{b}") for b in range(2)]
        vch = sem("o_vchain")
        setup = sem("o_setup")
        block = ctx.enter_context(nc.Block())
        y_v = y_dram.rearrange("(b p) t -> p b t", p=P)

        @block.sync
        def _(sp):
            for credited in (y_hi, y_lo, filled, squared, rooted, drained, ready, *stored):
                sp.sem_inc(credited, CREDIT)
            with nc.allow_non_contiguous_dma("broadcast over partitions"):
                sp.dma_start(pg[:], post_g[0:1, :].to_broadcast([P, D])).then_inc(g_loaded, 16)
            for kb in range(KB):
                if kb:
                    sp.wait_ge(w_freed, kb)
                sp.dma_start(wst[:], w_out[0, kb * P:(kb + 1) * P, :]).then_inc(w_loaded, 16)

            def load(t, u):
                if not (isinstance(t, int) and t == 0):
                    sp.wait_ge(y_lo, CREDIT + t - 1)
                sp.dma_start(yt[:, u], y_v[:, :, bass.ds(t * TT, TT)]).then_inc(y_loaded[u], 16)

            def store(t, u):
                sp.wait_ge(ready, CREDIT + t * 2 + 2)
                sp.dma_start(out[0, bass.ds(t * TT, TT), :], ot[:, u, :]).then_inc(stored[u], 16)

            load(0, 0)
            with sp.Fori(0, NT // 2 - 1) as pair:
                load(pair * 2 + 1, 1)
                store(pair * 2, 0)
                load(pair * 2 + 2, 0)
                store(pair * 2 + 1, 1)
            load(NT - 1, 1)
            store(NT - 2, 0)
            store(NT - 1, 1)
            for u in range(2):
                sp.wait_ge(stored[u], CREDIT + NT // 2 * 16)

        @block.gpsimd
        def _(pool):
            with pool.Fori(0, NT // 2) as pair:
                i = pair * 2
                for u in range(2):
                    pool.wait_ge(ready, CREDIT + i * 2)
                    pool.dma_start(xt[:, u, :], x[0, bass.ts(i + u, TT), :]).then_inc(x_loaded[u], 16)

        @block.scalar
        def _(act):
            for kb in range(KB):
                act.wait_ge(w_loaded, 16 * (kb + 1))
                act.activation(whi[:, kb, :], wst[:], ACT.Copy).then_inc(w_hi, 1)
            act.wait_ge(setup, 1)

            def high(t, u):
                act.wait_ge(y_loaded[u], (t - u) * 8 + 16)
                if not (isinstance(t, int) and t == 0):
                    act.wait_ge(drained, CREDIT + t - 1)
                act.activation(yhi[:, u], yt[:, u], ACT.Copy).then_inc(y_hi, 1)

            def root(t, u):
                act.wait_ge(filled, CREDIT + t + 1)
                act.wait_ge(drained, CREDIT + t)
                act.activation(junk[:], pO[u][:], ACT.Square, accum_out=ss[:, 0:1]).then_inc(squared, 1)
                act.wait_ge(squared, CREDIT + t + 1)
                act.activation(ss[:, 1:2], ss[:, 0:1], ACT.Sqrt, scale=1.0 / D, bias=eps[:]).then_inc(rooted, 1)

            high(0, 0)
            with act.Fori(0, NT // 2 - 1) as pair:
                high(pair * 2 + 1, 1)
                root(pair * 2, 0)
                high(pair * 2 + 2, 0)
                root(pair * 2 + 1, 1)
            high(NT - 1, 1)
            root(NT - 2, 0)
            root(NT - 1, 1)

        @block.vector
        def _(v):
            ch = Chain(v, vch)
            v.memset(eps[:], RMS_EPS).then_inc(setup, 1)
            for kb in range(KB):
                v.wait_ge(w_hi, kb + 1)
                v.tensor_tensor(wlo[:, kb, :], wst[:], whi[:, kb, :].bitcast(F32), ALU.subtract).then_inc(w_freed, 1)
            v.wait_ge(g_loaded, 16)

            def low(t, u):
                v.wait_ge(y_hi, CREDIT + t + 1)
                v.tensor_tensor(ylo[:, u], yt[:, u], yhi[:, u].bitcast(F32), ALU.subtract).then_inc(y_lo, 1)

            def finish(t, u):
                v.wait_ge(rooted, CREDIT + t + 1)
                ch.link(v.reciprocal(ss[:, 1:2], ss[:, 1:2]))
                v.wait_ge(stored[u], CREDIT + (t - u) * 8)
                for c in range(2):
                    cs = slice(c * 512, (c + 1) * 512)
                    last = v.scalar_tensor_tensor(ot[:, u, cs], pO[u][:, cs], ss[:, 1:2], pg[:, cs], ALU.mult, ALU.mult)
                    if c == 0:
                        ch.mark(last)
                last.then_inc(drained, 1)
                ch.restart()
                v.wait_ge(x_loaded[u], (t - u) * 8 + 16)
                v.wait_ge(drained, CREDIT + t + 1)
                for c in range(2):
                    cs = slice(c * 512, (c + 1) * 512)
                    v.tensor_tensor(ot[:, u, cs], ot[:, u, cs], xt[:, u, cs], ALU.add).then_inc(ready, 1)

            low(0, 0)
            with v.Fori(0, NT // 2 - 1) as pair:
                low(pair * 2 + 1, 1)
                finish(pair * 2, 0)
                low(pair * 2 + 2, 0)
                finish(pair * 2 + 1, 1)
            low(NT - 1, 1)
            finish(NT - 2, 0)
            finish(NT - 1, 1)

        @block.tensor
        def _(pe):
            pe.wait_ge(w_freed, KB)
            with pe.Fori(0, NT // 2) as pair:
                i = pair * 2
                for u in range(2):
                    pe.wait_ge(y_lo, CREDIT + i + u + 1)
                    pe.wait_ge(drained, CREDIT + i)
                    for c in range(2):
                        cs = slice(c * 512, (c + 1) * 512)
                        for kb in range(KB):
                            for n, (y, w) in enumerate(((yhi, whi), (yhi, wlo), (ylo, whi))):
                                last = pe.matmul(pO[u][:, cs], y[:, u, kb, :], w[:, kb, cs], start=kb == 0 and n == 0,
                                                 stop=kb == KB - 1 and n == 2)
                    last.then_inc(filled, 1)


def hybrid_kernel(nc, inp, consts, place, out):
    ht_dram = nc.dram_tensor("hT_blocks", [NRB, P, 2, KB, RB], F16, kind="Internal").ap()
    y_dram = nc.dram_tensor("mixed_T", [D, SEQ], F32, kind="Internal").ap()

    def shape_tile(ctx, names):
        width = sum(place[name][1] for name in names)
        ct = ctx.enter_context(nc.sbuf_tensor("shape_consts_" + names[-1], [P, width], F32))
        where, at = {}, 0
        with nc.semaphore("consts_loaded_" + names[-1]) as loaded, nc.Block() as block:
            for name in names:
                where[name] = ct[:, at:at + place[name][1]]
                at += place[name][1]

            @block.sync
            def _(sp):
                for name in names:
                    first, n = place[name]
                    sp.dma_start(where[name], consts[:, first:first + n]).then_inc(loaded, 16)
                sp.wait_ge(loaded, 16 * len(names))
        return where.__getitem__

    with ExitStack() as rw:
        unscale_t = rw.enter_context(nc.sbuf_tensor("unscale", [P, 1], F32))
        whi_r = rw.enter_context(nc.sbuf_tensor("w_rwkv_hi", [P, KB, NSH], F16))
        wlo_r = rw.enter_context(nc.sbuf_tensor("w_rwkv_lo", [P, KB, NSH], F16))
        with ExitStack() as cv:
            cst = shape_tile(cv, ["ident", "mean"])
            whi_c = cv.enter_context(nc.sbuf_tensor("w_conv_hi", [P, KB, 3 * DC], F16))
            wlo_c = cv.enter_context(nc.sbuf_tensor("w_conv_lo", [P, KB, 3 * DC], F16))
            weights_phase(nc, inp["w_in"], inp["pre_g"], whi_r, wlo_r, whi_c, wlo_c, unscale_t[:])
            conv_phase(nc, cst, inp["x"], inp["dw_w"], inp["dw_b"], inp["ln_g"], inp["ln_b"], whi_c, wlo_c,
                       unscale_t[:], ht_dram, y_dram[DR:, :])
        cst = shape_tile(rw, [name for name in place if name != "mean"])
        rwkv_phase(nc, cst, inp, whi_r, wlo_r, unscale_t[:], ht_dram, y_dram[0:DR, :])
    out_phase(nc, inp["x"], inp["w_out"], inp["post_g"], y_dram, out)


_INS = ["x", "pre_g", "post_g", "w_in", "mu_shift", "w0", "w_up", "a0", "a_up", "k_k", "k_a", "r_k", "gn_g", "gn_b",
        "dw_w", "dw_b", "ln_g", "ln_b", "w_out"]


def kernel(**inputs):
    import concourse.bacc as bacc
    from concourse.bass_utils import run_bass_kernel_spmd

    nc = bacc.Bacc("TRN2", target_bir_lowering=False, num_devices=1)
    arrays, aps = {}, {}
    for name in _INS:
        a = np.ascontiguousarray(inputs[name])
        arrays[f"in_{name}"] = a
        aps[name] = nc.dram_tensor(f"in_{name}", a.shape, mybir.dt.from_np(a.dtype), kind="ExternalInput").ap()
    consts, place = shape_constants()
    arrays["in_consts"] = consts
    cap = nc.dram_tensor("in_consts", consts.shape, F32, kind="ExternalInput").ap()
    out = nc.dram_tensor("out_x", [1, SEQ, D], F32, kind="ExternalOutput").ap()
    hybrid_kernel(nc, aps, cap, place, out)
    r = run_bass_kernel_spmd(nc, [arrays], core_ids=[0])
    return r.results[0]["out_x"]
```

```python
import math
from contextlib import ExitStack

import numpy as np

import concourse.bass as bass
from concourse import mybir
from concourse.alu_op_type import AluOpType as ALU

F32 = mybir.dt.float32
F32R = mybir.dt.float32r
F16 = mybir.dt.float16
I32 = mybir.dt.int32
ACT = mybir.ActivationFunctionType
AX = mybir.AxisListType.X
RMAX = bass.bass_isa.ReduceOp.max

P = 128
SEQ, D = 4096, 1024
DR = 512
DC = 512
NP = DR // P
HD = 64
NH = DR // HD
CH = 64
TAPS = 31
HALO = TAPS - 1
LORA = 64
NSH = 4 * DR + 2 * LORA
NU = NSH // P
NIN = NSH + 3 * DC
KB = D // P
TB = 512
NB = SEQ // TB
TT = 128
JT = TB // TT
RB = 256
NRB = SEQ // RB
RJ = RB // TT
NT = SEQ // TT
KAPPA = float(np.exp(-0.5))
H_SCALE = 1024.0
W_TOP = 16384.0
RMS_EPS, GN_EPS, LN_EPS = 1e-6, 64e-5, 1e-5
CREDIT = 1
LEVELS = (2, 4, 8, 16, 32)


def shape_constants():
    s = np.arange(P)[:, None]
    t = np.arange(P)[None, :]
    same = s // CH == t // CH
    tc = np.arange(CH)[None, :]
    parts = {
        "ident": s == t,
        "tri": same & (s <= t),
        "pair0": (t % 2 == 1) & (s == t - 1),
        "mask_r": s % CH <= tc,
        "mask_a": s % CH < tc,
        "heads": s // HD == t // HD,
        "sel2": s // HD == np.arange(2)[None, :],
        "mean": np.full((P, P), 1.0 / DC),
    }
    for b in LEVELS:
        parts[f"level{b}"] = (s // b % 2 == 1) & (tc // b == s // b // 2)
    place, at = {}, 0
    for name, a in parts.items():
        place[name] = (at, a.shape[1])
        at += a.shape[1]
    return np.concatenate([a.astype(np.float32) for a in parts.values()], axis=1), place


class Chain:

    def __init__(self, eng, sem):
        self.eng, self.sem, self.n = eng, sem, 0

    def mark(self, ins):
        ins.then_inc(self.sem, 1)
        self.n += 1
        return self.n

    def wait(self, n):
        self.eng.wait_ge(self.sem, n)

    def link(self, ins):
        self.wait(self.mark(ins))

    def restart(self):
        if self.n:
            self.wait(self.n)
            self.eng.sem_clear(self.sem)
        self.n = 0


def rsqrt_small(v, chain, x, y, t):
    chain.link(v.tensor_scalar(y.bitcast(I32), x.bitcast(I32), 1, None, ALU.logical_shift_right))
    chain.link(v.tensor_scalar(y.bitcast(I32), y.bitcast(I32), -1.0, float(0x5F3759DF), ALU.mult, ALU.add))
    for _ in range(3):
        chain.link(v.tensor_tensor(t, x, y, ALU.mult))
        chain.link(v.scalar_tensor_tensor(t, t, -0.5, y, ALU.mult, ALU.mult))
        chain.link(v.scalar_tensor_tensor(y, t, 1.5, y, ALU.add, ALU.mult))


W_STAGES = 5


def weights_phase(nc, w_in, pre_g, whi_r, wlo_r, whi_c, wlo_c, unscale):
    with ExitStack() as ctx:
        sb = lambda name, shape, dt=F32: ctx.enter_context(nc.sbuf_tensor(name, shape, dt))
        sem = lambda name: ctx.enter_context(nc.semaphore(name))
        wbuf = sb("w_stage", [P, W_STAGES, NIN])
        wmax = sb("w_max", [P, KB])
        gcol = sb("pre_g_col", [P, KB])
        m2 = sb("w_m2", [P, 2])
        m2a = sb("w_m2a", [P, 2])
        pw = sb("w_pow", [P, 4])
        gs = sb("pre_g_scaled", [P, KB])
        w_loaded = [sem(f"w_loaded{b}") for b in range(W_STAGES)]
        g_loaded = sem("g_loaded")
        w_freed = sem("w_freed")
        gs_ready = sem("w_scale_ready")
        hi_done = sem("w_hi_done")
        max_ready = sem("w_max_ready")
        max_all = sem("w_max_all")
        vch = sem("w_vchain")
        loads = [(kb, kb % W_STAGES) for kb in range(KB)]
        loads += [(kb, (kb + KB) % W_STAGES) for kb in range(KB - W_STAGES)]
        splits = [(kb, kb % W_STAGES) for kb in range(KB - W_STAGES, KB)] + loads[KB:]
        loads_of = lambda stage, upto: sum(st == stage for _, st in loads[:upto])
        block = ctx.enter_context(nc.Block())

        @block.sync
        def _(sp):
            with nc.allow_non_contiguous_dma("64 columns of one number"):
                sp.dma_start(gcol[:], pre_g.rearrange("a (k p) -> p (a k)", p=P)).then_inc(g_loaded, 16)
            for n, (kb, stage) in enumerate(loads):
                if n >= W_STAGES:
                    sp.wait_ge(w_freed, n - W_STAGES + 1 if n < KB else n + 1)
                sp.dma_start(wbuf[:, stage, :], w_in[0, kb * P:(kb + 1) * P, :]).then_inc(w_loaded[stage], 16)

        @block.gpsimd
        def _(pool):
            pool.wait_ge(max_ready, 1)
            nc.gpsimd.partition_all_reduce(m2a[:], m2[:], P, RMAX).then_inc(max_all, 1)

        @block.vector
        def _(v):
            ch = Chain(v, vch)
            for n in range(KB):
                v.wait_ge(w_loaded[n % W_STAGES], 16 * loads_of(n % W_STAGES, n + 1))
                v.tensor_reduce(wmax[:, n:n + 1], wbuf[:, n % W_STAGES, :], AX, ALU.max,
                                apply_absolute_value=True).then_inc(w_freed, 1)
            v.wait_ge(w_freed, KB)
            ch.link(v.tensor_reduce(m2[:, 0:1], wmax[:], AX, ALU.max))
            v.wait_ge(g_loaded, 16)
            v.tensor_reduce(m2[:, 1:2], gcol[:], AX, ALU.max, apply_absolute_value=True).then_inc(max_ready, 1)
            v.wait_ge(max_all, 1)
            ch.link(v.tensor_scalar(pw[:, 0:1], m2a[:, 0:1], m2a[:, 1:2], 1e-30, ALU.mult, ALU.max))
            ch.link(v.tensor_scalar(pw[:, 1:2].bitcast(I32), pw[:, 0:1].bitcast(I32), 0x7F800000, None,
                                    ALU.bitwise_and))
            ch.link(v.reciprocal(pw[:, 2:3], pw[:, 1:2]))
            ch.link(v.tensor_scalar(pw[:, 3:4], pw[:, 2:3], W_TOP, None, ALU.mult))
            v.tensor_scalar(gs[:], gcol[:], pw[:, 3:4], None, ALU.mult).then_inc(gs_ready, 1)
            ch.link(v.tensor_scalar(unscale, pw[:, 1:2], 1.0 / (W_TOP * H_SCALE), None, ALU.mult))
            for n, (kb, stage) in enumerate(splits):
                v.wait_ge(hi_done, 2 * n + 2)
                for lo, hi, cs in ((wlo_r, whi_r, slice(0, NSH)), (wlo_c, whi_c, slice(NSH, NIN))):
                    last = v.scalar_tensor_tensor(lo[:, kb, :], wbuf[:, stage, cs], gs[:, kb:kb + 1], hi[:, kb, :],
                                                  ALU.mult, ALU.subtract)
                last.then_inc(w_freed, 1)

        @block.scalar
        def _(act):
            act.wait_ge(gs_ready, 1)
            for n, (kb, stage) in enumerate(splits):
                if n >= W_STAGES:
                    act.wait_ge(w_loaded[stage], 16 * loads_of(stage, KB + n - W_STAGES + 1))
                for hi, cs in ((whi_r, slice(0, NSH)), (whi_c, slice(NSH, NIN))):
                    act.activation(hi[:, kb, :], wbuf[:, stage, cs], ACT.Copy,
                                   scale=gs[:, kb:kb + 1]).then_inc(hi_done, 1)


CONV_CONSTS = ["ident", "mean"]

UNIT_ORDER = [("gate", 0), ("value", 0)]
for _b in range(1, NP):
    UNIT_ORDER += [("gate", _b), ("value", _b), ("z", _b - 1)]
UNIT_ORDER += [("z", NP - 1)]


def conv_phase(nc, shapes, x, dw_w, dw_b, ln_g, ln_b, whi, wlo, unscale, ht_dram, y_dram):
    cst, load_shapes = shapes
    with ExitStack() as ctx:
        sb = lambda name, shape, dt=F32: ctx.enter_context(nc.sbuf_tensor(name, shape, dt))
        ps = lambda name, shape, dt=F32: ctx.enter_context(nc.psum_tensor(name, shape, dt))
        sem = lambda name: ctx.enter_context(nc.semaphore(name))
        xt = sb("c_x", [P, JT, D])
        hh = sb("c_h_hi", [P, D], F16)
        hl = sb("c_h_lo", [P, D], F16)
        ht = sb("c_hT", [P, 2, KB, TB], F16)
        ident16 = sb("c_ident16", [P, P], F16)
        ss = sb("c_ss", [P, JT])
        rs = sb("c_rs", [P, JT])
        rt = sb("c_rt", [P, JT])
        G = sb("c_glu", [P, NP, HALO + TB])
        acc = sb("c_acc", [P, 2, NP, TB])
        odd = sb("c_acc_odd", [P, TB])
        sz = sb("c_silu_z", [P, 2, NP, TB])
        sq = sb("c_sq", [P, 2, TB])
        tn = sb("c_tanh_n", [P, 2, TB])
        wcv = sb("c_w", [P, NP, TAPS])
        cols = sb("c_cols", [P, 3, NP])
        half = sb("c_half", [P, 3])
        tp = [ps(f"c_tp{b}", [P, KB, P], F16) for b in range(2)]
        pj = [ps(f"c_pj{b}", [P, TB]) for b in range(2)]
        pz = [ps(f"c_pz{b}", [P, TB]) for b in range(2)]
        pmean, pvar = ps("c_mean", [P, TB]), ps("c_var", [P, TB])
        c_loaded = sem("c_const_loaded")
        x_loaded = sem("c_x_loaded")
        ss_ready = sem("c_ss_ready")
        rs_ready = sem("c_rs_ready")
        hi_ready = sem("c_hi_ready")
        lo_ready = sem("c_lo_ready")
        tp_filled, tp_drained = sem("c_tp_filled"), sem("c_tp_drained")
        ht_stored = sem("c_hT_stored")
        pj_filled = sem("c_pj_filled")
        gate_ready = sem("c_gate_ready")
        glu_ready = sem("c_glu_ready")
        tz_ready = sem("c_tz_ready")
        sz_ready = sem("c_sz_ready")
        acc_ready = sem("c_acc_ready")
        halo_kept = sem("c_halo_kept")
        mean_filled = sem("c_mean_filled")
        cen_ready = sem("c_centred")
        sq_ready = sem("c_sq_ready")
        sq_used = sem("c_sq_used")
        std_ready = sem("c_std_ready")
        n_ready = sem("c_norm_ready")
        aff_ready = sem("c_affine_ready")
        tn_ready = sem("c_tanh_n_ready")
        y_ready, y_stored = sem("c_y_ready"), sem("c_y_stored")
        vch = sem("c_vchain")
        ech = sem("c_echain")
        setup = sem("c_setup")
        block = ctx.enter_context(nc.Block())
        x_v = x[0].rearrange("(n j p) d -> n p j d", p=P, j=JT)

        def unit_filled(i, kind, b):
            return CREDIT + i * 3 * NP + UNIT_ORDER.index((kind, b)) + 1

        def run(engine, step, first, last):
            first()
            step(0, 0, False, True)
            with engine.Fori(0, (NB - 2) // 2) as k:
                step(k * 2 + 1, 1, True, True)
                step(k * 2 + 2, 0, True, True)
            step(NB - 1, 1, True, False)
            last(NB, 0)

        @block.sync
        def _(sp):
            for credited in (ss_ready, rs_ready, hi_ready, lo_ready, tp_filled, tp_drained, ht_stored, pj_filled,
                             gate_ready, glu_ready, tz_ready, sz_ready, acc_ready, halo_kept, mean_filled, cen_ready,
                             sq_ready, sq_used, std_ready, n_ready, aff_ready, tn_ready, y_ready, y_stored):
                sp.sem_inc(credited, CREDIT)
            load_shapes(sp, c_loaded)
            with nc.allow_non_contiguous_dma("small constants"):
                for b in range(NP):
                    sp.dma_start(wcv[:, b, :], dw_w[0, :, b * P:(b + 1) * P].rearrange("t p -> p t")).then_inc(c_loaded, 16)
                for k, c in enumerate((dw_b, ln_g, ln_b)):
                    sp.dma_start(cols[:, k, :], c.rearrange("a (b p) -> p (a b)", p=P)).then_inc(c_loaded, 16)

            def first():
                sp.dma_start(xt[:], x_v[0]).then_inc(x_loaded, 16)

            def store_y(i, buf):
                sp.wait_ge(y_ready, CREDIT + i * NP)
                sp.dma_start(y_dram[:, bass.ds((i - 1) * TB, TB)].rearrange("(b p) t -> p b t", p=P),
                             acc[:, 1 - buf]).then_inc(y_stored, 16)

            def step(i, buf, has_last, has_next):
                sp.wait_ge(tp_drained, CREDIT + i * 8 + 8)
                for b in range(TB // RB):
                    sp.dma_start(ht_dram[i * (TB // RB) + b], ht[:, :, :, b * RB:(b + 1) * RB]).then_inc(ht_stored, 16)
                if has_next:
                    sp.wait_ge(lo_ready, CREDIT + i * JT + JT)
                    sp.wait_ge(hi_ready, CREDIT + i * JT + JT)
                    sp.dma_start(xt[:], x_v[i + 1]).then_inc(x_loaded, 16)
                if has_last:
                    store_y(i, buf)

            run(sp, step, first, store_y)
            sp.wait_ge(y_stored, CREDIT + NB * 16)
            sp.wait_ge(ht_stored, CREDIT + NB * 32)

        @block.scalar
        def _(act):
            ch = Chain(act, ech)
            act.wait_ge(setup, 2)

            def squares(i):
                act.wait_ge(x_loaded, i * 16 + 16)
                act.wait_ge(tp_filled, CREDIT + i * 8)
                for j in range(JT):
                    last = act.activation(hh[:], xt[:, j, :], ACT.Square, accum_out=ss[:, j:j + 1])
                    if j < JT - 1:
                        ch.link(last)
                last.then_inc(ss_ready, 1)
                ch.restart()
                act.wait_ge(ss_ready, CREDIT + i + 1)

            def high(i, j):
                if j == 0:
                    act.wait_ge(rs_ready, CREDIT + i + 1)
                act.wait_ge(tp_filled, CREDIT + (i * 8 + 2 * j - 1 if j else i * 8))
                if j:
                    act.wait_ge(lo_ready, CREDIT + i * JT + j)
                act.activation(hh[:], xt[:, j, :], ACT.Copy, scale=rs[:, j:j + 1]).then_inc(hi_ready, 1)

            def parts(i):
                act.wait_ge(ht_stored, CREDIT + i * 32)
                act.wait_ge(pj_filled, CREDIT + i * 12)
                for j in range(JT):
                    for part in range(2):
                        act.wait_ge(tp_filled, CREDIT + i * 8 + 2 * j + part + 1)
                        act.activation(ht[:, part, :, j * P:(j + 1) * P], tp[part][:], ACT.Copy).then_inc(tp_drained, 1)
                        if part == 0 and j < JT - 1:
                            high(i, j + 1)

            def first():
                squares(0)
                high(0, 0)
                parts(0)

            def variance(i, buf):
                for q in range(NP):
                    act.wait_ge(cen_ready, CREDIT + (i - 1) * NP + q + 1)
                    act.wait_ge(sq_used, CREDIT + ((i - 1) * NP + q - 1 if q else (i - 1) * NP))
                    act.activation(sq[:, q % 2, :], acc[:, 1 - buf, q, :], ACT.Square).then_inc(sq_ready, 1)
                act.wait_ge(sq_used, CREDIT + i * NP)
                act.activation(pvar[:], pvar[:], ACT.Sqrt, bias=half[:, 2:3]).then_inc(std_ready, 1)

            def affine(i, buf):
                for q in range(NP):
                    a = acc[:, 1 - buf, q, :]
                    act.wait_ge(n_ready, CREDIT + (i - 1) * NP + q + 1)
                    act.activation(a, a, ACT.Identity, scale=cols[:, 1, q:q + 1], bias=cols[:, 2, q:q + 1]).then_inc(aff_ready, 1)

            def gates(i, buf):
                for q in range(NP):
                    act.wait_ge(aff_ready, CREDIT + (i - 1) * NP + q + 1)
                    act.wait_ge(y_ready, CREDIT + ((i - 1) * NP + q - 1 if q else (i - 1) * NP))
                    act.activation(tn[:, q % 2, :], acc[:, 1 - buf, q, :], ACT.Tanh, scale=0.5).then_inc(tn_ready, 1)

            def step(i, buf, has_last, has_next):
                for kind, b in UNIT_ORDER:
                    if kind == "gate":
                        act.wait_ge(pj_filled, unit_filled(i, kind, b))
                        act.wait_ge(halo_kept, CREDIT + i * NP + b)
                        act.activation(G[:, b, HALO:], pj[0][:], ACT.Tanh, scale=half[:, 0:1]).then_inc(gate_ready, 1)
                        if b == 3 and has_next:
                            high(i + 1, 0)
                        if b == 3 and has_last:
                            gates(i, buf)
                    if kind == "z":
                        act.wait_ge(pj_filled, unit_filled(i, kind, b))
                        act.activation(sz[:, buf, b, :], pz[b % 2][:], ACT.Tanh, scale=half[:, 0:1]).then_inc(tz_ready, 1)
                        if b == 0 and has_last:
                            variance(i, buf)
                        if b == 1 and has_last:
                            affine(i, buf)
                        if b == 1 and has_next:
                            squares(i + 1)
                if has_next:
                    parts(i + 1)

            def last(i, buf):
                variance(i, buf)
                affine(i, buf)
                gates(i, buf)

            run(act, step, first, last)

        @block.vector
        def _(v):
            ch = Chain(v, vch)
            v.wait_ge(c_loaded, 16 * (NP + 3 + len(CONV_CONSTS)))
            ch.link(v.tensor_copy(ident16[:], cst("ident")))
            ch.link(v.tensor_scalar(half[:, 0:1], unscale, 0.5, None, ALU.mult))
            ch.link(v.tensor_scalar(half[:, 1:2], unscale, 0.25, None, ALU.mult))
            ch.link(v.memset(half[:, 2:3], LN_EPS))
            v.tensor_scalar(wcv[:], wcv[:], half[:, 0:1], None, ALU.mult).then_inc(setup, 1)
            v.memset(G[:], 0.0).then_inc(setup, 1)
            v.wait_ge(setup, 2)
            ch.restart()

            def scales(i):
                v.wait_ge(ss_ready, CREDIT + i + 1)
                v.wait_ge(hi_ready, CREDIT + i * JT)
                ch.link(v.tensor_scalar(rt[:], ss[:], 1.0 / D, RMS_EPS, ALU.mult, ALU.add))
                rsqrt_small(v, ch, rt[:], rs[:], ss[:])
                v.tensor_scalar(rs[:], rs[:], H_SCALE, None, ALU.mult).then_inc(rs_ready, 1)

            def low(i, j):
                v.wait_ge(hi_ready, CREDIT + i * JT + j + 1)
                v.wait_ge(tp_filled, CREDIT + i * 8 + 2 * j)
                v.scalar_tensor_tensor(hl[:], xt[:, j, :], rs[:, j:j + 1], hh[:], ALU.mult,
                                       ALU.subtract).then_inc(lo_ready, 1)

            def first():
                scales(0)
                for j in range(JT):
                    low(0, j)
                ch.restart()

            def centre(i, buf):
                v.wait_ge(mean_filled, CREDIT + i)
                for q in range(NP):
                    a = acc[:, 1 - buf, q, :]
                    v.tensor_tensor(a, a, pmean[:], ALU.subtract).then_inc(cen_ready, 1)

            def normalise(i, buf):
                v.wait_ge(std_ready, CREDIT + i)
                ch.link(v.reciprocal(pvar[:], pvar[:]))
                for q in range(NP):
                    a = acc[:, 1 - buf, q, :]
                    v.wait_ge(sq_ready, CREDIT + (i - 1) * NP + q + 1)
                    v.tensor_tensor(a, a, pvar[:], ALU.mult).then_inc(n_ready, 1)

            def gated(i, buf):
                for q in range(NP):
                    v.wait_ge(tn_ready, CREDIT + (i - 1) * NP + q + 1)
                    tq, a = tn[:, q % 2, :], acc[:, 1 - buf, q, :]
                    ch.link(v.scalar_tensor_tensor(tq, tq, 1.0, a, ALU.add, ALU.mult))
                    v.scalar_tensor_tensor(a, tq, half[:, 1:2], sz[:, 1 - buf, q, :], ALU.mult, ALU.mult).then_inc(y_ready, 1)

            def step(i, buf, has_last, has_next):
                for b in range(NP):
                    g = G[:, b, HALO:]
                    v.wait_ge(pj_filled, unit_filled(i, "value", b))
                    v.wait_ge(gate_ready, CREDIT + i * NP + b + 1)
                    v.scalar_tensor_tensor(g, g, 1.0, pj[1][:], ALU.add, ALU.mult).then_inc(glu_ready, 1)
                    if b == 0 and has_last:
                        v.wait_ge(y_stored, CREDIT + (i - 1) * 16)
                    v.wait_ge(glu_ready, CREDIT + i * NP + b + 1)
                    a = acc[:, buf, b, :]
                    marks = [ch.mark(v.tensor_scalar(a, G[:, b, 0:TB], wcv[:, b, 0:1], cols[:, 0, b:b + 1],
                                                     ALU.mult, ALU.add)),
                             ch.mark(v.tensor_scalar(odd[:], G[:, b, 1:1 + TB], wcv[:, b, 1:2], None, ALU.mult))]
                    for t in range(2, TAPS):
                        o = a if t % 2 == 0 else odd[:]
                        ch.wait(marks[t % 2])
                        marks[t % 2] = ch.mark(v.scalar_tensor_tensor(o, G[:, b, t:t + TB], wcv[:, b, t:t + 1], o,
                                                                      ALU.mult, ALU.add))
                        if b == NP - 2 and has_next and t == TAPS // 2:
                            scales(i + 1)
                        if b == NP - 1 and has_next and t % 4 == 2 and t // 4 < JT:
                            low(i + 1, t // 4)
                    ch.wait(max(marks))
                    v.tensor_tensor(a, a, odd[:], ALU.add).then_inc(acc_ready, 1)
                    v.wait_ge(acc_ready, CREDIT + i * NP + b + 1)
                    v.tensor_copy(G[:, b, 0:HALO], G[:, b, TB:TB + HALO]).then_inc(halo_kept, 1)
                    ch.restart()
                    if has_last:
                        (centre, normalise, gated, lambda *_: None)[b](i, buf)
                    v.wait_ge(tz_ready, CREDIT + i * NP + b + 1)
                    z = sz[:, buf, b, :]
                    v.scalar_tensor_tensor(z, z, 1.0, pz[b % 2][:], ALU.add, ALU.mult).then_inc(sz_ready, 1)
                ch.restart()

            def last(i, buf):
                centre(i, buf)
                normalise(i, buf)
                gated(i, buf)

            run(v, step, first, last)

        @block.tensor
        def _(pe):
            pe.wait_ge(setup, 2)

            def transposes(i):
                for j in range(JT):
                    for part, (ready, src) in enumerate(((hi_ready, hh), (lo_ready, hl))):
                        pe.wait_ge(ready, CREDIT + i * JT + j + 1)
                        pe.wait_ge(tp_drained, CREDIT + (i * 8 + 2 * j + part - 1 if j else i * 8))
                        for kb in range(KB):
                            last = pe.transpose(tp[part][:, kb, :], src[:, kb * P:(kb + 1) * P], ident16[:])
                        last.then_inc(tp_filled, 1)

            def mean(i, buf):
                pe.wait_ge(acc_ready, CREDIT + i * NP)
                for q in range(NP):
                    last = pe.matmul(pmean[:], cst("mean"), acc[:, 1 - buf, q, :], start=q == 0, stop=q == NP - 1)
                last.then_inc(mean_filled, 1)

            def variance(i):
                for q in range(NP):
                    pe.wait_ge(sq_ready, CREDIT + (i - 1) * NP + q + 1)
                    pe.matmul(pvar[:], cst("mean"), sq[:, q % 2, :], start=q == 0, stop=q == NP - 1).then_inc(sq_used, 1)

            def step(i, buf, has_last, has_next):
                pe.wait_ge(tp_drained, CREDIT + i * 8 + 8)
                for kind, b in UNIT_ORDER:
                    n = ("value", "gate", "z").index(kind)
                    if kind != "z":
                        pe.wait_ge(glu_ready, CREDIT + i * NP + b)
                    elif b or not isinstance(i, int) or i:
                        pe.wait_ge(sz_ready, CREDIT + i * NP + b - 1)
                    out = {"value": pj[1], "gate": pj[0], "z": pz[b % 2]}[kind]
                    project(pe, out[:], whi, wlo, (ht[:, 0], ht[:, 1]), n * NP + b).then_inc(pj_filled, 1)
                    if (kind, b) == ("value", 0) and has_last:
                        mean(i, buf)
                    if (kind, b) == ("z", 0) and has_last:
                        variance(i)
                if has_next:
                    transposes(i + 1)

            def last(i, buf):
                mean(i, buf)
                variance(i)

            run(pe, step, lambda: transposes(0), last)


def project_steps(pe, out, whi, wlo, ht, unit):
    cols = slice(unit * P, (unit + 1) * P)
    for kb in range(KB):
        for n, (w, part) in enumerate(((whi, 0), (whi, 1), (wlo, 0))):
            yield pe.matmul(out, w[:, kb, cols], ht[part][:, kb, :], start=kb == 0 and n == 0,
                            stop=kb == KB - 1 and n == 2)


def project(pe, out, whi, wlo, ht, unit):
    for last in project_steps(pe, out, whi, wlo, ht, unit):
        pass
    return last


def tile_uses():
    uses = [("lora_w", 1), ("lora_a", 1), ("kk_sum", 1), ("cum", 1), ("kk_scale", 1), ("bonus", 1),
            ("avT0", 2), ("avT1", 2), ("bkT0", 1), ("bkT1", 1), ("aa0", 1), ("aa1", 1), ("aa2", 1), ("aa3", 1),
            ("ut0", 1), ("ut1", 1)]
    for b in LEVELS:
        uses += [(f"q{b}_{g}", 2) for g in range(2)] + [(f"d{b}_{g}", 1) for g in range(2)]
        if b != LEVELS[-1]:
            uses += [(f"t{b}_{g}", 1) for g in range(2)]
    uses += [("akv", 1), ("x0", 2), ("x1", 2), ("rm0", 1), ("rm1", 1), ("sy0_0", 2), ("sy0_1", 2), ("sy1_0", 2), ("sy1_1", 2),
             ("yT", 1)]
    return uses


USES = tile_uses()
ORDER = {name: n for n, (name, _) in enumerate(USES)}
RING = 6
PER_BANK = [len(USES[b::RING]) for b in range(RING)]
DRAINS = [sum(d for n, (_, d) in enumerate(USES) if n % RING == b) for b in range(RING)]
GROUP_NORM = ("norm0", "norm1", "norm2")


def fill_plan():
    shares = {"lora_w": 0, "lora_a": 6, "kk_sum": 14, "cum": 16, "kk_scale": 12, "bonus": 18, "bkT": 4, "avT": 5, "aa": 6,
              "ut": 5, "q": 1.5, "d": 1.5, "t": 1.5, "akv": 3, "x": 7, "rm": 4, "sy": 4, "norm": 30, "yT": 0}
    points = [name for name, _ in USES[:-1]] + list(GROUP_NORM) + [USES[-1][0]]
    kind = lambda name: name if name in shares else name.rstrip("0123456789_")
    return [(name, shares[kind(name)]) for name in points]


FILL = fill_plan()
LORA_AT = (NU - 1) // RJ


def unit_at(o):
    return o if o < LORA_AT else NU - 1 if o == LORA_AT else o - 1


def units_of(j):
    return list(range(0, LORA_AT) if j == 0 else range(LORA_AT, NU))


def steps_due(j, name):
    total, share, by_then = len(units_of(j)) * 24, sum(w for _, w in FILL), 0
    for point, w in FILL:
        by_then += w
        if point == name:
            return math.ceil(total * by_then / share - 1e-9)


class Tile:

    def __init__(self, i, j, filled, drained):
        self.i, self.j, self.filled_sems, self.drained_sems = i, j, filled, drained

    def count(self, per_tile, k):
        return self.i * (RJ * per_tile) + (self.j * per_tile + k)

    def before_fill(self, eng, name):
        n = ORDER[name]
        b = n % RING
        eng.wait_ge(self.drained_sems[b], CREDIT + self.count(DRAINS[b], sum(d for _, d in USES[b:n:RING])))

    def filled(self, ins, name):
        ins.then_inc(self.filled_sems[ORDER[name] % RING], 1)

    def wait_filled(self, eng, name):
        n = ORDER[name]
        eng.wait_ge(self.filled_sems[n % RING], CREDIT + self.count(PER_BANK[n % RING], n // RING + 1))

    def drained(self, ins, name):
        ins.then_inc(self.drained_sems[ORDER[name] % RING], 1)

    def wait_drained(self, eng, name):
        n = ORDER[name]
        b = n % RING
        eng.wait_ge(self.drained_sems[b], CREDIT + self.count(DRAINS[b], sum(d for _, d in USES[b:n + 1:RING])))


RWKV_CONSTS = ["ident", "tri", "pair0", "mask_r", "mask_a", "heads", "sel2"] + [f"level{b}" for b in LEVELS]


def rwkv_phase(nc, shapes, inp, whi, wlo, unscale, ht_dram, y_dram):
    cst, load_shapes = shapes
    with ExitStack() as ctx:
        sb = lambda name, shape, dt=F32: ctx.enter_context(nc.sbuf_tensor(name, shape, dt))
        ps = lambda name, shape, dt=F32: ctx.enter_context(nc.psum_tensor(name, shape, dt))
        sem = lambda name: ctx.enter_context(nc.semaphore(name))
        ht = sb("r_hT", [P, 4, KB, RB], F16)
        raw = sb("r_raw", [P, 2, RB + 1])
        keep = sb("r_keep", [P, 2, RB])
        carry = sb("r_carry", [P, NU])
        mix = sb("r_mix", [P, NU - 1, 2 * RB])
        lora = sb("r_lora", [P, RB])
        rn = sb("r_rn", [P, 3, NH])
        rnb = sb("r_rnb", [P, NH, HD])
        W = sb("r_W", [P, NP * 2, CH + 1])
        Wi = sb("r_Winv", [P, NP * 2, CH])
        bonv = sb("r_bonus", [P, NP, TT])
        BK = sb("r_BK", [P, NP * 2, 2 * CH])
        RAV = sb("r_RAV", [P, NP * 2, 3 * CH])
        FB = sb("r_FB", [P, 2, NP, 4 * HD])
        AkT = sb("r_AkT", [P, 2, NH, CH])
        XA = sb("r_XA", [P, NH, 2 * HD])
        XG = sb("r_XG", [P, 2, NH, 2 * HD])
        LT = sb("r_LT", [P, NH, TT])
        U = sb("r_U", [P, NH, TT])
        UT = sb("r_UT", [P, NH, TT])
        Q = sb("r_Q", [P, NH, TT])
        la, kk = UT[:, 0:NP, :], UT[:, NP:, :]
        km, sq = U[:, 0:NP, :], U[:, NP:, :]
        t1 = yg = Q[:, 0:NP, :]
        lw = Q[:, NP:, :].rearrange("p a t -> p (a t)")
        RM = sb("r_RM", [P, 2, NP, 2 * HD])
        S = sb("r_S", [P, NP, HD])
        Y = sb("r_Y", [P, NP, 2, HD])
        sz = sb("r_sz", [P, NP, TT])
        yo = sb("r_yo", [P, 2, NP, TT])
        w0b = sb("r_w0", [P, DR])
        lup = sb("r_lora_up", [P, DR])
        rk1 = sb("r_rk_ones", [P, NP, P])
        vec = sb("r_vec", [P, 6, NP])
        omk = sb("r_1_k_a", [P, NP])
        zero = sb("r_zero", [P, 1])
        mu = sb("r_mu", [P, NU])
        mq = sb("r_1_mu", [P, NU])
        pj = [ps(f"r_pj{b}", [P, RB]) for b in range(2)]
        bank = [ps(f"r_bank{b}", [P, 512]) for b in range(RING)]
        filled = [sem(f"r_filled{b}") for b in range(RING)]
        drained = [sem(f"r_drained{b}") for b in range(RING)]
        c_loaded, ht_loaded = sem("r_const_loaded"), sem("r_hT_loaded")
        pj_filled = [sem(f"r_pj_filled{b}") for b in range(2)]
        pj_drained = [sem(f"r_pj_drained{b}") for b in range(2)]
        shifted = sem("r_shifted")
        lora_ready = sem("r_lora_ready")
        tw_ready, ta_ready = sem("r_tanh_w"), sem("r_tanh_a")
        sq_ready = sem("r_sq_ready")
        ld_ready, rk_ready = sem("r_decay_ready"), sem("r_rk_ready")
        aw_ready, bk_ready, rw_ready = sem("r_aW_ready"), sem("r_bk_ready"), sem("r_rW_ready")
        ui_ready, v_ready = sem("r_ui_ready"), sem("r_v_ready")
        ut_ready = sem("r_ut_ready")
        yc_ready, yq_ready, yn_ready = sem("r_y_centred"), sem("r_y_squared"), sem("r_y_normed")
        tz_ready = sem("r_tanh_z")
        y_ready = sem("r_y_ready")
        y_stored = [sem(f"r_y_stored{b}") for b in range(2)]
        vch, ech, setup = sem("r_vchain"), sem("r_echain"), sem("r_setup")
        passed = sem("r_passed")
        block = ctx.enter_context(nc.Block())
        y_v = y_dram.rearrange("(b p) t -> p b t", p=P)

        def pj_count(n, o):
            b = o % 2
            return n * ((NU + 1 - b) // 2) + o // 2

        def heads4(name):
            return bank[ORDER[name] % RING][:].rearrange("p (h t) -> p h t", h=4)

        def heads8(name):
            return bank[ORDER[name] % RING][:].rearrange("p (h t) -> p h t", h=8)

        def flat(name):
            return bank[ORDER[name] % RING][:]

        def chunks(name):
            return bank[ORDER[name] % RING][:].rearrange("p (c t) -> p c t", t=CH)

        def halves(name, b):
            return bank[ORDER[name] % RING][:].rearrange("p (x h n t) -> p x h n t", x=2, h=4, t=b)

        def block_cols(a, g, b, odd):
            return a[:, 4 * g:4 * g + 4, :].rearrange("p h (n two t) -> p h two n t", two=2, t=b)[:, :, odd]

        def bc(col, n):
            return col.unsqueeze(2).to_broadcast([P, col.shape[1], n])

        def by_pair(a):
            return a.rearrange("p (g a) d -> p a g d", g=2)

        def part(group, i, j):
            return mix[:, group * NP:(group + 1) * NP, bass.ds((i % 2) * RB + j * TT, TT)]

        @block.sync
        def _(sp):
            for credited in (*filled, *drained, *pj_filled, *pj_drained, *y_stored, shifted, lora_ready, tw_ready,
                             ta_ready, sq_ready, ld_ready, rk_ready, aw_ready, bk_ready, rw_ready, ui_ready, v_ready, ut_ready,
                             yc_ready, yq_ready, yn_ready, tz_ready, y_ready):
                sp.sem_inc(credited, CREDIT)
            sp.dma_start(ht[:, 0:2], ht_dram[0]).then_inc(ht_loaded, 16)
            with nc.allow_non_contiguous_dma("small constants"):
                for k, name in enumerate(("a0", "k_k", "k_a", "r_k", "gn_g", "gn_b")):
                    src = inp[name].rearrange("a h d -> a (h d)") if name == "r_k" else inp[name]
                    sp.dma_start(vec[:, k, :], src.rearrange("a (b p) -> p (a b)", p=P)).then_inc(c_loaded, 16)
                sp.dma_start(mu[:], inp["mu_shift"].rearrange("a (b p) -> p (a b)", p=P)).then_inc(c_loaded, 16)
                sp.dma_start(w0b[:], inp["w0"][0:1, :].to_broadcast([P, DR])).then_inc(c_loaded, 16)
            sp.dma_start(lup[0:LORA, :], inp["w_up"][0]).then_inc(c_loaded, 16)
            sp.dma_start(lup[LORA:P, :], inp["a_up"][0]).then_inc(c_loaded, 16)
            load_shapes(sp, c_loaded)
            sp.wait_ge(ht_loaded, 16)
            sp.dma_start(ht[:, 2:4], ht_dram[1]).then_inc(ht_loaded, 16)

            def stores(i):
                for j in range(RJ):
                    sp.wait_ge(y_ready, CREDIT + i * RJ + j + 1)
                    sp.dma_start(y_v[:, 0:NP, bass.ds(i * RB + j * TT, TT)], yo[:, j]).then_inc(y_stored[j], 16)

            with sp.Fori(0, NRB - 2) as i:
                sp.wait_ge(pj_filled[0], CREDIT + pj_count(i, NU - 1) + 1)
                sp.wait_ge(ht_loaded, i * 16 + 32)
                sp.dma_start(ht[:, bass.ds((i % 2) * 2, 2)], ht_dram[i + 2]).then_inc(ht_loaded, 16)
                stores(i)
            for n in (NRB - 2, NRB - 1):
                stores(n)
            for j in range(RJ):
                sp.wait_ge(y_stored[j], CREDIT + NRB * 16)

        @block.scalar
        def _(act):
            ch = Chain(act, ech)

            def drain_unit(n, o):
                b, u = o % 2, unit_at(o)
                act.wait_ge(shifted, CREDIT + (n * NU + o - 1 if o else n * NU))
                act.activation(raw[:, b, 0:1], carry[:, u:u + 1], ACT.Copy)
                act.wait_ge(pj_filled[b], CREDIT + pj_count(n, o) + 1)
                act.activation(raw[:, b, 1:], pj[b][:], ACT.Copy, scale=unscale)
                act.activation(keep[:, b, :], pj[b][:], ACT.Copy, scale=mq[:, u:u + 1]).then_inc(pj_drained[b], 1)

            def lora_tanh(n):
                act.wait_ge(shifted, CREDIT + n * NU + LORA_AT + 1)
                act.activation(lora[0:LORA, :], lora[0:LORA, :], ACT.Tanh).then_inc(lora_ready, 1)

            def squares(i, j):
                for p in range(NP):
                    last = act.activation(sq[:, p, :], part(1, i, j)[:, p, :], ACT.Square, scale=vec[:, 1, p:p + 1])
                last.then_inc(sq_ready, 1)

            def tile(i, j, beside):
                t = Tile(i, j, filled, drained)
                todo = units_of(j) if beside else []
                taken = [0]

                def hook(name):
                    while taken[0] < len(todo) and steps_due(j, name) >= 24 * (taken[0] + 1):
                        o = todo[taken[0]]
                        drain_unit(i + 1, o)
                        if o == LORA_AT + 1:
                            lora_tanh(i + 1)
                        taken[0] += 1

                act.wait_ge(shifted, CREDIT + i * NU + NU)
                t.wait_drained(act, "lora_w")
                act.activation(lw[:], lw[:], ACT.Tanh, scale=0.5).then_inc(tw_ready, 1)
                t.wait_filled(act, "lora_a")
                for p in range(NP):
                    last = act.activation(la[:, p, :], heads4("lora_a")[:, p, :], ACT.Tanh, scale=0.5,
                                          bias=vec[:, 0, p:p + 1])
                    if p == 0:
                        act.wait_ge(tw_ready, CREDIT + t.count(1, 1))
                        act.activation(lw[:], lw[:], ACT.Copy, scale=-KAPPA / 2, bias=-KAPPA / 2).then_inc(ld_ready, 1)
                t.drained(last, "lora_a")
                t.wait_drained(act, "lora_a")
                act.wait_ge(y_ready, CREDIT + t.count(1, 0))
                for p in range(NP):
                    last = act.activation(t1[:, p, :], la[:, p, :], ACT.Identity, scale=vec[:, 2, p:p + 1],
                                          bias=omk[:, p:p + 1])
                last.then_inc(ta_ready, 1)
                act.wait_ge(ta_ready, CREDIT + t.count(2, 1))
                act.activation(la[:], la[:], ACT.Copy, scale=0.5, bias=0.5).then_inc(ta_ready, 1)
                act.activation(RAV[:, :, 2 * CH:].rearrange("p (a c) t -> p a c t", c=2),
                               part(2, i, j).rearrange("p a (c t) -> p a c t", c=2), ACT.Copy).then_inc(v_ready, 1)
                t.wait_filled(act, "cum")
                act.activation(W[:, :, 1:], chunks("cum"), ACT.Exp)
                t.drained(act.activation(Wi[:], chunks("cum"), ACT.Exp, scale=-1.0), "cum")
                act.activation(sz[:], part(3, i, j), ACT.Tanh, scale=0.5).then_inc(tz_ready, 1)
                hook("bonus")
                for c in range(2):
                    t.wait_filled(act, f"avT{c}")
                    t.drained(act.activation(by_pair(XG[CH:, c, :, HD:]),
                                             heads4(f"avT{c}")[CH:].rearrange("p a (g d) -> p a g d", g=2), ACT.Copy), f"avT{c}")
                for c in range(2):
                    t.wait_filled(act, f"bkT{c}")
                    src = heads4(f"bkT{c}").rearrange("p a (h d) -> p a h d", h=2)
                    t.drained(act.activation(FB[:, c].rearrange("p a (h d) -> p a h d", h=4)[:, :, 0:4:3, :], src,
                                             ACT.Copy), f"bkT{c}")
                for g in range(2):
                    last = act.activation(block_cols(UT, g, 1, 0), cst("ident").rearrange("p (n two) -> p two n", two=2)
                                          [:, 0].unsqueeze(1).unsqueeze(3).to_broadcast([P, 4, CH, 1]), ACT.Copy)
                last.then_inc(ui_ready, 1)
                hook("aa3")
                for g in range(2):
                    t.wait_filled(act, f"ut{g}")
                    t.drained(act.activation(U[:, 4 * g:4 * g + 4, :], heads4(f"ut{g}"), ACT.Copy), f"ut{g}")
                for b in LEVELS:
                    for g in range(2):
                        t.wait_filled(act, f"q{b}_{g}")
                        t.drained(act.activation(block_cols(Q, g, b, 1), zero[:, 0:1].unsqueeze(2).unsqueeze(3).to_broadcast(
                            [P, 4, CH // b, b]), ACT.Copy), f"q{b}_{g}")
                    hook(f"d{b}_0")
                    for g in range(2 if b != LEVELS[-1] else 0):
                        t.wait_filled(act, f"t{b}_{g}")
                        t.drained(act.activation(block_cols(U, g, b, 0), block_cols(heads4(f"t{b}_{g}"), 0, b, 0),
                                                 ACT.Copy), f"t{b}_{g}")
                t.wait_filled(act, "akv")
                t.drained(act.activation(XA[:, :, HD:], heads8("akv"), ACT.Copy), "akv")
                for g in range(2):
                    t.wait_filled(act, f"x{g}")
                    t.drained(act.activation(XG[0:CH, 0, 4 * g:4 * g + 4, :], heads4(f"x{g}")[0:CH], ACT.Copy), f"x{g}")
                hook("rm1")
                for c in range(2):
                    for g in range(2):
                        rows = slice((1 - g) * CH, (2 - g) * CH)
                        t.wait_filled(act, f"sy{c}_{g}")
                        t.drained(act.activation(Y[c * CH:(c + 1) * CH, :, g, :], heads8(f"sy{c}_{g}")[rows, 0:NP],
                                                 ACT.Copy), f"sy{c}_{g}")
                hook("sy1_1")
                act.wait_ge(yc_ready, CREDIT + t.count(1, 1))
                act.activation(yg[:], Y[:].rearrange("p a h d -> p a (h d)"), ACT.Square).then_inc(yq_ready, 1)
                hook("norm0")
                if j < RJ - 1:
                    squares(i, j + 1)
                elif beside:
                    act.wait_ge(shifted, CREDIT + (i + 1) * NU + 2 * NP)
                    squares(i + 1, 0)
                for name in GROUP_NORM[1:]:
                    hook(name)
                t.wait_filled(act, "yT")
                for p in range(NP):
                    last = act.activation(yg[:, p, :], heads4("yT")[:, p, :], ACT.Identity, scale=vec[:, 4, p:p + 1],
                                          bias=vec[:, 5, p:p + 1])
                t.drained(last, "yT")
                hook("yT")

            act.wait_ge(setup, 2)
            for o in range(NU):
                drain_unit(0, o)
            lora_tanh(0)
            act.wait_ge(shifted, CREDIT + 2 * NP)
            squares(0, 0)
            with act.Fori(0, NRB - 1) as i:
                for j in range(RJ):
                    tile(i, j, True)
            for j in range(RJ):
                tile(NRB - 1, j, False)

        @block.vector
        def _(v):
            ch = Chain(v, vch)
            MUL, ADD = ALU.mult, ALU.add
            level = {b: cst(f"level{b}") for b in LEVELS}

            def over4(mask):
                return mask.unsqueeze(1).to_broadcast([mask.shape[0], 4, *mask.shape[1:]])

            def odd_cols(name):
                return cst(name).rearrange("p (n two t) -> p two n t", two=2, t=1)[:, 1]

            def shift_unit(n, o):
                b, u = o % 2, unit_at(o)
                v.wait_ge(pj_drained[b], CREDIT + pj_count(n, o) + 1)
                dst = lora[:] if u == NU - 1 else mix[:, u, bass.ds((n % 2) * RB, RB)]
                v.tensor_copy(carry[:, u:u + 1], raw[:, b, RB:])
                v.scalar_tensor_tensor(dst, raw[:, b, 0:RB], mu[:, u:u + 1], keep[:, b, :], MUL,
                                       ADD).then_inc(shifted, 1)

            def gate(i, j, t):
                t.wait_drained(v, "yT")
                ch.link(v.tensor_tensor(yg[:], yg[:], bonv[:], ADD))
                v.wait_ge(y_stored[j], CREDIT + i * 16)
                v.scalar_tensor_tensor(yo[:, j], yg[:], 0.5, sz[:], MUL, MUL).then_inc(y_ready, 1)

            def tile(i, j, beside):
                t = Tile(i, j, filled, drained)
                todo = units_of(j) if beside else []
                taken = [0]

                def hook(name):
                    while taken[0] < len(todo) and steps_due(j, name) >= 24 * (taken[0] + 1):
                        shift_unit(i + 1, todo[taken[0]])
                        taken[0] += 1

                ch.restart()
                r, k, vv, z = (part(g, i, j) for g in range(4))
                v.wait_ge(shifted, CREDIT + i * NU + NU)
                t.wait_filled(v, "lora_w")
                t.drained(v.tensor_tensor(lw[:], flat("lora_w"), w0b[:], ADD), "lora_w")
                if j:
                    gate(i, j - 1, Tile(i, j - 1, filled, drained))
                t.wait_filled(v, "kk_sum")
                m = ch.mark(v.tensor_scalar(rn[:, 0, :], flat("kk_sum")[:, 0:NH], 1e-24, None, ALU.max))
                kk_made = ch.mark(v.tensor_tensor(kk[:], k, bc(vec[:, 1, :], TT), MUL))
                ch.wait(m)
                rsqrt_small(v, ch, rn[:, 0, :], rn[:, 1, :], rn[:, 2, :])
                t.drained(v.tensor_copy(rnb[:], bc(rn[:, 1, :], HD)), "kk_sum")
                v.wait_ge(ta_ready, CREDIT + t.count(2, 1))
                ch.link(v.tensor_tensor(km[:], k, t1[:], MUL))
                v.tensor_tensor(sq[:], r, km[:], MUL).then_inc(rk_ready, 1)
                t.wait_filled(v, "kk_scale")
                ch.wait(kk_made)
                t.drained(v.tensor_tensor(kk[:], kk[:], heads4("kk_scale"), MUL), "kk_scale")
                t.wait_drained(v, "cum")
                as8 = lambda a: a.rearrange("p a (c t) -> p (a c) t", c=2)
                t.wait_drained(v, "kk_scale")
                v.scalar_tensor_tensor(RAV[:, :, CH:2 * CH], as8(kk[:]), -1.0, W[:, :, 0:CH], MUL, MUL).then_inc(aw_ready, 1)
                v.wait_ge(ta_ready, CREDIT + t.count(2, 2))
                m = ch.mark(v.tensor_tensor(la[:], la[:], kk[:], MUL))
                v.tensor_tensor(BK[:, :, CH:], as8(km[:]), Wi[:], MUL)
                ch.wait(m)
                v.tensor_tensor(BK[:, :, 0:CH], as8(la[:]), Wi[:], MUL).then_inc(bk_ready, 1)
                v.tensor_tensor(RAV[:, :, 0:CH].rearrange("p (a c) t -> p a c t", c=2),
                                r.rearrange("p a (c t) -> p a c t", c=2),
                                W[:, :, 1:].rearrange("p (a c) t -> p a c t", c=2), MUL).then_inc(rw_ready, 1)
                hook("kk_scale")
                t.wait_filled(v, "bonus")
                t.drained(v.tensor_tensor(bonv[:], heads4("bonus"), vv, MUL), "bonus")
                hook("bonus")
                for c in range(2):
                    t.wait_filled(v, f"avT{c}")
                    t.drained(v.tensor_copy(by_pair(XA[c * CH:(c + 1) * CH, :, 0:HD]),
                                            heads4(f"avT{c}")[0:CH].rearrange("p a (g d) -> p a g d", g=2)), f"avT{c}")
                v.wait_ge(tz_ready, CREDIT + t.count(1, 1))
                v.scalar_tensor_tensor(sz[:], sz[:], 1.0, z, ADD, MUL)
                for n in range(4):
                    g, c = n // 2, n % 2
                    hs, chunk = slice(4 * g, 4 * g + 4), slice(c * CH, (c + 1) * CH)
                    t.wait_filled(v, f"aa{n}")
                    lt = ch.mark(v.tensor_tensor(LT[chunk, hs, chunk], heads4(f"aa{n}")[0:CH, :, CH:],
                                                 over4(cst("mask_a")[0:CH]), MUL))
                    v.tensor_tensor(FB[:, c, :, (1 + g) * HD:(2 + g) * HD], heads4(f"aa{n}")[:, :, 0:CH],
                                    over4(cst("mask_r")), MUL)
                    t.drained(v.tensor_tensor(AkT[CH:, c, hs, :], heads4(f"aa{n}")[CH:, :, CH:],
                                              over4(cst("mask_a")[CH:]), MUL), f"aa{n}")
                    if c:
                        odd = block_cols(UT, g, 1, 1)
                        ch.wait(lt)
                        ch.link(v.tensor_tensor(odd, block_cols(LT, g, 1, 1), over4(odd_cols("pair0")), MUL))
                        v.tensor_tensor(odd, odd, over4(odd_cols("ident")), ADD).then_inc(ut_ready, 1)
                hook("aa3")
                v.wait_ge(ut_ready, CREDIT + t.count(2, 2))
                for b in LEVELS:
                    for g in range(2):
                        t.wait_filled(v, f"q{b}_{g}")
                        mask = level[b].rearrange("p (n t) -> p n t", t=b).unsqueeze(1).to_broadcast([P, 4, CH // b, b])
                        t.drained(v.tensor_tensor(block_cols(Q, g, b, 0), halves(f"q{b}_{g}", b)[:, 0], mask, MUL),
                                  f"q{b}_{g}")
                    for g in range(2):
                        t.wait_filled(v, f"d{b}_{g}")
                        cols = block_cols(UT, g, b, 1)
                        t.drained(v.tensor_tensor(cols, cols, halves(f"d{b}_{g}", b)[:, 0], ADD), f"d{b}_{g}")
                    hook(f"d{b}_0")
                    t.wait_drained(v, f"d{b}_0")
                    t.wait_drained(v, f"d{b}_1")
                for g in range(2):
                    t.wait_filled(v, f"x{g}")
                    t.drained(v.tensor_copy(XG[0:CH, 1, 4 * g:4 * g + 4, :], heads4(f"x{g}")[CH:]), f"x{g}")
                for c in range(2):
                    t.wait_filled(v, f"rm{c}")
                    rw = RAV[:].rearrange("p (a c) t -> p a c t", c=2)[:, :, c, 0:CH]
                    one = cst("ident")
                    src = heads4(f"rm{c}")
                    v.tensor_tensor(RM[0:HD, c, :, 0:HD], src[0:HD, :, 0:HD], over4(one[0:HD, 0:HD]), ADD)
                    v.tensor_tensor(RM[0:HD, c, :, HD:], src[0:HD, :, HD:], rw[0:HD], ADD)
                    v.tensor_tensor(RM[HD:, c, :, 0:HD], src[HD:, :, 0:HD], rw[HD:], ADD)
                    t.drained(v.tensor_tensor(RM[HD:, c, :, HD:], src[HD:, :, HD:], over4(one[HD:, HD:]), ADD), f"rm{c}")
                hook("rm1")
                for c in range(2):
                    wc = W[:].rearrange("p (a c) t -> p a c t", c=2)[:, :, c, CH:]
                    for g in range(2):
                        rows = slice(g * HD, (g + 1) * HD)
                        t.wait_filled(v, f"sy{c}_{g}")
                        t.drained(v.tensor_tensor(S[rows], heads8(f"sy{c}_{g}")[rows, 0:NP],
                                                  wc[rows].to_broadcast([HD, NP, HD]), MUL), f"sy{c}_{g}")
                t.wait_drained(v, "sy1_0")
                t.wait_drained(v, "sy1_1")
                y8 = Y[:].rearrange("p a h d -> p (a h) d")
                ch.link(v.tensor_reduce(rn[:, 0, :], y8, AX, ADD))
                v.scalar_tensor_tensor(y8, bc(rn[:, 0, :], HD), -1.0 / HD, y8, MUL, ADD).then_inc(yc_ready, 1)
                v.wait_ge(yq_ready, CREDIT + t.count(1, 1))
                ch.link(v.tensor_reduce(rn[:, 0, :], yg[:].rearrange("p a (h d) -> p (a h) d", h=2), AX, ADD))
                ch.link(v.tensor_scalar(rn[:, 0, :], rn[:, 0, :], 1.0 / HD, GN_EPS, MUL, ADD))
                hook("norm0")
                rsqrt_small(v, ch, rn[:, 0, :], rn[:, 1, :], rn[:, 2, :])
                hook("norm1")
                v.tensor_tensor(y8, y8, bc(rn[:, 1, :], HD), MUL).then_inc(yn_ready, 1)
                hook("norm2")
                if j == RJ - 1:
                    gate(i, j, t)
                hook("yT")

            v.memset(S[:], 0.0)
            v.memset(carry[:], 0.0)
            v.memset(LT[:], 0.0)
            v.memset(zero[:], 0.0)
            v.memset(W[:], 1.0).then_inc(setup, 1)
            v.wait_ge(c_loaded, 16 * (10 + len(RWKV_CONSTS)))
            ch.link(v.tensor_scalar(mq[:], mu[:], -1.0, 1.0, MUL, ADD))
            ch.link(v.tensor_scalar(vec[:, 2, :], vec[:, 2, :], 0.5, None, MUL))
            ch.link(v.tensor_scalar(omk[:], vec[:, 2, :], -1.0, 1.0, MUL, ADD))
            ch.link(v.tensor_scalar(vec[:, 0, :], vec[:, 0, :], 0.5, None, MUL))
            for p in range(NP):
                last = v.tensor_scalar(rk1[:, p, :], cst("heads"), vec[:, 3, p:p + 1], None, MUL)
            ch.link(last)
            v.tensor_scalar(mq[:], mq[:], unscale, None, MUL).then_inc(setup, 1)
            v.wait_ge(setup, 2)
            for o in range(NU):
                shift_unit(0, o)
            ch.restart()
            with v.Fori(0, NRB - 1) as i:
                for j in range(RJ):
                    tile(i, j, True)
                ch.restart()
            for j in range(RJ):
                tile(NRB - 1, j, False)

        @block.tensor
        def _(pe):
            ident = cst("ident")

            def unit_steps(n, o):
                b, u = o % 2, unit_at(o)
                block_ht = [ht[:, bass.ds((n % 2) * 2 + part, 1)].rearrange("p a k t -> p (a k) t") for part in range(2)]
                pe.wait_ge(pj_drained[b], CREDIT + pj_count(n, o))
                if o == 0:
                    pe.wait_ge(ht_loaded, n * 16 + 16)
                for k, last in enumerate(project_steps(pe, pj[b][:], whi, wlo, block_ht, u)):
                    if k == 23:
                        last.then_inc(pj_filled[b], 1)
                    yield

            def tile(i, j, beside):
                t = Tile(i, j, filled, drained)
                steps = (s for u in (units_of(j) if beside else []) for s in unit_steps(i + 1, u))
                issued = [0]

                def end(name, last):
                    t.filled(last, name)
                    fill(name)

                def fill(name):
                    while issued[0] < steps_due(j, name) and beside:
                        next(steps)
                        issued[0] += 1

                ts = slice(j * TT, (j + 1) * TT)
                pe.wait_ge(lora_ready, CREDIT + i + 1)
                t.before_fill(pe, "lora_w")
                end("lora_w", pe.matmul(flat("lora_w"), lora[0:LORA, ts], lup[0:LORA, :], start=True, stop=True))
                t.before_fill(pe, "lora_a")
                for p in range(NP):
                    last = pe.matmul(heads4("lora_a")[:, p, :], lup[LORA:, p * P:(p + 1) * P], lora[LORA:, ts],
                                     start=True, stop=True)
                end("lora_a", last)
                pe.wait_ge(sq_ready, CREDIT + t.count(1, 1))
                t.before_fill(pe, "kk_sum")
                for p in range(NP):
                    last = pe.matmul(flat("kk_sum")[:, 2 * p:2 * p + 2], sq[:, p, :], cst("sel2"), start=True, stop=True)
                end("kk_sum", last)
                pe.wait_ge(ld_ready, CREDIT + t.count(1, 1))
                t.before_fill(pe, "cum")
                for p in range(NP):
                    last = pe.matmul(heads4("cum")[:, p, :], lw[:, p * P:(p + 1) * P], cst("tri"), start=True, stop=True)
                end("cum", last)
                t.wait_drained(pe, "kk_sum")
                t.before_fill(pe, "kk_scale")
                for p in range(NP):
                    last = pe.matmul(heads4("kk_scale")[:, p, :], rnb[:, 2 * p:2 * p + 2, :].rearrange("p h d -> p (h d)"),
                                     ident, start=True, stop=True)
                end("kk_scale", last)
                pe.wait_ge(rk_ready, CREDIT + t.count(1, 1))
                t.before_fill(pe, "bonus")
                for p in range(NP):
                    last = pe.matmul(heads4("bonus")[:, p, :], rk1[:, p, :], sq[:, p, :], start=True, stop=True)
                end("bonus", last)
                pe.wait_ge(v_ready, CREDIT + t.count(1, 1))
                pe.wait_ge(aw_ready, CREDIT + t.count(1, 1))
                for c in range(2):
                    t.before_fill(pe, f"avT{c}")
                    for p in range(NP):
                        last = pe.transpose(heads4(f"avT{c}")[:, p, :], RAV[:, 2 * p + c, CH:], ident)
                    end(f"avT{c}", last)
                pe.wait_ge(bk_ready, CREDIT + t.count(1, 1))
                for c in range(2):
                    t.before_fill(pe, f"bkT{c}")
                    for p in range(NP):
                        last = pe.transpose(heads4(f"bkT{c}")[:, p, :], BK[:, 2 * p + c, :], ident)
                    end(f"bkT{c}", last)
                pe.wait_ge(rw_ready, CREDIT + t.count(1, 1))
                for n in range(4):
                    c, h = n % 2, slice(n // 2 * HD, (n // 2 + 1) * HD)
                    t.before_fill(pe, f"aa{n}")
                    for p in range(NP):
                        last = pe.matmul(heads4(f"aa{n}")[:, p, :], BK[h, 2 * p + c, :], RAV[h, 2 * p + c, 0:2 * CH],
                                         start=True, stop=True)
                    end(f"aa{n}", last)
                def turn(name, g):
                    t.before_fill(pe, name)
                    for q in range(4):
                        last = pe.transpose(heads4(name)[:, q, :], UT[:, 4 * g + q, :], ident)
                    end(name, last)

                pe.wait_ge(ui_ready, CREDIT + t.count(1, 1))
                for g in range(2):
                    pe.wait_ge(ut_ready, CREDIT + t.count(2, g + 1))
                    turn(f"ut{g}", g)
                source = "ut{g}"
                for b in LEVELS:
                    for g in range(2):
                        t.wait_drained(pe, source.format(g=g))
                        t.before_fill(pe, f"q{b}_{g}")
                        for q in range(4):
                            last = pe.matmul(halves(f"q{b}_{g}", b)[:, 0, q], LT[:, 4 * g + q, :],
                                             block_cols(U, g, b, 0)[:, q], start=True, stop=True)
                        end(f"q{b}_{g}", last)
                    for g in range(2):
                        t.wait_drained(pe, f"q{b}_{g}")
                        t.before_fill(pe, f"d{b}_{g}")
                        for q in range(4):
                            last = pe.matmul(halves(f"d{b}_{g}", b)[:, 0, q], Q[:, 4 * g + q, :],
                                             block_cols(UT, g, b, 1)[:, q], start=True, stop=True)
                        end(f"d{b}_{g}", last)
                    if b != LEVELS[-1]:
                        for g in range(2):
                            t.wait_drained(pe, f"d{b}_{g}")
                            turn(f"t{b}_{g}", g)
                        source = f"t{b}_" + "{g}"
                t.before_fill(pe, "akv")
                pe.sem_inc(passed, 1)
                for c in range(2):
                    for h in range(NH):
                        last = pe.matmul(heads8("akv")[c * CH:(c + 1) * CH, h, :], AkT[CH:, c, h, :],
                                         XG[CH:, c, h, HD:], start=True, stop=True)
                end("akv", last)
                t.wait_drained(pe, "akv")
                for g in range(2):
                    t.wait_drained(pe, f"d{LEVELS[-1]}_{g}")
                    t.before_fill(pe, f"x{g}")
                    for q in range(4):
                        last = pe.matmul(heads4(f"x{g}")[:, q, :], UT[:, 4 * g + q, :], XA[:, 4 * g + q, :],
                                         start=True, stop=True)
                    end(f"x{g}", last)
                t.wait_drained(pe, "x0")
                t.wait_drained(pe, "x1")
                for c in range(2):
                    t.before_fill(pe, f"rm{c}")
                    pe.sem_inc(passed, 1)
                    for h in range(NH):
                        g, p = h // NP, h % NP
                        last = pe.matmul(heads4(f"rm{c}")[g * HD:(g + 1) * HD, p, :], XG[0:CH, c, h, 0:HD],
                                         FB[0:CH, c, p, g * 2 * HD:(g + 1) * 2 * HD], start=True, stop=True)
                    end(f"rm{c}", last)
                for c in range(2):
                    t.wait_drained(pe, f"rm{c}")
                    for g in range(2):
                        if c:
                            t.wait_drained(pe, f"sy0_{g}")
                        t.before_fill(pe, f"sy{c}_{g}")
                        rows = slice(g * HD, (g + 1) * HD)
                        for p in range(NP):
                            out = heads8(f"sy{c}_{g}")[:, p, :]
                            pe.matmul(out, FB[:, c, p, g * 2 * HD:(g + 1) * 2 * HD], XG[:, c, g * NP + p, HD:],
                                      start=True, stop=False)
                            last = pe.matmul(out, RM[rows, c, p, :], S[rows, p, :], start=False, stop=True)
                        end(f"sy{c}_{g}", last)
                for name in GROUP_NORM:
                    fill(name)
                pe.wait_ge(yn_ready, CREDIT + t.count(1, 1))
                t.before_fill(pe, "yT")
                for p in range(NP):
                    last = pe.transpose(heads4("yT")[:, p, :], Y[:, p].rearrange("p h d -> p (h d)"), ident)
                end("yT", last)

            for u in range(NU):
                for _ in unit_steps(0, u):
                    pass
            pe.wait_ge(setup, 2)
            with pe.Fori(0, NRB - 1) as i:
                for j in range(RJ):
                    tile(i, j, True)
            for j in range(RJ):
                tile(NRB - 1, j, False)


STAGES = 4
DRAINED_CREDIT = 2


def out_phase(nc, x, w_out, post_g, y_dram, out):
    with ExitStack() as ctx:
        sb = lambda name, shape, dt=F32: ctx.enter_context(nc.sbuf_tensor(name, shape, dt))
        ps = lambda name, shape, dt=F32: ctx.enter_context(nc.psum_tensor(name, shape, dt))
        sem = lambda name: ctx.enter_context(nc.semaphore(name))
        wst = sb("o_w_stage", [P, STAGES, D])
        whi = sb("o_w_hi", [P, KB, D], F32R)
        wlo = sb("o_w_lo", [P, KB, D], F32R)
        yt = sb("o_y", [P, 2, KB, 2 * TT])
        yhi = sb("o_y_hi", [P, 2, KB, TT], F32R)
        ylo = sb("o_y_lo", [P, 2, KB, TT], F32R)
        xt = sb("o_x", [P, 2, D])
        ot = sb("o_out", [P, 2, D])
        junk = sb("o_junk", [P, D])
        pg = sb("o_post_g", [P, D])
        ss = sb("o_ss", [P, 2])
        eps = sb("o_eps", [P, 1])
        pO = [ps(f"o_acc{b}", [P, D]) for b in range(2)]
        w_loaded = [sem(f"o_w_loaded{b}") for b in range(STAGES)]
        w_hi, w_freed, g_loaded = sem("o_w_hi_ready"), sem("o_w_freed"), sem("o_g_loaded")
        y_loaded, x_loaded = sem("o_y_loaded"), [sem(f"o_x_loaded{b}") for b in range(2)]
        y_hi, y_lo = sem("o_y_hi_ready"), sem("o_y_lo_ready")
        filled, squared, rooted, drained = sem("o_filled"), sem("o_squared"), sem("o_rooted"), sem("o_drained")
        ready = sem("o_ready")
        stored = [sem(f"o_stored{b}") for b in range(2)]
        vch = sem("o_vchain")
        setup = sem("o_setup")
        block = ctx.enter_context(nc.Block())
        y_v = y_dram.rearrange("(b p) t -> p b t", p=P)

        def tokens(pair, u):
            return yt[:, bass.ds(pair % 2, 1), :, u * TT:(u + 1) * TT].rearrange("p a k t -> p (a k) t")

        @block.sync
        def _(sp):
            for credited in (y_hi, y_lo, filled, squared, rooted, ready, *stored):
                sp.sem_inc(credited, CREDIT)
            sp.sem_inc(drained, DRAINED_CREDIT)

            def load(pair):
                sp.dma_start(yt[:, bass.ds(pair % 2, 1)].rearrange("p a k t -> p (a k) t"),
                             y_v[:, :, bass.ds(pair * 2 * TT, 2 * TT)]).then_inc(y_loaded, 16)

            def store(t, u):
                sp.wait_ge(ready, CREDIT + t * 2 + 2)
                sp.dma_start(out[0, bass.ds(t * TT, TT), :], ot[:, u, :]).then_inc(stored[u], 16)

            for kb in range(KB):
                if kb >= STAGES:
                    sp.wait_ge(w_freed, kb - STAGES + 1)
                sp.dma_start(wst[:, kb % STAGES], w_out[0, kb * P:(kb + 1) * P, :]).then_inc(w_loaded[kb % STAGES], 16)
                if kb == 0:
                    load(0)
            with nc.allow_non_contiguous_dma("broadcast over partitions"):
                sp.dma_start(pg[:], post_g[0:1, :].to_broadcast([P, D])).then_inc(g_loaded, 16)
            with sp.Fori(0, NT // 2 - 1) as pair:
                sp.wait_ge(y_loaded, pair * 16 + 16)
                sp.wait_ge(y_lo, CREDIT + pair * 2)
                load(pair + 1)
                for u in range(2):
                    store(pair * 2 + u, u)
            for u in range(2):
                store(NT - 2 + u, u)
            for u in range(2):
                sp.wait_ge(stored[u], CREDIT + NT // 2 * 16)

        @block.gpsimd
        def _(pool):
            with pool.Fori(0, NT // 2) as pair:
                i = pair * 2
                for u in range(2):
                    pool.wait_ge(ready, CREDIT + i * 2)
                    pool.dma_start(xt[:, u, :], x[0, bass.ts(i + u, TT), :]).then_inc(x_loaded[u], 16)

        @block.scalar
        def _(act):
            def high(pair, t, u):
                act.wait_ge(y_loaded, pair * 16 + 16)
                if not (isinstance(t, int) and t == 0):
                    act.wait_ge(drained, DRAINED_CREDIT + t - 1)
                act.activation(yhi[:, u], tokens(pair, u), ACT.Copy).then_inc(y_hi, 1)

            for kb in range(KB):
                act.wait_ge(w_loaded[kb % STAGES], 16 * (kb // STAGES + 1))
                act.activation(whi[:, kb, :], wst[:, kb % STAGES], ACT.Copy).then_inc(w_hi, 1)
                if kb == 0:
                    high(0, 0, 0)
            act.wait_ge(setup, 1)

            def root(t, u):
                act.wait_ge(filled, CREDIT + t + 1)
                act.wait_ge(drained, DRAINED_CREDIT + t)
                act.activation(junk[:], pO[u][:], ACT.Square, accum_out=ss[:, 0:1]).then_inc(squared, 1)
                act.wait_ge(squared, CREDIT + t + 1)
                act.activation(ss[:, 1:2], ss[:, 0:1], ACT.Sqrt, scale=1.0 / D, bias=eps[:]).then_inc(rooted, 1)

            with act.Fori(0, NT // 2 - 1) as pair:
                high(pair, pair * 2 + 1, 1)
                root(pair * 2, 0)
                high(pair + 1, pair * 2 + 2, 0)
                root(pair * 2 + 1, 1)
            high(NT // 2 - 1, NT - 1, 1)
            root(NT - 2, 0)
            root(NT - 1, 1)

        @block.vector
        def _(v):
            ch = Chain(v, vch)
            v.memset(eps[:], RMS_EPS).then_inc(setup, 1)

            def low(pair, t, u):
                v.wait_ge(y_hi, CREDIT + t + 1)
                v.tensor_tensor(ylo[:, u], tokens(pair, u), yhi[:, u].bitcast(F32), ALU.subtract).then_inc(y_lo, 1)

            for kb in range(KB):
                v.wait_ge(w_hi, kb + 1)
                v.tensor_tensor(wlo[:, kb, :], wst[:, kb % STAGES], whi[:, kb, :].bitcast(F32),
                                ALU.subtract).then_inc(w_freed, 1)
                if kb == 0:
                    low(0, 0, 0)
            v.wait_ge(g_loaded, 16)

            def finish(t, u):
                v.wait_ge(rooted, CREDIT + t + 1)
                ch.link(v.reciprocal(ss[:, 1:2], ss[:, 1:2]))
                v.wait_ge(stored[u], CREDIT + (t - u) * 8)
                for c in range(2):
                    cs = slice(c * 512, (c + 1) * 512)
                    last = v.scalar_tensor_tensor(ot[:, u, cs], pO[u][:, cs], ss[:, 1:2], pg[:, cs], ALU.mult, ALU.mult)
                    if c == 0:
                        ch.mark(last)
                last.then_inc(drained, 1)
                ch.restart()
                v.wait_ge(x_loaded[u], (t - u) * 8 + 16)
                v.wait_ge(drained, DRAINED_CREDIT + t + 1)
                for c in range(2):
                    cs = slice(c * 512, (c + 1) * 512)
                    v.tensor_tensor(ot[:, u, cs], ot[:, u, cs], xt[:, u, cs], ALU.add).then_inc(ready, 1)

            with v.Fori(0, NT // 2 - 1) as pair:
                low(pair, pair * 2 + 1, 1)
                finish(pair * 2, 0)
                low(pair + 1, pair * 2 + 2, 0)
                finish(pair * 2 + 1, 1)
            low(NT // 2 - 1, NT - 1, 1)
            finish(NT - 2, 0)
            finish(NT - 1, 1)

        @block.tensor
        def _(pe):
            def product(t, u, first):
                pe.wait_ge(y_lo, CREDIT + t + 1)
                pe.wait_ge(drained, DRAINED_CREDIT + t - 1)
                for kb in range(KB):
                    if first:
                        pe.wait_ge(w_freed, kb + 1)
                    for c in range(2):
                        cs = slice(c * 512, (c + 1) * 512)
                        for n, (y, w) in enumerate(((yhi, whi), (yhi, wlo), (ylo, whi))):
                            last = pe.matmul(pO[u][:, cs], y[:, u, kb, :], w[:, kb, cs], start=kb == 0 and n == 0,
                                             stop=kb == KB - 1 and n == 2)
                last.then_inc(filled, 1)

            product(0, 0, True)
            product(1, 1, False)
            with pe.Fori(1, NT // 2) as pair:
                for u in range(2):
                    product(pair * 2 + u, u, False)


def hybrid_kernel(nc, inp, consts, place, out):
    ht_dram = nc.dram_tensor("hT_blocks", [NRB, P, 2, KB, RB], F16, kind="Internal").ap()
    y_dram = nc.dram_tensor("mixed_T", [D, SEQ], F32, kind="Internal").ap()

    def shape_tile(ctx, names):
        width = sum(place[name][1] for name in names)
        ct = ctx.enter_context(nc.sbuf_tensor("shape_consts_" + names[-1], [P, width], F32))
        where, at = {}, 0
        for name in names:
            where[name] = ct[:, at:at + place[name][1]]
            at += place[name][1]

        def load(sp, loaded):
            for name in names:
                first, n = place[name]
                sp.dma_start(where[name], consts[:, first:first + n]).then_inc(loaded, 16)
            return len(names)

        return where.__getitem__, load

    with ExitStack() as rw:
        unscale_t = rw.enter_context(nc.sbuf_tensor("unscale", [P, 1], F32))
        whi_r = rw.enter_context(nc.sbuf_tensor("w_rwkv_hi", [P, KB, NSH], F16))
        wlo_r = rw.enter_context(nc.sbuf_tensor("w_rwkv_lo", [P, KB, NSH], F16))
        with ExitStack() as cv:
            cst = shape_tile(cv, CONV_CONSTS)
            whi_c = cv.enter_context(nc.sbuf_tensor("w_conv_hi", [P, KB, 3 * DC], F16))
            wlo_c = cv.enter_context(nc.sbuf_tensor("w_conv_lo", [P, KB, 3 * DC], F16))
            weights_phase(nc, inp["w_in"], inp["pre_g"], whi_r, wlo_r, whi_c, wlo_c, unscale_t[:])
            conv_phase(nc, cst, inp["x"], inp["dw_w"], inp["dw_b"], inp["ln_g"], inp["ln_b"], whi_c, wlo_c,
                       unscale_t[:], ht_dram, y_dram[DR:, :])
        cst = shape_tile(rw, RWKV_CONSTS)
        rwkv_phase(nc, cst, inp, whi_r, wlo_r, unscale_t[:], ht_dram, y_dram[0:DR, :])
    out_phase(nc, inp["x"], inp["w_out"], inp["post_g"], y_dram, out)


_INS = ["x", "pre_g", "post_g", "w_in", "mu_shift", "w0", "w_up", "a0", "a_up", "k_k", "k_a", "r_k", "gn_g", "gn_b",
        "dw_w", "dw_b", "ln_g", "ln_b", "w_out"]


def kernel(**inputs):
    import concourse.bacc as bacc
    from concourse.bass_utils import run_bass_kernel_spmd

    nc = bacc.Bacc("TRN2", target_bir_lowering=False, num_devices=1)
    arrays, aps = {}, {}
    for name in _INS:
        a = np.ascontiguousarray(inputs[name])
        arrays[f"in_{name}"] = a
        aps[name] = nc.dram_tensor(f"in_{name}", a.shape, mybir.dt.from_np(a.dtype), kind="ExternalInput").ap()
    consts, place = shape_constants()
    arrays["in_consts"] = consts
    cap = nc.dram_tensor("in_consts", consts.shape, F32, kind="ExternalInput").ap()
    out = nc.dram_tensor("out_x", [1, SEQ, D], F32, kind="ExternalOutput").ap()
    hybrid_kernel(nc, aps, cap, place, out)
    r = run_bass_kernel_spmd(nc, [arrays], core_ids=[0])
    return r.results[0]["out_x"]
```
